# Optimizing a Trainium2 kernel written in Bass

```python
import math
import jax, jax.numpy as jnp
from jax import lax
import numpy as np

D_MODEL = 1024
BATCH = 1
SEQ = 1024
DEPTH = 1

GLA_HEADS = 4
GLA_DK = 64
GLA_DV = 128
GLA_LR = 16
GLA_GATE_TAU = 16.0
GLA_CHUNK = 64
S5_WIDTH = 512
S5_GROUP = 16
S5_GROUPS = S5_WIDTH // S5_GROUP
S5_STATE = 64
S5_DT_MIN = 0.001
S5_DT_MAX = 0.1
DIFF_HEADS = 4
DIFF_DH = 64
DIFF_DV = 2 * DIFF_DH
QBLOCK = 128
D_FF = 2816
CONV_W = 3
EPS = 1e-6

GLA_QK_COLS = GLA_HEADS * GLA_DK
GLA_V_COLS = GLA_HEADS * GLA_DV
DIFF_QK_COLS = DIFF_HEADS * 2 * DIFF_DH
DIFF_V_COLS = DIFF_HEADS * DIFF_DV
IN_SPLITS = (GLA_QK_COLS, GLA_QK_COLS, GLA_V_COLS, GLA_V_COLS, GLA_LR, S5_WIDTH,
             DIFF_QK_COLS, DIFF_QK_COLS, DIFF_V_COLS, 3 * D_MODEL)
IN_COLS = sum(IN_SPLITS)

kernel_name = 'hybrid_gla_s5_diffattn_block'

def _split_points():
    pts, acc = [], 0
    for s in IN_SPLITS[:-1]:
        acc += s
        pts.append(acc)
    return pts

def rms_norm(x, g):
    xf = x.astype(jnp.float32)
    y = xf * lax.rsqrt(jnp.mean(xf * xf, axis=-1, keepdims=True) + EPS)
    return (y * g.astype(jnp.float32)).astype(x.dtype)

def gla_mixer(q, k, v, r, g_lr, gk_w, gk_b, norm_g):
    f32 = jnp.float32
    Bn, S, _ = q.shape
    N = S // GLA_CHUNK

    def heads(t, d):
        return t.astype(f32).reshape(Bn, N, GLA_CHUNK, GLA_HEADS, d).transpose(0, 3, 1, 2, 4)

    log_a = jax.nn.log_sigmoid((g_lr @ gk_w + gk_b).astype(f32)) / GLA_GATE_TAU
    qh = heads(q, GLA_DK) * GLA_DK ** -0.5
    kh = heads(k, GLA_DK)
    vh = heads(v, GLA_DV)
    b = jnp.cumsum(heads(log_a, GLA_DK), axis=3)
    b_last = b[:, :, :, -1:, :]
    q_dec = qh * jnp.exp(b)
    causal = jnp.tril(jnp.ones((GLA_CHUNK, GLA_CHUNK), bool))
    attn = jnp.einsum('bhncd,bhnsd->bhncs', q_dec, kh * jnp.exp(-b))
    attn = jnp.where(causal, attn, 0.0)
    o_intra = jnp.einsum('bhncs,bhnse->bhnce', attn, vh)
    d_state = jnp.einsum('bhncd,bhnce->nbhde', kh * jnp.exp(b_last - b), vh)
    decay = jnp.exp(b_last[:, :, :, 0, :]).transpose(2, 0, 1, 3)

    def step(state, inp):
        dec, ds = inp
        return dec[..., None] * state + ds, state

    s0 = jnp.zeros((Bn, GLA_HEADS, GLA_DK, GLA_DV), f32)
    _, s_in = lax.scan(step, s0, (decay, d_state))
    o_inter = jnp.einsum('bhncd,nbhde->bhnce', q_dec, s_in)
    o = (o_intra + o_inter).transpose(0, 2, 3, 1, 4)
    o = rms_norm(o, norm_g).reshape(Bn, S, GLA_V_COLS)
    return (o * jax.nn.silu(r.astype(f32))).astype(q.dtype)

def s5_mixer(u, lam_re, lam_im, b_re, b_im, c_re, c_im, d_skip, log_dt, glu_w, glu_b):
    f32 = jnp.float32
    Bn, S, _ = u.shape
    uf = u.astype(f32)
    dt = jnp.exp(log_dt.astype(f32))[:, None]
    lam = lax.complex(lam_re.astype(f32), lam_im.astype(f32))
    lam_bar = jnp.exp(lam * dt)
    b_bar = ((lam_bar - 1.0) / lam)[..., None] * lax.complex(b_re.astype(f32), b_im.astype(f32))
    ug = uf.reshape(Bn, S, S5_GROUPS, S5_GROUP).astype(jnp.complex64)
    bu = jnp.einsum('bsgh,gph->bsgp', ug, b_bar)
    a = jnp.broadcast_to(lam_bar, bu.shape)

    def combine(e1, e2):
        a1, b1 = e1
        a2, b2 = e2
        return a2 * a1, a2 * b1 + b2

    _, xs = lax.associative_scan(combine, (a, bu), axis=1)
    cmat = lax.complex(c_re.astype(f32), c_im.astype(f32))
    y = jnp.einsum('bsgp,ghp->bsgh', xs, cmat).real.reshape(Bn, S, S5_WIDTH) + d_skip.astype(f32) * uf
    g = jax.nn.gelu(y)
    out = g * jax.nn.sigmoid(g @ glu_w.astype(f32) + glu_b.astype(f32))
    return out.astype(u.dtype)

def diff_attention(q, k, v, q_g, k_g, lq1, lk1, lq2, lk2, subln_g, lambda_init):
    f32 = jnp.float32
    Bn, S, _ = q.shape
    nb = S // QBLOCK
    q = rms_norm(q.reshape(Bn, S, DIFF_HEADS, 2, DIFF_DH), q_g) * DIFF_DH ** -0.5
    k = rms_norm(k.reshape(Bn, S, DIFF_HEADS, 2, DIFF_DH), k_g)
    v = v.reshape(Bn, S, DIFF_HEADS, DIFF_DV)
    lam = (jnp.exp(jnp.sum(lq1.astype(f32) * lk1.astype(f32)))
           - jnp.exp(jnp.sum(lq2.astype(f32) * lk2.astype(f32))) + lambda_init)
    slopes = jnp.exp2(-8.0 * jnp.arange(1, DIFF_HEADS + 1, dtype=f32) / DIFF_HEADS)
    k_pos = jnp.arange(S)
    qb = q.reshape(Bn, nb, QBLOCK, DIFF_HEADS, 2, DIFF_DH).transpose(1, 0, 2, 3, 4, 5)
    starts = jnp.arange(nb) * QBLOCK

    def block(args):
        q_blk, start = args
        s = jnp.einsum('bqhjd,bkhjd->bhjqk', q_blk, k).astype(f32)
        dist = (start + jnp.arange(QBLOCK))[:, None] - k_pos[None, :]
        bias = -slopes[:, None, None, None] * dist.astype(f32)
        s = jnp.where(dist >= 0, s + bias, -jnp.inf)
        p = jax.nn.softmax(s, axis=-1)
        w = p[:, :, 0] - lam * p[:, :, 1]
        return jnp.einsum('bhqk,bkhe->bqhe', w.astype(v.dtype), v)

    o = lax.map(block, (qb, starts))
    o = o.transpose(1, 0, 2, 3, 4).reshape(Bn, S, DIFF_HEADS, DIFF_DV)
    o = rms_norm(o, subln_g) * (1.0 - lambda_init)
    return o.reshape(Bn, S, DIFF_V_COLS)

def causal_dwconv(h, w, b):
    C = h.shape[-1]
    y = lax.conv_general_dilated(h, w[:, None, :].astype(h.dtype), window_strides=(1,),
                                 padding=[(CONV_W - 1, 0)],
                                 dimension_numbers=('NWC', 'WIO', 'NWC'),
                                 feature_group_count=C)
    return y + b

def conv_gated_mlp(h, w_up, conv_w, conv_b, w_down):
    hh = causal_dwconv(h @ w_up, conv_w, conv_b)
    a, g = jnp.split(hh, 2, axis=-1)
    return (jax.nn.silu(a) * g) @ w_down

def setup_inputs(seed: int = 0) -> dict:
    key = jax.random.key(seed)
    ks = iter(jax.random.split(key, 48))
    L, D, F = DEPTH, D_MODEL, D_FF
    f32 = jnp.float32

    def nrm(shape, scale):
        return jax.random.normal(next(ks), shape, f32) * scale

    def gain(shape):
        return 1.0 + nrm(shape, 0.05)

    x = nrm((BATCH, SEQ, D), 1.0)
    c = nrm((BATCH, D), 1.0)
    n_idx = jnp.arange(S5_STATE, dtype=f32)
    lam_re = -0.5 + nrm((L, S5_GROUPS, S5_STATE), 0.01)
    lam_im = math.pi * n_idx + nrm((L, S5_GROUPS, S5_STATE), 0.01)
    log_dt = jax.random.uniform(next(ks), (L, S5_GROUPS), f32,
                                math.log(S5_DT_MIN), math.log(S5_DT_MAX))
    return {
        'x': x,
        'c': c,
        'ada_w': nrm((L, D, 6 * D), 0.5 * D ** -0.5),
        'ada_b': nrm((L, 6 * D), 0.01),
        'norm1_g': gain((L, D)),
        'w_in': nrm((L, D, IN_COLS), D ** -0.5),
        'gla_gk_w': nrm((L, GLA_LR, GLA_QK_COLS), GLA_LR ** -0.5),
        'gla_gk_b': nrm((L, GLA_QK_COLS), 0.1),
        'gla_norm_g': gain((L, GLA_DV)),
        's5_lambda_re': lam_re,
        's5_lambda_im': lam_im,
        's5_b_re': nrm((L, S5_GROUPS, S5_STATE, S5_GROUP), (2 * S5_GROUP) ** -0.5),
        's5_b_im': nrm((L, S5_GROUPS, S5_STATE, S5_GROUP), (2 * S5_GROUP) ** -0.5),
        's5_c_re': nrm((L, S5_GROUPS, S5_GROUP, S5_STATE), (2 * S5_STATE) ** -0.5),
        's5_c_im': nrm((L, S5_GROUPS, S5_GROUP, S5_STATE), (2 * S5_STATE) ** -0.5),
        's5_d': nrm((L, S5_WIDTH), 0.5),
        's5_log_dt': log_dt,
        's5_glu_w': nrm((L, S5_WIDTH, S5_WIDTH), S5_WIDTH ** -0.5),
        's5_glu_b': nrm((L, S5_WIDTH), 0.01),
        'diff_q_norm_g': gain((L, DIFF_DH)),
        'diff_k_norm_g': gain((L, DIFF_DH)),
        'diff_lambda_q1': nrm((L, DIFF_DH), 0.1),
        'diff_lambda_k1': nrm((L, DIFF_DH), 0.1),
        'diff_lambda_q2': nrm((L, DIFF_DH), 0.1),
        'diff_lambda_k2': nrm((L, DIFF_DH), 0.1),
        'diff_subln_g': gain((L, DIFF_DV)),
        'w_branch_gla': nrm((L, GLA_V_COLS, D), GLA_V_COLS ** -0.5),
        'w_branch_s5': nrm((L, S5_WIDTH, D), S5_WIDTH ** -0.5),
        'w_branch_diff': nrm((L, DIFF_V_COLS, D), DIFF_V_COLS ** -0.5),
        'w_out': nrm((L, D, D), D ** -0.5),
        'norm2_g': gain((L, D)),
        'ffn_w_up': nrm((L, D, 2 * F), D ** -0.5),
        'ffn_conv_w': nrm((L, CONV_W, 2 * F), CONV_W ** -0.5),
        'ffn_conv_b': nrm((L, 2 * F), 0.01),
        'ffn_w_down': nrm((L, F, D), F ** -0.5),
    }

def reference(x, c, ada_w, ada_b, norm1_g, w_in, gla_gk_w, gla_gk_b, gla_norm_g,
              s5_lambda_re, s5_lambda_im, s5_b_re, s5_b_im, s5_c_re, s5_c_im, s5_d, s5_log_dt,
              s5_glu_w, s5_glu_b, diff_q_norm_g, diff_k_norm_g, diff_lambda_q1, diff_lambda_k1,
              diff_lambda_q2, diff_lambda_k2, diff_subln_g, w_branch_gla, w_branch_s5,
              w_branch_diff, w_out, norm2_g, ffn_w_up, ffn_conv_w, ffn_conv_b, ffn_w_down):
    split_pts = _split_points()
    c_act = jax.nn.silu(c)
    for l in range(DEPTH):
        lambda_init = 0.8 - 0.6 * math.exp(-0.3 * l)
        mod = (c_act @ ada_w[l] + ada_b[l])[:, None, :]
        sh1, sc1, gt1, sh2, sc2, gt2 = jnp.split(mod, 6, axis=-1)

        h = rms_norm(x, norm1_g[l]) * (1.0 + sc1) + sh1
        proj = h @ w_in[l]
        gq, gk, gv, gr, glr, su, dq, dk, dv, gates = jnp.split(proj, split_pts, axis=-1)
        o_a = gla_mixer(gq, gk, gv, gr, glr, gla_gk_w[l], gla_gk_b[l], gla_norm_g[l])
        o_b = s5_mixer(su, s5_lambda_re[l], s5_lambda_im[l], s5_b_re[l], s5_b_im[l],
                       s5_c_re[l], s5_c_im[l], s5_d[l], s5_log_dt[l], s5_glu_w[l], s5_glu_b[l])
        o_c = diff_attention(dq, dk, dv, diff_q_norm_g[l], diff_k_norm_g[l],
                             diff_lambda_q1[l], diff_lambda_k1[l], diff_lambda_q2[l],
                             diff_lambda_k2[l], diff_subln_g[l], lambda_init)
        g_a, g_b, g_c = jnp.split(jax.nn.sigmoid(gates), 3, axis=-1)
        merged = (g_a * (o_a @ w_branch_gla[l]) + g_b * (o_b @ w_branch_s5[l])
                  + g_c * (o_c @ w_branch_diff[l]))
        x = x + gt1 * (merged @ w_out[l])

        h = rms_norm(x, norm2_g[l]) * (1.0 + sc2) + sh2
        x = x + gt2 * conv_gated_mlp(h, ffn_w_up[l], ffn_conv_w[l], ffn_conv_b[l], ffn_w_down[l])
    return x


_drawn_inputs = setup_inputs


def setup_inputs(seed=0):
    import zlib

    import numpy as np

    out = dict(_drawn_inputs(seed))
    spreads = {}
    factors = {'ada_b': 4.877,
     'norm1_g': 4.29,
     'gla_gk_b': 8.0,
     'gla_norm_g': 8.0,
     's5_lambda_re': 64.0,
     's5_lambda_im': 64.0,
     's5_b_re': 64.0,
     's5_b_im': 64.0,
     's5_c_re': 64.0,
     's5_c_im': 64.0,
     's5_log_dt': 64.0,
     's5_glu_w': 8.0,
     's5_glu_b': 64.0,
     'diff_q_norm_g': 8.0,
     'diff_k_norm_g': 8.0,
     'diff_lambda_q1': 8.0,
     'diff_lambda_k1': 8.0,
     'diff_lambda_q2': 6.542,
     'diff_lambda_k2': 4.172,
     'diff_subln_g': 35.53,
     'norm2_g': 3.635,
     'ffn_conv_b': 29.84}
    for name, (base, spread) in spreads.items():
        noise = np.random.default_rng([zlib.crc32(name.encode()), seed]).standard_normal(out[name].shape)
        drawn = base * np.exp(spread * noise) if base else spread * noise
        out[name] = __import__('jax').numpy.asarray(drawn.astype(out[name].dtype))
    for name, factor in factors.items():
        out[name] = (out[name] * factor).astype(out[name].dtype)
    return out
```

```python
import math

import concourse.bass as bass
from concourse import mybir
from contextlib import ExitStack

F32 = mybir.dt.float32
F32R = mybir.dt.float32r
I32 = mybir.dt.int32
ALU = mybir.AluOpType
ACT = mybir.ActivationFunctionType
AX = mybir.AxisListType

P = 128
D = 1024
T = 1024
KD = D // P
HALF = 512
GLA_HEADS, GLA_DK, GLA_DV, GLA_LR, GLA_CHUNK = 4, 64, 128, 16, 64
GLA_PAIRS = GLA_HEADS // 2
NCH = T // GLA_CHUNK
S5W, S5G, S5H, S5P = 512, 32, 16, 64
S5T = S5W // P
PAIRS = S5G // 2
LC = 8
NC8 = T // LC
DH, DD = 4, 64
QB = 128
NQB = T // QB
F = 2816
FG = F // 256
N_ROWS = 24
EPS = 1e-6
LAMBDA_INIT = 0.8 - 0.6 * math.exp(-0.3 * 0)

C_GQ = 0
C_GK = C_GQ + GLA_HEADS * GLA_DK
C_GV = C_GK + GLA_HEADS * GLA_DK
C_GR = C_GV + GLA_HEADS * GLA_DV
C_LR = C_GR + GLA_HEADS * GLA_DV
C_SU = C_LR + GLA_LR
C_DQ = C_SU + S5W
C_DK = C_DQ + DH * 2 * DD
C_DV = C_DK + DH * 2 * DD
C_GATE = C_DV + DH * 2 * DD

V_ADAB, V_N1, V_N2, V_C, V_GKB, V_S5D, V_GLUB, V_GLAG, V_SUBG, V_QG, V_KG, V_ROWS = (
    0, 48, 56, 64, 72, 74, 78, 82, 83, 84, 85, 86)
V_CONV = V_ROWS
NT_FF = 2 * F // P
V_CONVB = V_CONV + 3 * NT_FF
V_END = V_CONVB + NT_FF
M_SH1, M_SC1, M_GT1, M_SH2, M_SC2, M_GT2 = 0, 8, 16, 24, 32, 40


class Chain:

    def __init__(self, eng, sem):
        self.eng, self.sem, self.n, self.extra, self.base, self.per = eng, sem, 0, 0, 0, 0

    def loop(self, reg, per):
        self.base, self.per, self.extra = self.n, per, reg * per

    def end(self, count):
        assert self.n - self.base == self.per, (self.n - self.base, self.per)
        self.n, self.extra = self.base + self.per * count, 0

    def did(self, ins):
        ins.then_inc(self.sem, 1)
        self.n += 1

    def wait(self):
        self.eng.wait_ge(self.sem, self.extra + self.n)


class Count:

    def __init__(self):
        self.n, self.reg, self.per, self.base = 0, None, 0, 0

    def loop(self, reg, per):
        assert per % 2 == 0 and self.n % 2 == 0
        self.base, self.reg, self.per = self.n, reg, per

    def end(self, count):
        assert self.n - self.base == self.per, (self.n - self.base, self.per)
        self.n, self.reg = self.base + self.per * count, None

    def next(self):
        self.n += 1
        return self.n - 1

    def whole(self, n):
        return n + 1 if self.reg is None else self.reg * self.per + (n + 1)

    def half(self, n):
        return n // 2 + 1 if self.reg is None else self.reg * (self.per // 2) + (n // 2 + 1)


def build(nc, a, last_stage=99):
    w_in = a["w_in"][0]
    ctx = ExitStack()

    KB = 1024
    ctx.enter_context(nc.sbuf_tensor("slab", [P, 415 * 128], F32))
    BASE = 16512

    def at(name, shape, dt, off):
        return nc.alloc_sbuf_tensor_at(name, shape, dt, offset=BASE + off)

    small = [0]

    def const(name, shape, dt=F32):
        n = 4
        for s in shape[1:]:
            n *= s
        t = at(name, shape, dt, small[0])
        small[0] += (n + 31) // 32 * 32
        return t

    ident = const("ident", [P, P])
    ones = const("ones", [P, P])
    half_ones = const("half_ones", [P, P])
    gla_mask = const("gla_mask", [P, P], I32)
    cols = const("cols", [P, V_END])
    mod = const("mod", [P, 48])
    scale1 = const("scale1", [P, KD])
    scale2 = const("scale2", [P, KD])
    c_act = const("c_act", [P, KD])
    eps_col = const("eps_col", [P, 1])
    one_col = const("one_col", [P, 1])
    gkw = const("gkw", [GLA_LR, GLA_HEADS * GLA_DK])
    gkw_cur = const("gkw_cur", [GLA_LR, P])
    junk = const("junk", [P, 2])
    lam_in = const("lam_in", [DD, 4])
    lam_pr = const("lam_pr", [DD, 2])
    lam_e = const("lam_e", [P, 2])
    neg_lam = const("neg_lam", [P, 1])
    subg = const("subg", [P, 1])
    qg = const("qg", [P, 1])
    mx = const("mx", [P, 2, 2])
    nmx = const("nmx", [P, 2, 2])
    rsum = const("rsum", [P, 2, 2])
    rinv = const("rinv", [P, 2, 2])
    assert small[0] <= 6 * KB - 512, small[0]
    o_sq = at("o_sq", [P, HALF], F32, 6 * KB - 512)
    w_raw = at("w_raw", [P, 2, 8, P], F32, 8 * KB - 512)
    w_hi = at("w_hi", [P, 2, 8, P], F32R, 16 * KB - 512)
    w_lo = at("w_lo", [P, 2, 8, P], F32R, 24 * KB - 512)
    H0, O0, M0, A0 = 32 * KB - 512, 96 * KB - 512, 128 * KB - 512, 160 * KB - 512
    h_hi = at("h_hi", [P, KD, T], F32R, H0)
    h_lo = at("h_lo", [P, KD, T], F32R, H0 + 32 * KB)
    o_hi = at("o_hi", [P, 4, T], F32R, O0)
    o_lo = at("o_lo", [P, 4, T], F32R, O0 + 16 * KB)
    M = at("M", [P, KD, T], F32, M0)

    rows_a = at("rows_a", [P, P], F32, H0)
    rows_b = at("rows_b", [P, P], F32, H0 + 512)
    R0 = at("R0", [P, T], F32, H0 + 8 * KB)
    rows_c = at("rows_c", [P, P], F32, H0 + KB)
    x_tok = at("x_tok", [P, NQB, D], F32, O0)
    ada_ring = at("ada_ring", [P, 2, KD, HALF], F32, M0)
    xT0 = at("xT0", [P, KD, T], F32, A0)
    n_tmp = at("n_tmp", [P, 2, T], F32, A0 + 32 * KB)
    n_rstd = at("n_rstd", [P, T], F32, A0 + 40 * KB)

    pA = ctx.enter_context(nc.psum_tensor("pA", [P, T], F32))
    pB = ctx.enter_context(nc.psum_tensor("pB", [P, T], F32))
    pX = ctx.enter_context(nc.psum_tensor("pX", [P, T], F32))
    pY = ctx.enter_context(nc.psum_tensor("pY", [P, T], F32))
    acc = [pA, pB]

    def sem(name):
        return ctx.enter_context(nc.semaphore(name))

    w_loaded = [sem("w_loaded0"), sem("w_loaded1")]
    w_hi_done = sem("w_hi_done")
    w_split = sem("w_split")
    w_started = sem("w_started")
    acc_full = [sem("acc_full0"), sem("acc_full1")]
    acc_free = [sem("acc_free0"), sem("acc_free1")]
    act_chain, dve_chain, pool_chain = sem("act_chain"), sem("dve_chain"), sem("pool_chain")

    settled = {e.engine: sem(f"settled_{n}") for n, e in
               (("sp", nc.sync), ("pool", nc.gpsimd), ("pe", nc.tensor), ("dve", nc.vector))}
    block = ctx.enter_context(nc.Block())
    S = {}
    total_units = [0]

    def s(name):
        if name not in S:
            S[name] = sem(name)
        return S[name]

    def settle(eng):
        eng.sem_inc(settled[eng.engine], 1)

    def ds_col(n):
        return HALF * (n % 2) + P * (n % 8 // 2)

    def v3(t, n):
        return t.rearrange("p (a b) -> p a b", a=n)

    def gemm(pe, units, tiles, new_unit, ks, lhs, rhs_hi, rhs_lo, extra=None):
        if new_unit:
            u = units.next()
            pe.wait_ge(w_split, units.whole(u))
        else:
            u = units.n - 1
        t = tiles.next()
        if t >= 2:
            pe.wait_ge(acc_free[t % 2], tiles.half(t) - 1)
        dst = acc[t % 2]
        n, total = 0, len(ks) * 6
        for k, w in ks:
            for wp, rp in ((w_hi, rhs_hi), (w_hi, rhs_lo), (w_lo, rhs_hi)):
                for hf in range(2):
                    ins = nc.tensor.matmul(dst[:, hf * HALF:(hf + 1) * HALF], wp[:, u % 2, w, :],
                                           rp[:, k, hf * HALF:(hf + 1) * HALF],
                                           start=(n < 2), stop=(n >= total - 2))
                    if n == 0 and new_unit:
                        ins.then_inc(w_started, 1)
                    n += 1
        ins.then_inc(acc_full[t % 2], 1)

    K8 = [(k, k) for k in range(8)]

    def gemm_h(pe, units, tiles):
        gemm(pe, units, tiles, True, K8, None, h_hi, h_lo)

    def load(sp, units, src, view):
        u = units.next()
        if u >= 2:
            sp.wait_ge(w_split, units.whole(u) - 2)
            settle(sp)
        sp.dma_start(view(w_raw[:, u % 2]), src).then_inc(w_loaded[u % 2], 16)

    def load_cols(sp, units, w, col):
        load(sp, units, w[:, bass.ds(col, P)].rearrange("(k p) c -> p k c", p=P), lambda t: t)

    def load_k4(sp, units, w, col):
        load(sp, units, w[:, bass.ds(col, 256)].rearrange("(k p) c -> p k c", p=P),
             lambda t: t.rearrange("p (k c) n -> p k (c n)", k=4))

    def load_down(sp, units, w, row, col):
        load(sp, units, w[bass.ds(row, 256), col:col + 512].rearrange("(k p) c -> p k c", p=P),
             lambda t: t.rearrange("p (k c) n -> p k (c n)", k=2))


    xT_dram = nc.dram_tensor("xT_scratch", (D, T), F32).ap()
    R_dram = nc.dram_tensor("alibi_scratch", (P, T), F32).ap()
    u_dram = nc.dram_tensor("u_scratch", (S5W, T), F32).ap()
    y_dram = nc.dram_tensor("y_scratch", (S5W, T), F32).ap()

    rows_s = at("rows_s", [PAIRS, 3, P], F32, H0 + 2 * KB)
    dt_row = at("dt_row", [PAIRS, 2], F32, H0 + 4 * KB)
    s_G = [at(f"s_G{r}", [P, PAIRS, 9, S5H], F32, A0 + 9216 * r) for r in range(2)]
    s_U = at("s_U", [P, S5G, NC8], F32, A0 + 18 * KB)
    s_uP = at("s_uP", [P, S5T, LC, NC8], F32, M0 + 16 * KB)
    s_PT = [at(f"s_PT{r}", [P, PAIRS, P], F32, M0 + 8 * KB * r) for r in range(2)]
    s_Toep = at("s_Toep", [P, S5G, P], F32, M0 + 16 * KB)
    s_Ppre = [at(f"s_Ppre{r}", [P, PAIRS, P], F32, O0 + 8 * KB * r) for r in range(2)]
    s_K = at("s_K", [S5H, S5G, P], F32, O0)
    s_V = [at(f"s_V{r}", [P, PAIRS, NC8], F32, O0 + 8 * KB * r) for r in range(2)]
    s_E = [at(f"s_E{r}", [P, PAIRS, NC8], F32, O0 + 16 * KB + 8 * KB * r) for r in range(2)]
    s_X = [at(f"s_X{r}", [P, PAIRS, NC8], F32, M0 + 8 * KB * r) for r in range(2)]
    s_t = at("s_t", [P, 4 * 640], F32, A0 + 34 * KB)
    s_Y = at("s_Y", [P, S5G, NC8], F32, O0)
    s_Yp = at("s_Yp", [P, S5T, T], F32, A0)
    s_uP2 = at("s_uP2", [P, S5T, T], F32, M0)
    s_sig = at("s_sig", [P, T], F32, A0 + 18 * KB)
    s_res = at("s_res", [P, S5T, T], F32, M0 + 16 * KB)
    s_big = at("s_big", [P, 2, T], F32, O0 + 16 * KB)
    SM = A0 + 44 * KB

    def small_s5():
        off = [SM]

        def mk(name, shape, dt=F32):
            n = 4
            for x in shape[1:]:
                n *= x
            t = at(name, shape, dt, off[0])
            off[0] += (n + 31) // 32 * 32
            assert off[0] <= A0 + 48 * KB + 1024 * 0 + 16 * KB * 0 + 0 or True
            return t
        return mk, off

    mk, _off = small_s5()
    l_re, l_im, l_dt = mk("l_re", [P, PAIRS]), mk("l_im", [P, PAIRS]), mk("l_dt", [P, PAIRS])
    e_x, e_n, e_r, e_q, e_em, e_e = [mk(f"e_{i}", [P, PAIRS]) for i in range(6)]
    e_int = mk("e_int", [P, PAIRS], I32)
    th, sn, sh, cm = [mk(f"ph_{i}", [P, PAIRS]) for i in range(4)]
    cosv, cr, ci, inv = [mk(f"cc_{i}", [P, PAIRS]) for i in range(4)]
    wv_re, wv_im, mag8 = [mk(f"wv_{i}", [P, PAIRS]) for i in range(3)]
    Lp = [mk(f"Lp{r}", [P, PAIRS, 9]) for r in range(2)]
    assert _off[0] <= A0 + 48 * KB, _off[0]
    s_LR = [at(f"s_LR{r}", [P, PAIRS, 8], F32, O0 + 24 * KB + 512 * r) for r in range(2)]
    s_B = [at(f"s_B{r}", [P, PAIRS, S5H], F32, O0 + 26 * KB + KB * r) for r in range(2)]
    s_Bb = [at(f"s_Bb{r}", [P, PAIRS, S5H], F32, O0 + 28 * KB + KB * r) for r in range(2)]
    s_C = [at(f"s_C{r}", [P, PAIRS, S5H], F32, O0 + 30 * KB + KB * r) for r in range(2)]
    c_rows = at("c_rows", [P, 2, 2, P], F32, O0 + 16 * KB)
    s_tt = at("s_tt", [P, 4, 2304 // 2], F32, A0 + 18 * KB)

    def blk(name, n, shape):
        return at(name, shape, F32, A0 + 4 * KB * n)
    g_lr = blk("g_lr", 0, [GLA_LR, T])
    g_S = blk("g_S", 1, [P, T])
    g_vT = blk("g_vT", 1, [P, T])
    g_rstd = blk("g_rstd", 1, [P, T])
    g_eb = blk("g_eb", 2, [P, T])
    g_kinv = blk("g_kinv", 3, [P, T])
    g_kl = blk("g_kl", 4, [P, T])
    g_attn = blk("g_attn", 4, [P, 8, P])
    g_qd = blk("g_qd", 5, [P, T])
    g_klT = blk("g_klT", 6, [P, 8, P])
    g_sq = blk("g_sq", 6, [P, T])
    g_S0 = blk("g_S0", 7, [P, NCH, P])
    g_v = blk("g_v", 9, [P, 2, 8, P])
    g_sil = blk("g_sil", 11, [P, T])

    d_R = blk("d_R", 0, [P, T])
    d_q = blk("d_q", 1, [P, T])
    d_k = blk("d_k", 2, [P, T])
    d_v = blk("d_v", 3, [P, 8, P])
    d_s = blk("d_s", 4, [P, 2, 2, T])
    d_tmp = blk("d_tmp", 4, [P, 2, T])
    d_wT = blk("d_wT", 8, [P, 8, 512])
    d_vT = blk("d_vT", 8, [P, T])
    d_rs = blk("d_rs", 9, [P, T])

    m_sig = blk("m_sig", 0, [P, 2, T])
    m_t = blk("m_t", 2, [P, T])
    f_a = blk("f_a", 0, [P, 2, T])
    f_g = blk("f_g", 2, [P, 2, T])
    out_tok = blk("out_tok", 6, [P, 2, D])

    @block.sync
    def _(sp):
        units = Count()
        x_v = a["x"][0].rearrange("(n p) d -> p n d", p=P)
        for q in range(4):
            sp.dma_start(x_tok[:, 2 * q:2 * q + 2, :], x_v[:, 2 * q:2 * q + 2, :]).then_inc(s(f"x_in{q}"), 16)
        ada_v = a["ada_w"][0].rearrange("(k p) c -> p k c", p=P)
        for n in range(12):
            if n >= 2:
                sp.wait_ge(s("ada_used"), n - 1)
            sp.dma_start(ada_ring[:, n % 2], ada_v[:, :, n * HALF:(n + 1) * HALF]).then_inc(s(f"ada_in{n % 2}"), 16)
            if n == 2:
                sp.wait_ge(s("xT_copied"), KD)
                sp.dma_start(xT_dram.rearrange("(k p) t -> p k t", p=P), xT0[:]).then_inc(s("xT_stored"), 16)

        for t in range(2):
            load_cols(sp, units, w_in, C_SU + t * P)
        for r, nm in enumerate(("s5_b_re", "s5_b_im")):
            for gp in range(2):
                sp.dma_start(s_B[r][64 * gp:64 * gp + 64],
                             a[nm][0].rearrange("(r g) p h -> g p r h", g=2)[gp]).then_inc(s("s5_b_in"), 16)
        for r, nm in enumerate(("s5_c_re", "s5_c_im")):
            cv = a[nm][0].rearrange("(t r g) h p -> t g r h p", g=2, t=2)
            for t in range(2):
                for gp in range(2):
                    sp.dma_start(c_rows[:, r, t, 64 * gp:64 * gp + 64], cv[t, gp]).then_inc(s("s5_c_in"), 16)
        for t in range(2, 4):
            load_cols(sp, units, w_in, C_SU + t * P)
        for t in range(S5T):
            sp.wait_ge(acc_free[t % 2], t // 2 + 1)
            sp.dma_start(u_dram[t * P:(t + 1) * P, :], s_uP[:, t]).then_inc(s("u_out"), 16)
        sp.wait_ge(s("u_out"), 16 * S5T)
        sp.wait_ge(s("G_ready"), 1)
        u_v = u_dram.rearrange("(g h) (j c) -> j h g c", h=S5H, j=LC)
        for j in range(LC):
            sp.dma_start(s_U[16 * j:16 * j + 16], u_v[j]).then_inc(s("U_in"), 16)
        sp.wait_ge(s("K_copied"), 4)
        sp.wait_ge(s("Toep_zero"), 1)
        for j in range(LC):
            sp.dma_start(s_Toep[16 * j:16 * j + 16, :, 16 * j:P], s_K[:, :, 0:P - 16 * j]).then_inc(s("Toep_in"), 16)
        load_k4(sp, units, a["s5_glu_w"][0], 0)
        load_k4(sp, units, a["s5_glu_w"][0], 256)
        y_v = y_dram.rearrange("(g h) (j c) -> j h g c", h=S5H, j=LC)
        sp.wait_ge(s("Y_copied"), 4)
        for j in range(LC):
            sp.dma_start(y_v[j], s_Y[16 * j:16 * j + 16]).then_inc(s("y_out"), 16)
        sp.dma_start(s_uP2[:], u_dram.rearrange("(t p) n -> p t n", p=P)).then_inc(s("uP_in"), 16)
        sp.wait_ge(s("y_out"), 16 * LC)
        sp.dma_start(s_Yp[:], y_dram.rearrange("(t p) n -> p t n", p=P)).then_inc(s("Yp_in"), 16)

        def merge_loads(b, w):
            with sp.Fori(0, 2) as i:
                units.loop(i, 6)
                for j in (0, 2):
                    load_cols(sp, units, w_in, C_GATE + b * D + (i * 4 + j) * P)
                    load_cols(sp, units, w_in, C_GATE + b * D + (i * 4 + j + 1) * P)
                    load_k4(sp, units, w, (i * 4 + j) * P)
            units.end(2)

        if last_stage >= 2:
            merge_loads(1, a["w_branch_s5"][0])
        if last_stage >= 3:
            load_cols(sp, units, w_in, C_LR)
            load_cols(sp, units, w_in, C_LR)
            with sp.Fori(0, GLA_PAIRS) as i:
                units.loop(i, 6)
                load_cols(sp, units, w_in, C_GK + i * P)
                load_cols(sp, units, w_in, C_GQ + i * P)
                load_cols(sp, units, w_in, C_GV + i * 256)
                load_cols(sp, units, w_in, C_GV + i * 256 + P)
                load_cols(sp, units, w_in, C_GR + i * 256)
                load_cols(sp, units, w_in, C_GR + i * 256 + P)
            units.end(GLA_PAIRS)
            merge_loads(0, a["w_branch_gla"][0])
        if last_stage >= 4:
            sp.wait_ge(s("merged_add"), KD)
            sp.dma_start(d_R[:], R_dram).then_inc(s("R_in"), 16)
            with sp.Fori(0, DH // 2) as i:
                units.loop(i, 6)
                for hh in range(2):
                    for c in (C_DQ, C_DK, C_DV):
                        load_cols(sp, units, w_in, c + (i * 2 + hh) * P)
            units.end(DH // 2)
            merge_loads(2, a["w_branch_diff"][0])
        if last_stage >= 5:
            with sp.Fori(0, 4) as i:
                units.loop(i, 2)
                for j in range(2):
                    load_cols(sp, units, a["w_out"][0], (i * 2 + j) * P)
            units.end(4)
        if last_stage >= 6:
            w_up, w_down = a["ffn_w_up"][0], a["ffn_w_down"][0]

            def up_loads(g):
                for c in (0, 1):
                    load_cols(sp, units, w_up, (g * 2 + c) * P)
                    load_cols(sp, units, w_up, (g * 2 + c) * P + F)

            def down_loads(g):
                load_down(sp, units, w_down, g * 256, 0)
                load_down(sp, units, w_down, g * 256, HALF)

            up_loads(0)
            with sp.Fori(0, (FG - 1) // 2) as i:
                units.loop(i, 12)
                for q in range(2):
                    up_loads(i * 2 + q + 1)
                    down_loads(i * 2 + q)
            units.end((FG - 1) // 2)
            down_loads(FG - 1)
        total_units[0] = units.n

        if last_stage >= 7:
            out_v = a["out"][0]
            for tt in range(NQB):
                sp.wait_ge(s("out_ready"), tt + 1)
                sp.dma_start(out_v[tt * P:(tt + 1) * P, :], out_tok[:, tt % 2]).then_inc(s(f"out_stored{tt % 2}"), 16)
            for q in range(2):
                sp.wait_ge(s(f"out_stored{q}"), 16 * (NQB // 2))

    @block.gpsimd
    def _(pool):
        g = nc.gpsimd
        chain = Chain(pool, pool_chain)
        d, w = chain.did, chain.wait
        d(g.memset(ident[:], 0.0))
        d(g.memset(ones[:], 1.0))
        d(g.memset(half_ones[:], 0.0))
        d(g.memset(eps_col[:], EPS))
        d(g.memset(one_col[:], 1.0))
        d(g.memset(gla_mask[:], 1))
        w()
        d(g.affine_select(out=ident[:], in_=ident[:], compare_op=ALU.not_equal, fill=1.0, base=0,
                          pattern=[[-1, P]], channel_multiplier=1))
        w()
        d(g.memset(half_ones[0:64, 0:64], 1.0))
        w()
        d(g.memset(half_ones[64:128, 64:128], 1.0))
        w()
        d(g.affine_select(out=gla_mask[:], in_=gla_mask[:], compare_op=ALU.is_ge, fill=0.0, base=0,
                          pattern=[[1, P]], channel_multiplier=-1))
        w()
        g.affine_select(out=gla_mask[:, 64:128], in_=gla_mask[:, 64:128], compare_op=ALU.is_ge, fill=0.0,
                        base=-64, pattern=[[0, 64]], channel_multiplier=1).then_inc(s("const_ready"), 1)
        d(g.iota(R0[:], [[1, T]], base=QB - T, channel_multiplier=-1, allow_small_or_imprecise_dtypes=True))
        w()
        d(g.affine_select(out=R0[:], in_=R0[:], compare_op=ALU.is_ge, fill=-1e30, base=T - QB,
                          pattern=[[-1, T]], channel_multiplier=1))
        w()
        pool.dma_start(R_dram, R0[:]).then_inc(s("R_stored"), 16)
        pool.wait_ge(s("R_stored"), 16)

        def split(n, extra_hi, slot):
            g.tensor_copy(w_hi[:, slot], w_raw[:, slot]).then_inc(w_hi_done, 1)
            pool.wait_ge(w_hi_done, extra_hi)
            g.tensor_tensor(w_lo[:, slot], w_raw[:, slot], w_hi[:, slot].bitcast(F32), ALU.subtract).then_inc(w_split, 1)

        for u in range(2):
            pool.wait_ge(w_loaded[u], 16)
            split(u, u + 1, u)
        with pool.Fori(0, (total_units[0] - 2) // 2) as i:
            for q in range(2):
                pool.wait_ge(w_loaded[q], i * 16 + 32)
                pool.wait_ge(w_started, i * 2 + (q + 2))
                settle(pool)
                split(None, i * 2 + (q + 3), q)

    @block.tensor
    def _(pe):
        units, tiles = Count(), Count()
        mm, tr = nc.tensor.matmul, nc.tensor.transpose
        s5_col = lambda q: HALF * (q % 2) + P * (q // 2)

        def col_sums(lhs, src, dst, ready, name):
            pe.wait_ge(s(ready[0]), ready[1])
            for hf in range(2):
                ins = mm(dst[:, hf * HALF:(hf + 1) * HALF], lhs[:], src[:, hf * HALF:(hf + 1) * HALF],
                         start=True, stop=True)
            ins.then_inc(s(name), 1)

        def norm_sums(tag):
            for k in range(KD):
                pe.wait_ge(s(f"sq_ready{tag}"), k + 1)
                for hf in range(2):
                    ins = mm(pY[:, hf * HALF:(hf + 1) * HALF], ones[:], n_tmp[:, k % 2, hf * HALF:(hf + 1) * HALF],
                             start=(k == 0), stop=(k == KD - 1))
                ins.then_inc(s(f"sq_summed{tag}"), 1)

        pe.wait_ge(s("const_ready"), 1)
        pe.wait_ge(s("rows_in"), 16 * N_ROWS)
        tr(pA[:, 0:V_ROWS], rows_a[0:V_ROWS, :], ident[0:V_ROWS, 0:V_ROWS])
        tr(pA[:, 128:256], rows_b[:], ident[:])
        tr(pA[:, 256:304], rows_c[0:48, :], ident[0:48, 0:48])
        tr(pA[:, 320:336], rows_s[:, 0, :], ident[0:PAIRS, 0:PAIRS])
        tr(pA[:, 336:352], rows_s[:, 1, :], ident[0:PAIRS, 0:PAIRS])
        pe.wait_ge(s("dt_rows"), 1)
        tr(pA[:, 352:368], rows_s[:, 2, :], ident[0:PAIRS, 0:PAIRS])
        mm(pA[:, 368:370], ones[0:DD, :], lam_pr[:], start=True, stop=True).then_inc(s("rows_T"), 1)
        for q in range(4):
            pe.wait_ge(s(f"x_in{q}"), 16)
        for k in range(KD):
            if k >= 2:
                pe.wait_ge(s("xT_copied"), k - 1)
            for tt in range(NQB):
                ins = tr([pX, pY][k % 2][:, tt * P:(tt + 1) * P], x_tok[:, tt, k * P:(k + 1) * P], ident[:])
            ins.then_inc(s("xT_full"), 1)
        pe.wait_ge(s("xT_copied"), KD)
        norm_sums(1)
        pe.wait_ge(s("c_ready"), 1)
        for n in range(12):
            pe.wait_ge(s(f"ada_in{n % 2}"), 16 * (n // 2 + 1))
            for c in range(4):
                for k in range(KD):
                    ins = mm(pA[:, 512 + 4 * n + c:513 + 4 * n + c], ada_ring[:, n % 2, k, c * P:(c + 1) * P],
                             c_act[:, k:k + 1], start=(k == 0), stop=(k == KD - 1))
            ins.then_inc(s("ada_used"), 1)

        pe.wait_ge(s("mod_ready"), 1)
        pe.wait_ge(s("h_ready1"), KD)
        for t in range(S5T):
            gemm_h(pe, units, tiles)
        pe.wait_ge(s("s5_c_in"), 16 * 8)
        for r in range(2):
            for t in range(2):
                ins = tr(pX[:, (2 * r + t) * P:(2 * r + t + 1) * P], c_rows[:, r, t, :], ident[:])
        ins.then_inc(s("C_T"), 1)
        for r in range(2):
            pe.wait_ge(s("Ppre_ready"), 1)
            pe.wait_ge(s("C_copied"), 1)
            if r:
                pe.wait_ge(s("PT_copied"), 2)
            for pr in range(PAIRS):
                ins = tr([pX, pY][pr // 8][:, (pr % 8) * P:(pr % 8 + 1) * P], s_Ppre[r][:, pr, :], ident[:])
                if pr % 8 == 7:
                    ins.then_inc(s("PT_full"), 1)
        pe.wait_ge(s("G_ready"), 1)
        for rnd in range(4):
            pe.wait_ge(s("PT_copied"), 4)
            if rnd >= 2:
                pe.wait_ge(s("K_copied"), rnd - 1)
            for q in range(8):
                gr = rnd * 8 + q
                pr, gp = gr // 2, gr % 2
                for r in range(2):
                    ins = mm([pX, pY][rnd % 2][0:S5H, s5_col(q):s5_col(q) + P], s_Bb[r][64 * gp:64 * gp + 64, pr, :],
                             s_G[r][64 * gp:64 * gp + 64, pr, 0:8, :].rearrange("p a b -> p (a b)"),
                             start=(r == 0), stop=(r == 1))
            ins.then_inc(s("K_full"), 1)
        pe.wait_ge(s("U_in"), 16 * LC)
        pe.wait_ge(s("K_copied"), 4)
        for r in range(2):
            for half in range(2):
                if r:
                    pe.wait_ge(s("V_copied"), half + 1)
                for pr in range(8 * half, 8 * half + 8):
                    for gp in range(2):
                        ins = mm([pX, pY][half][64 * gp:64 * gp + 64, (pr % 8) * P:(pr % 8 + 1) * P],
                                 s_PT[r][:, pr, 64 * gp:64 * gp + 64], s_U[:, 2 * pr + gp, :], start=True, stop=True)
                ins.then_inc(s("V_full"), 1)
        pe.wait_ge(s("X_ready"), 1)
        pe.wait_ge(s("Toep_in"), 16 * LC)
        pe.wait_ge(s("V_copied"), 4)
        for rnd in range(4):
            if rnd >= 2:
                pe.wait_ge(s("Y_copied"), rnd - 1)
            for q in range(8):
                gr = rnd * 8 + q
                pr, gp = gr // 2, gr % 2
                dst = [pX, pY][rnd % 2][:, s5_col(q):s5_col(q) + P]
                mm(dst, s_Toep[:, gr, :], s_U[:, gr, :], start=True, stop=False)
                for r in range(2):
                    ins = mm(dst, s_G[r][64 * gp:64 * gp + 64, pr, 1:9, :].rearrange("p a b -> p (a b)"),
                             s_X[r][64 * gp:64 * gp + 64, pr, :], start=False, stop=(r == 1))
            ins.then_inc(s("Y_full"), 1)
        pe.wait_ge(s("gelu_split"), S5T)
        for t in range(4):
            gemm(pe, units, tiles, t % 2 == 0, [(k, 2 * k + t % 2) for k in range(4)], None, o_hi, o_lo)

        def merge(b, ready, count):
            pe.wait_ge(s(ready), count)
            with pe.Fori(0, 2) as i:
                units.loop(i, 6)
                tiles.loop(i, 8)
                for j in (0, 2):
                    gemm_h(pe, units, tiles)
                    gemm_h(pe, units, tiles)
                    for c in range(2):
                        gemm(pe, units, tiles, c == 0, [(k, 2 * k + c) for k in range(4)], None, o_hi, o_lo)
            units.end(2)
            tiles.end(2)

        if last_stage >= 2:
            merge(1, "s5_split", S5T)

        if last_stage >= 3:
            gemm_h(pe, units, tiles)
            gemm(pe, units, tiles, True, [(0, 0)], None, h_hi, h_lo)
            pe.wait_ge(acc_free[0], tiles.half(tiles.n - 2))
            with pe.Fori(0, GLA_PAIRS) as i:
                units.loop(i, 6)
                tiles.loop(i, 6)
                pe.wait_ge(s("gkw_ready"), i + 1)
                for hf in range(2):
                    ins = mm(pX[:, hf * HALF:(hf + 1) * HALF], gkw_cur[:], g_lr[:, hf * HALF:(hf + 1) * HALF],
                             start=True, stop=True)
                ins.then_inc(s("z_full"), 1)
                gemm_h(pe, units, tiles)
                gemm_h(pe, units, tiles)
                gemm_h(pe, units, tiles)
                t_v = tiles.n - 1
                pe.wait_ge(s("kl_ready"), i + 1)
                for tb in range(8):
                    ins = tr(pX[:, tb * P:(tb + 1) * P], g_kl[:, tb * P:(tb + 1) * P], ident[:])
                ins.then_inc(s("klT_full"), 1)
                for hd in range(2):
                    if hd == 0:
                        gemm_h(pe, units, tiles)
                    else:
                        gemm_h(pe, units, tiles)
                    pe.wait_ge(acc_free[(t_v + hd) % 2], tiles.half(t_v + hd))
                    if hd:
                        pe.wait_ge(s("v_copied"), i * 2 + 1)
                    for tb in range(8):
                        ins = tr(pY[:, tb * P:(tb + 1) * P], g_vT[:, tb * P:(tb + 1) * P], ident[:])
                    ins.then_inc(s("v_full"), 1)
                pe.wait_ge(s("klT_copied"), i + 1)
                pe.wait_ge(s("v_copied"), i * 2 + 2)
                settle(pe)
                for n in range(NCH - 1):
                    tb, hb = n // 2, 64 * (n % 2)
                    for hd in range(2):
                        ins = mm([pX, pY][n // 8][64 * hd:64 * hd + 64, ds_col(n):ds_col(n) + P],
                                 g_klT[hb:hb + 64, tb, 64 * hd:64 * hd + 64], g_v[hb:hb + 64, hd, tb, :],
                                 start=True, stop=True)
                    if n % 8 == 7 or n == NCH - 2:
                        ins.then_inc(s("ds_full"), 1)
                pe.wait_ge(s("S0_ready"), i + 1)
                for hd in range(2):
                    r0 = 64 * hd
                    if hd:
                        pe.wait_ge(s("g_rstd_var"), i * 2 + 1)
                    for tb in range(8):
                        ins = mm(pX[:, tb * P:(tb + 1) * P], g_kinv[r0:r0 + 64, tb * P:(tb + 1) * P],
                                 g_qd[r0:r0 + 64, tb * P:(tb + 1) * P], start=True, stop=True)
                    ins.then_inc(s("attn_full"), 1)
                    if hd:
                        gemm_h(pe, units, tiles)
                    pe.wait_ge(s("attn_ready"), i * 2 + (hd + 1))
                    if hd:
                        pe.wait_ge(s("g_o_read"), i * 2 + 1)
                    for tb in range(8):
                        mm(pY[:, tb * P:(tb + 1) * P], g_v[:, hd, tb, :], g_attn[:, tb, :], start=True, stop=False)
                        for c in range(2):
                            t0 = tb * P + 64 * c
                            ins = mm(pY[:, t0:t0 + 64], g_S0[r0:r0 + 64, 2 * tb + c, :], g_qd[r0:r0 + 64, t0:t0 + 64],
                                     start=False, stop=(c == 1))
                    ins.then_inc(s("g_o_full"), 1)
                    col_sums(ones, g_sq, pX, ("g_sq_ready", i * 2 + (hd + 1)), "g_ss_full")
            units.end(GLA_PAIRS)
            tiles.end(GLA_PAIRS)
            merge(0, "gla_split", GLA_HEADS)

        if last_stage >= 4:
            with pe.Fori(0, DH // 2) as i:
                units.loop(i, 6)
                tiles.loop(i, 38)
                for hh in range(2):
                    for qk in range(2):
                        gemm_h(pe, units, tiles)
                        t_k = tiles.n - 1
                        pe.wait_ge(s("d_sq_ready"), i * 4 + (2 * hh + qk + 1))
                        if hh or qk:
                            pe.wait_ge(s("d_var_read"), i * 4 + (2 * hh + qk))
                        for hf in range(2):
                            ins = mm(pX[:, hf * HALF:(hf + 1) * HALF], half_ones[:], d_tmp[:, 0, hf * HALF:(hf + 1) * HALF],
                                     start=True, stop=True)
                        ins.then_inc(s("d_ss_full"), 1)
                    gemm_h(pe, units, tiles)
                    t_v = tiles.n - 1
                    pe.wait_ge(acc_free[t_v % 2], tiles.half(t_v))
                    for tb in range(8):
                        ins = tr(pY[:, tb * P:(tb + 1) * P], d_vT[:, tb * P:(tb + 1) * P], ident[:])
                    ins.then_inc(s("d_v_full"), 1)
                    pe.wait_ge(acc_free[t_k % 2], tiles.half(t_k))

                    def scores(qb):
                        kw = (qb + 1) * QB
                        for j in range(2):
                            t = tiles.next()
                            pe.wait_ge(acc_free[t % 2], tiles.half(t) - 1)
                            for c0 in range(0, kw, HALF):
                                c1 = min(kw, c0 + HALF)
                                ins = mm(acc[t % 2][:, c0:c1], d_q[64 * j:64 * j + 64, qb * QB:(qb + 1) * QB],
                                         d_k[64 * j:64 * j + 64, c0:c1], start=True, stop=True)
                            ins.then_inc(acc_full[t % 2], 1)

                    def weights_T(qb):
                        pe.wait_ge(s("d_w_ready"), i * 16 + (8 * hh + qb + 1))
                        if hh == 0 and qb == 0:
                            pe.wait_ge(s("d_var_read"), i * 4 + 2)
                        elif qb == 0:
                            pe.wait_ge(s("d_var_read"), i * 4 + 4)
                        else:
                            pe.wait_ge(s("d_wT_copied"), i * 16 + (8 * hh + qb))
                        for kb in range(qb + 1):
                            ins = tr(pX[:, kb * P:(kb + 1) * P], d_s[:, qb % 2, 0, kb * P:(kb + 1) * P], ident[:])
                        ins.then_inc(s("d_wT_full"), 1)

                    def values(grp):
                        pe.wait_ge(s("d_wT_copied"), i * 16 + (8 * hh + 4 * grp + 4))
                        if grp:
                            pe.wait_ge(s("d_o_read"), i * 4 + (2 * hh + 1))
                        else:
                            pe.wait_ge(s("d_v_copied"), i * 2 + (hh + 1))
                        nkb = 4 * grp + 4
                        for kb in range(nkb):
                            c0 = max(0, kb - 4 * grp) * P
                            ins = mm(pY[:, c0:HALF], d_v[:, kb, :], d_wT[:, kb, c0:HALF], start=(kb == 0), stop=(kb == nkb - 1))
                        ins.then_inc(s("d_o_full"), 1)
                        pe.wait_ge(s("d_osq_ready"), i * 4 + (2 * hh + grp + 1))
                        mm(pY[:, HALF:T], ones[:], o_sq[:], start=True, stop=True).then_inc(s("d_oss_full"), 1)

                    scores(0)
                    for qb in range(NQB):
                        if qb + 1 < NQB:
                            scores(qb + 1)
                        weights_T(qb)
                        if qb % 4 == 3:
                            values(qb // 4)
            units.end(DH // 2)
            tiles.end(DH // 2)
            merge(2, "diff_split", 2 * DH)

        if last_stage >= 5:
            pe.wait_ge(s("merged_split"), 1)
            with pe.Fori(0, 4) as i:
                units.loop(i, 2)
                tiles.loop(i, 2)
                for j in range(2):
                    gemm_h(pe, units, tiles)
            units.end(4)
            tiles.end(4)
            norm_sums(2)

        if last_stage >= 6:
            pe.wait_ge(s("h_ready2"), KD)

            def down(q, g):
                pe.wait_ge(s("act_split"), g * 2 + 2)
                for n in range(2):
                    for m in range(4):
                        gemm_down(pe, units, tiles, m, q)

            def gemm_down(pe, units, tiles, m, q):
                gemm(pe, units, tiles, m == 0, [(2 * q + k, 4 * k + m) for k in range(2)], None, o_hi, o_lo)

            for t in range(4):
                gemm_h(pe, units, tiles)
            with pe.Fori(0, (FG - 1) // 2) as i:
                units.loop(i, 12)
                tiles.loop(i, 24)
                for q in range(2):
                    for t in range(4):
                        gemm_h(pe, units, tiles)
                    down(q, i * 2 + q)
            units.end((FG - 1) // 2)
            tiles.end((FG - 1) // 2)
            down(0, FG - 1)

        if last_stage >= 7:
            for q in range(2):
                pe.wait_ge(acc_free[q], tiles.half(tiles.n - 2))
            for tt in range(NQB):
                if tt >= 2:
                    pe.wait_ge(s("out_ready"), tt - 1)
                for k in range(KD):
                    ins = tr([pX, pY][tt % 2][:, k * P:(k + 1) * P], M[:, k, tt * P:(tt + 1) * P], ident[:])
                ins.then_inc(s("out_full"), 1)

    @block.scalar
    def _(act):
        units, tiles = Count(), Count()
        act_ = nc.scalar.activation
        chain = Chain(act, act_chain)
        d, w = chain.did, chain.wait

        def full(t):
            act.wait_ge(acc_full[t % 2], tiles.half(t))

        def rows(v, n):
            return a[v][0].rearrange("(m p) -> m p", m=n)

        def row_in(dst, src):
            act.dma_start(dst, src).then_inc(s("rows_in"), 16)

        row_in(rows_a[V_ADAB:V_N1, :], rows("ada_b", 48))
        row_in(rows_a[V_N1:V_N2, :], rows("norm1_g", 8))
        row_in(rows_a[V_N2:V_C, :], rows("norm2_g", 8))
        row_in(rows_a[V_C:V_GKB, :], rows("c", 8))
        row_in(rows_a[V_GKB:V_S5D, :], rows("gla_gk_b", 2))
        row_in(rows_a[V_S5D:V_GLUB, :], rows("s5_d", 4))
        row_in(rows_a[V_GLUB:V_GLAG, :], rows("s5_glu_b", 4))
        row_in(rows_a[V_GLAG:V_SUBG, :], rows("gla_norm_g", 1))
        row_in(rows_a[V_SUBG:V_QG, :], rows("diff_subln_g", 1))
        for j in range(2):
            row_in(rows_a[V_QG:V_KG, DD * j:DD * j + DD], rows("diff_q_norm_g", 1))
            row_in(rows_a[V_KG:V_ROWS, DD * j:DD * j + DD], rows("diff_k_norm_g", 1))
        cw = a["ffn_conv_w"][0].rearrange("w (m p) -> (w m) p", p=P)
        row_in(rows_b[:], cw[0:P])
        row_in(rows_c[0:4, :], cw[P:3 * NT_FF])
        row_in(rows_c[4:48, :], rows("ffn_conv_b", NT_FF))
        for r, nm in enumerate(("s5_lambda_re", "s5_lambda_im")):
            row_in(rows_s[:, r, :], a[nm][0].rearrange("(r g) p -> r (g p)", g=2))
        row_in(dt_row[:], a["s5_log_dt"][0].rearrange("(r g) -> r g", g=2))
        row_in(gkw[:], a["gla_gk_w"][0])
        for q, nm in enumerate(("diff_lambda_q1", "diff_lambda_k1", "diff_lambda_q2", "diff_lambda_k2")):
            row_in(lam_in[:, q:q + 1], a[nm][0].rearrange("(p o) -> p o", o=1))

        for k in range(KD):
            act.wait_ge(s("xT_full"), k + 1)
            if k >= 2:
                act.wait_ge(s("sq_summed1"), k - 1) if False else None
            act_(xT0[:, k, :], [pX, pY][k % 2][:], ACT.Copy).then_inc(s("xT_copied"), 1)

        def norm_squares(tag, X, ready):
            for k in range(KD):
                if ready is not None:
                    ready(k)
                if k >= 2:
                    act.wait_ge(s(f"sq_summed{tag}"), k - 1)
                act_(n_tmp[:, k % 2, :], X[:, k, :], ACT.Square).then_inc(s(f"sq_ready{tag}"), 1)

        def norm_rest(tag):
            act.wait_ge(s(f"nrm_inv{tag}"), 1)
            act_(n_rstd[:], n_rstd[:], ACT.Sqrt).then_inc(s(f"nrm_rstd{tag}"), 1)
            for k in range(KD):
                act.wait_ge(s(f"nrm_t{tag}"), k + 1)
                act_(h_hi[:, k, :], n_tmp[:, k % 2, :], ACT.Copy).then_inc(s(f"nrm_hi{tag}"), 1)

        norm_squares(1, xT0, lambda k: act.wait_ge(s("xT_copied"), k + 1))
        act.wait_ge(s("rows_T"), 1)
        act_(cols[:, 0:V_ROWS], pA[:, 0:V_ROWS], ACT.Copy)
        act_(cols[:, V_CONV:V_CONV + P], pA[:, 128:256], ACT.Copy)
        act_(cols[:, V_CONV + P:V_END], pA[:, 256:304], ACT.Copy)
        act_(l_re[:], pA[:, 320:336], ACT.Copy)
        act_(l_im[:], pA[:, 336:352], ACT.Copy)
        act_(l_dt[:], pA[:, 352:368], ACT.Copy)
        act_(lam_e[:], pA[:, 368:370], ACT.Exp).then_inc(s("cols_ready"), 1)
        act.wait_ge(s("cols_ready"), 1)
        act_(c_act[:], cols[:, V_C:V_C + KD], ACT.Silu).then_inc(s("c_ready"), 1)
        act.wait_ge(s("R_stored"), 16)
        norm_rest(1)

        for t in range(S5T):
            n = tiles.next()
            full(n)
            act_(s_uP[:, t], acc[n % 2].rearrange("p (c j) -> p j c", j=LC), ACT.Copy).then_inc(acc_free[n % 2], 1)
        act.wait_ge(s("C_T"), 1)
        act_(s_C[0].rearrange("p a b -> p (a b)"), pX[:, 0:256], ACT.Copy)
        act_(s_C[1].rearrange("p a b -> p (a b)"), pX[:, 256:512], ACT.Copy).then_inc(s("C_copied"), 1)
        act.wait_ge(s("angle_ready"), 1)
        act_(sn[:], th[:], ACT.Sin)
        act_(sh[:], th[:], ACT.Sin, scale=0.5).then_inc(s("sines"), 1)
        for n in range(4):
            act.wait_ge(s("PT_full"), n + 1)
            act_(s_PT[n // 2][:, 8 * (n % 2):8 * (n % 2) + 8, :].rearrange("p a b -> p (a b)"), [pX, pY][n % 2][:],
                 ACT.Copy).then_inc(s("PT_copied"), 1)
        for n in range(4):
            act.wait_ge(s("K_full"), n + 1)
            act_(s_K[:, 8 * n:8 * n + 8, :].rearrange("p (r g) b -> p g r b", g=2),
                 [pX, pY][n % 2][0:S5H, :].rearrange("p (g r b) -> p g r b", g=2, b=P),
                 ACT.Copy).then_inc(s("K_copied"), 1)
        act.wait_ge(s("Toep_in"), 16 * LC)
        for n in range(4):
            act.wait_ge(s("V_full"), n + 1)
            act_(s_V[n // 2][:, 8 * (n % 2):8 * (n % 2) + 8, :].rearrange("p a b -> p (a b)"), [pX, pY][n % 2][:],
                 ACT.Copy).then_inc(s("V_copied"), 1)
        for n in range(4):
            act.wait_ge(s("Y_full"), n + 1)
            act_(s_Y[:, 8 * n:8 * n + 8, :].rearrange("p (r g) b -> p g r b", g=2),
                 [pX, pY][n % 2][:].rearrange("p (g r b) -> p g r b", g=2, b=P),
                 ACT.Copy).then_inc(s("Y_copied"), 1)
        for t in range(S5T):
            act.wait_ge(s("yd_ready"), t + 1)
            d(act_(s_Yp[:, t, :], s_Yp[:, t, :], ACT.Gelu_apprx_tanh))
            w()
            act_(o_hi[:, t, :], s_Yp[:, t, :], ACT.Copy).then_inc(s("gelu_hi"), 1)
        for t in range(S5T):
            n = tiles.next()
            full(n)
            if t:
                act.wait_ge(s("glu_out"), t)
            act_(s_sig[:], acc[n % 2][:], ACT.Sigmoid, bias=cols[:, V_GLUB + t:V_GLUB + t + 1]).then_inc(acc_free[n % 2], 1)
        for t in range(S5T):
            act.wait_ge(s("glu_out"), S5T)
            act_(o_hi[:, t, :].rearrange("p (c j) -> p j c", j=LC), s_res[:, t, :].rearrange("p (j c) -> p j c", j=LC),
                 ACT.Copy).then_inc(s("s5_hi"), 1)

        def merge(first):
            with act.Fori(0, 2) as i:
                tiles.loop(i, 8)
                for j in (0, 2):
                    for q in range(2):
                        n = tiles.next()
                        full(n)
                        act_(m_sig[:, q, :], acc[n % 2][:], ACT.Sigmoid).then_inc(acc_free[n % 2], 1)
                    tiles.n += 2
            tiles.end(2)

        if last_stage >= 2:
            merge(True)

        if last_stage >= 3:
            n = tiles.next()
            full(n)
            act_(g_lr[:], acc[n % 2][0:GLA_LR, :], ACT.Copy).then_inc(acc_free[n % 2], 1)
            n = tiles.next()
            full(n)
            act_(junk[:], acc[n % 2][:, 0:2], ACT.Copy).then_inc(acc_free[n % 2], 1)
            with act.Fori(0, GLA_PAIRS) as i:
                tiles.loop(i, 6)
                chain.loop(i, 2)
                act.wait_ge(s("g_z"), i + 1)
                d(act_(g_eb[:], g_kinv[:], ACT.Abs))
                w()
                d(act_(g_eb[:], g_eb[:], ACT.Exp, scale=-1.0))
                w()
                act_(g_eb[:], g_eb[:], ACT.Ln, bias=one_col[:]).then_inc(s("g_ln"), 1)
                act.wait_ge(s("g_S_ready"), i + 1)
                act_(g_eb[:], g_S[:], ACT.Exp, scale=1.0 / 16)
                act_(g_kinv[:], g_S[:], ACT.Exp, scale=-1.0 / 16).then_inc(s("g_exps"), 1)
                act.wait_ge(s("g_kx_ready"), i + 1)
                act_(g_kl[:], g_kl[:], ACT.Exp, scale=1.0 / 16).then_inc(s("g_klx"), 1)
                tiles.n += 2
                n = tiles.next()
                full(n)
                act_(g_vT[:], acc[n % 2][:], ACT.Copy).then_inc(acc_free[n % 2], 1)
                act.wait_ge(s("klT_full"), i + 1)
                act_(g_klT.rearrange("p a b -> p (a b)"), pX[:], ACT.Copy).then_inc(s("klT_copied"), 1)
                act.wait_ge(s("v_full"), i * 2 + 1)
                act_(g_v[:, 0].rearrange("p a b -> p (a b)"), pY[:], ACT.Copy).then_inc(s("v_copied"), 1)
                n = tiles.next()
                full(n)
                act_(g_vT[:], acc[n % 2][:], ACT.Copy).then_inc(acc_free[n % 2], 1)
                n = tiles.next()
                full(n)
                act_(g_sil[:], acc[n % 2][:], ACT.Silu).then_inc(acc_free[n % 2], 1)
                act.wait_ge(s("v_full"), i * 2 + 2)
                act_(g_v[:, 1].rearrange("p a b -> p (a b)"), pY[:], ACT.Copy).then_inc(s("v_copied"), 1)
                for hd in range(2):
                    if hd:
                        n = tiles.next()
                        full(n)
                        act_(g_sil[:], acc[n % 2][:], ACT.Silu).then_inc(acc_free[n % 2], 1)
                        act.wait_ge(s("gla_split"), i * 2 + 1)
                    act.wait_ge(s("g_o_full"), i * 2 + (hd + 1))
                    act_(g_sq[:], pY[:], ACT.Square).then_inc(s("g_sq_ready"), 1)
                    act.wait_ge(s("g_inv"), i * 2 + (hd + 1))
                    act_(g_rstd[:], g_rstd[:], ACT.Sqrt).then_inc(s("g_rstd_ready"), 1)
                    act.wait_ge(s("g_y_ready"), i * 2 + (hd + 1))
                    act_(o_hi[:, bass.ds(i * 2 + hd, 1), :].rearrange("p a b -> p (a b)"), g_sq[:], ACT.Copy).then_inc(s("g_hi"), 1)
            tiles.end(GLA_PAIRS)
            chain.end(GLA_PAIRS)
            merge(False)

        if last_stage >= 4:
            with act.Fori(0, DH // 2) as i:
                tiles.loop(i, 38)
                for hh in range(2):
                    for qk in range(2):
                        n = tiles.next()
                        full(n)
                        if qk:
                            act.wait_ge(s("d_ss_full"), i * 4 + (2 * hh + 1))
                        act_(d_tmp[:, 0, :], acc[n % 2][:], ACT.Square).then_inc(s("d_sq_ready"), 1)
                        act.wait_ge(s("d_inv"), i * 4 + (2 * hh + qk + 1))
                        act_(d_rs[:], d_rs[:], ACT.Sqrt).then_inc(s("d_rstd_ready"), 1)
                    n = tiles.next()
                    full(n)
                    act_(d_vT[:], acc[n % 2][:], ACT.Copy).then_inc(acc_free[n % 2], 1)
                    act.wait_ge(s("d_v_full"), i * 2 + (hh + 1))
                    act_(d_v.rearrange("p a b -> p (a b)"), pY[:], ACT.Copy).then_inc(s("d_v_copied"), 1)

                    def exps(qb):
                        kw = (qb + 1) * QB
                        act.wait_ge(s("d_mx_ready"), i * 16 + (8 * hh + qb + 1))
                        for j in range(2):
                            ins = act_(d_s[:, qb % 2, j, 0:kw], d_s[:, qb % 2, j, 0:kw], ACT.Exp,
                                       bias=nmx[:, qb % 2, j:j + 1], accum_out=rsum[:, qb % 2, j:j + 1])
                        ins.then_inc(s("d_p_ready"), 1)

                    exps(0)
                    for qb in range(NQB):
                        if qb + 1 < NQB:
                            exps(qb + 1)
                        act.wait_ge(s("d_wT_full"), i * 16 + (8 * hh + qb + 1))
                        act_(d_wT[:, 0:qb + 1, (qb % 4) * QB:(qb % 4 + 1) * QB],
                             pX[:, 0:(qb + 1) * QB].rearrange("p (a b) -> p a b", b=QB), ACT.Copy).then_inc(s("d_wT_copied"), 1)
                        if qb % 4 == 3:
                            grp = qb // 4
                            no = i * 4 + (2 * hh + grp + 1)
                            act.wait_ge(s("d_o_full"), no)
                            act_(o_sq[:], pY[:, 0:HALF], ACT.Square).then_inc(s("d_osq_ready"), 1)
                            act.wait_ge(s("d_oinv"), no)
                            act_(o_sq[:], pY[:, HALF:T], ACT.Sqrt).then_inc(s("d_orstd"), 1)
                            act.wait_ge(s("d_o_read"), no)
                            act_(o_hi[:, bass.ds(i * 2 + hh, 1), grp * HALF:(grp + 1) * HALF].rearrange("p a b -> p (a b)"),
                                 o_sq[:], ACT.Copy).then_inc(s("d_hi"), 1)
                    tiles.n += 16
            tiles.end(DH // 2)
            merge(False)

        if last_stage >= 5:
            for k in range(KD):
                act.wait_ge(s("merged_add"), 2 * KD)
                act_(h_hi[:, k, :], M[:, k, :], ACT.Copy).then_inc(s("merged_hi"), 1)
            act.wait_ge(s("merged_split"), 1)
            act.dma_start(M[:], xT_dram.rearrange("(k p) t -> p k t", p=P)).then_inc(s("xT_in"), 16)
            first = tiles.n
            tiles.n += 8
            norm_squares(2, M, lambda k: act.wait_ge(acc_free[(first + k) % 2], tiles.half(first + k)))
            norm_rest(2)

        if last_stage >= 6:
            def up(g, par, start):
                for c in range(2):
                    for ag in range(2):
                        n = tiles.next()
                        full(n)
                        buf = [f_a, f_g][ag]
                        if ag == 0 and not start:
                            act.wait_ge(s("act_split"), (g - 1) * 2 + (c + 1))
                        ch = V_CONV + 2 * NT_FF + 22 * ag + g * 2 + c
                        chb = V_CONVB + 22 * ag + g * 2 + c
                        act_(buf[:, c, :], acc[n % 2][:], ACT.Identity, scale=cols[:, bass.ds(ch, 1)],
                             bias=cols[:, bass.ds(chb, 1)]).then_inc(s("f_lin"), 1)
                        if ag == 0:
                            act.wait_ge(acc_free[n % 2], tiles.half(n))
                            act_(f_a[:, c, :], f_a[:, c, :], ACT.Silu).then_inc(s("f_silu"), 1)
                    act.wait_ge(s("f_prod"), g * 2 + (c + 1))
                    act_(o_hi[:, 2 * par + c, :], f_a[:, c, :], ACT.Copy).then_inc(s("f_hi"), 1)

            up(0, 0, True)
            with act.Fori(0, (FG - 1) // 2) as i:
                tiles.loop(i, 24)
                for q in range(2):
                    up(i * 2 + (q + 1), (q + 1) % 2, False)
                    tiles.n += 8
            tiles.end((FG - 1) // 2)
            tiles.n += 8

        if last_stage >= 7:
            for tt in range(NQB):
                act.wait_ge(s("out_full"), tt + 1)
                if tt >= 2:
                    act.wait_ge(s(f"out_stored{tt % 2}"), 16 * (tt // 2))
                act_(out_tok[:, tt % 2, :], [pX, pY][tt % 2][:], ACT.Copy).then_inc(s("out_ready"), 1)

    @block.vector
    def _(dve):
        v = nc.vector
        tiles = Count()
        chain = Chain(dve, dve_chain)
        d, w = chain.did, chain.wait
        TT, TS, STT = v.tensor_tensor, v.tensor_scalar, v.scalar_tensor_tensor
        MUL, ADD, SUB = ALU.mult, ALU.add, ALU.subtract

        def one(ins):
            d(ins)
            w()

        def full(t):
            dve.wait_ge(acc_full[t % 2], tiles.half(t))

        def freed(t):
            dve.wait_ge(acc_free[t % 2], tiles.half(t))

        dve.wait_ge(s("rows_in"), 16 * N_ROWS)
        d(TT(lam_pr[:, 0:1], lam_in[:, 0:1], lam_in[:, 1:2], MUL))
        d(TT(lam_pr[:, 1:2], lam_in[:, 2:3], lam_in[:, 3:4], MUL))
        v.tensor_copy(rows_s[:, 2, :].rearrange("p (g q) -> p g q", g=2),
                      dt_row[:].unsqueeze(2).to_broadcast([PAIRS, 2, S5P])).then_inc(s("dt_rows"), 1)
        dve.wait_ge(s("cols_ready"), 1)
        one(STT(neg_lam[:], lam_e[:, 1:2], LAMBDA_INIT, lam_e[:, 0:1], SUB, SUB))
        d(TS(subg[:], cols[:, V_SUBG:V_SUBG + 1], 1.0 - LAMBDA_INIT, None, MUL))
        d(TS(qg[:], cols[:, V_QG:V_QG + 1], DD ** -0.5, None, MUL))

        def norm_head(tag):
            dve.wait_ge(s(f"sq_summed{tag}"), KD)
            one(TS(n_rstd[:], pY[:], 1.0 / D, EPS, MUL, ADD))
            v.reciprocal(n_rstd[:], n_rstd[:]).then_inc(s(f"nrm_inv{tag}"), 1)

        def norm_rest(tag, X, scale, shift):
            dve.wait_ge(s(f"nrm_rstd{tag}"), 1)

            def lo(k):
                dve.wait_ge(s(f"nrm_hi{tag}"), k + 1)
                TT(h_lo[:, k, :], n_tmp[:, k % 2, :], h_hi[:, k, :].bitcast(F32), SUB).then_inc(s(f"h_ready{tag}"), 1)
            for k in range(KD):
                if k >= 2:
                    dve.wait_ge(s(f"h_ready{tag}"), k - 1)
                one(TT(n_tmp[:, k % 2, :], X[:, k, :], n_rstd[:], MUL))
                TS(n_tmp[:, k % 2, :], n_tmp[:, k % 2, :], scale[:, k:k + 1], mod[:, shift + k:shift + k + 1],
                   MUL, ADD).then_inc(s(f"nrm_t{tag}"), 1)
                if k:
                    lo(k - 1)
            lo(KD - 1)

        norm_head(1)
        dve.wait_ge(s("ada_used"), 12)
        one(TT(mod[:], pA[:, 512:560], cols[:, V_ADAB:V_ADAB + 48], ADD))
        d(STT(scale1[:], mod[:, M_SC1:M_SC1 + 8], 1.0, cols[:, V_N1:V_N1 + 8], ADD, MUL))
        STT(scale2[:], mod[:, M_SC2:M_SC2 + 8], 1.0, cols[:, V_N2:V_N2 + 8], ADD, MUL).then_inc(s("mod_ready"), 1)
        dve.wait_ge(s("mod_ready"), 1)
        norm_rest(1, xT0, scale1, M_SH1)

        def expm1(out_m1, out_e, x):
            one(TS(e_x[:], x, -87.3, 88.7, ALU.max, ALU.min))
            one(TS(e_n[:], e_x[:], 1.0 / math.log(2.0), 12582912.0, MUL, ADD))
            one(TS(e_n[:], e_n[:], 12582912.0, None, SUB))
            one(STT(e_r[:], e_n[:], -0.693145751953125, e_x[:], MUL, ADD))
            one(STT(e_r[:], e_n[:], -1.4286068203094172e-06, e_r[:], MUL, ADD))
            one(TS(e_q[:], e_r[:], 1.0 / 8, 1.0, MUL, ADD))
            for k in range(7, 1, -1):
                one(STT(e_q[:], e_q[:], 1.0 / k, e_r[:], MUL, MUL))
                one(TS(e_q[:], e_q[:], 1.0, None, ADD))
            one(TT(e_q[:], e_q[:], e_r[:], MUL))
            one(TS(e_n[:], e_n[:], 127.0, 8388608.0, ADD, MUL))
            one(v.tensor_copy(e_int[:], e_n[:]))
            two_n = e_int[:].bitcast(F32)
            one(TT(e_q[:], e_q[:], two_n, MUL))
            one(TT(out_e, e_q[:], two_n, ADD))
            one(STT(out_m1, two_n, 1.0, e_q[:], SUB, ADD))

        def cmul(oi, ar, ai, br, bi, tmp):
            d(TT(tmp[0], ar, br, MUL))
            d(TT(tmp[1], ai, bi, MUL))
            d(TT(tmp[2], ar, bi, MUL))
            one(TT(tmp[3], ai, br, MUL))
            d(TT(oi[0], tmp[0], tmp[1], SUB))
            one(TT(oi[1], tmp[2], tmp[3], ADD))

        one(TS(l_re[:], l_re[:], 1.0, None, MUL))
        expm1(e_em[:], l_dt[:], l_dt[:])
        one(TT(th[:], l_im[:], l_dt[:], MUL))
        one(TS(sn[:], th[:], 1.0 / (2 * math.pi), 12582912.0, MUL, ADD))
        one(TS(sn[:], sn[:], 12582912.0, None, SUB))
        for c in (-6.28125, -0.0019340515136718750, -1.2556659146e-06):
            one(STT(th[:], sn[:], c, th[:], MUL, ADD))
        TS(th[:], th[:], -3.1415925, 3.1415925, ALU.max, ALU.min).then_inc(s("angle_ready"), 1)
        one(TT(cosv[:], l_re[:], l_dt[:], MUL))
        expm1(e_em[:], e_e[:], cosv[:])
        dve.wait_ge(s("sines"), 1)
        one(TT(cm[:], sh[:], sh[:], MUL))
        one(TS(cm[:], cm[:], -2.0, None, MUL))
        one(TS(cosv[:], cm[:], 1.0, None, ADD))
        one(TT(cr[:], e_e[:], cm[:], MUL))
        one(TT(cr[:], cr[:], e_em[:], ADD))
        one(TT(ci[:], e_e[:], sn[:], MUL))
        L = [Lp[0], Lp[1]]
        d(v.memset(L[0][:, :, 0], 1.0))
        d(v.memset(L[1][:, :, 0], 0.0))
        d(TS(L[0][:, :, 1], cr[:], 1.0, None, ADD))
        one(v.tensor_copy(L[1][:, :, 1], ci[:]))

        def small_tmp(n):
            return [s_tt[:, q, 0:PAIRS * n].rearrange("p (a b) -> p a b", b=n) for q in range(4)]

        def wide(t, n):
            return t.to_broadcast([P, PAIRS, n])

        for lo_, n in ((1, 1), (1, 2), (1, 4)):
            cmul([L[r][:, :, n + 1:2 * n + 1] for r in range(2)], L[0][:, :, 1:n + 1], L[1][:, :, 1:n + 1],
                 wide(L[0][:, :, n:n + 1], n), wide(L[1][:, :, n:n + 1], n), small_tmp(n))
        one(TT(inv[:], l_re[:], l_re[:], MUL))
        one(TT(wv_re[:], l_im[:], l_im[:], MUL))
        one(TT(inv[:], inv[:], wv_re[:], ADD))
        one(v.reciprocal(inv[:], inv[:]))
        d(TT(e_x[:], cr[:], l_re[:], MUL))
        d(TT(e_n[:], ci[:], l_im[:], MUL))
        d(TT(e_r[:], ci[:], l_re[:], MUL))
        one(TT(e_q[:], cr[:], l_im[:], MUL))
        d(TT(wv_re[:], e_x[:], e_n[:], ADD))
        one(TT(wv_im[:], e_r[:], e_q[:], SUB))
        d(TT(wv_re[:], wv_re[:], inv[:], MUL))
        one(TT(wv_im[:], wv_im[:], inv[:], MUL))
        dve.wait_ge(s("s5_b_in"), 16 * 4)
        cmul([s_Bb[0][:], s_Bb[1][:]], s_B[0][:], s_B[1][:], wv_re[:].unsqueeze(2).to_broadcast([P, PAIRS, S5H]),
             wv_im[:].unsqueeze(2).to_broadcast([P, PAIRS, S5H]), small_tmp(S5H))
        for r in range(2):
            for j in range(LC):
                d(v.tensor_copy(s_LR[r][:, :, j], L[r][:, :, LC - 1 - j]))
        w()
        HP = PAIRS // 2
        for hp in range(2):
            q = slice(hp * HP, hp * HP + HP)
            sh4 = [P, HP, LC, S5H]
            tmp = [s_tt[:, n, 0:1024].rearrange("p (a b c) -> p a b c", a=HP, b=LC) for n in range(4)]
            cmul([s_Ppre[r][:, q, :].rearrange("p a (b c) -> p a b c", b=LC) for r in range(2)],
                 s_Bb[0][:, q, :].unsqueeze(2).to_broadcast(sh4), s_Bb[1][:, q, :].unsqueeze(2).to_broadcast(sh4),
                 s_LR[0][:, q, :].unsqueeze(3).to_broadcast(sh4), s_LR[1][:, q, :].unsqueeze(3).to_broadcast(sh4), tmp)
        v.memset(junk[:], 0.0).then_inc(s("Ppre_ready"), 1)
        dve.wait_ge(s("C_copied"), 1)
        dve.wait_ge(s("xT_stored"), 16)
        for hp in range(2):
            q = slice(hp * HP, hp * HP + HP)
            sh4 = [P, HP, 9, S5H]
            tmp = [s_tt[:, n, :].rearrange("p (a b c) -> p a b c", a=HP, b=9) for n in range(4)]
            ins4 = [(s_C[r][:, q, :].unsqueeze(2).to_broadcast(sh4)) for r in range(2)]
            lam4 = [(L[r][:, q, :].unsqueeze(3).to_broadcast(sh4)) for r in range(2)]
            d(TT(tmp[0], ins4[0], lam4[0], MUL))
            d(TT(tmp[1], ins4[1], lam4[1], MUL))
            d(TT(tmp[2], ins4[0], lam4[1], MUL))
            one(TT(tmp[3], ins4[1], lam4[0], MUL))
            d(TT(s_G[0][:, q], tmp[0], tmp[1], SUB))
            one(STT(s_G[1][:, q].rearrange("p a b c -> p (a b c)"), s_tt[:, 2, :], -1.0, s_tt[:, 3, :], MUL, SUB))
        v.memset(junk[:], 0.0).then_inc(s("G_ready"), 1)
        dve.wait_ge(s("u_out"), 16 * S5T)
        v.memset(s_Toep[:], 0.0).then_inc(s("Toep_zero"), 1)
        dve.wait_ge(s("K_copied"), 4)
        u_r, u_i = cosv, sn
        for sq in range(3):
            cmul([u_r[:], u_i[:]], u_r[:], u_i[:], u_r[:], u_i[:], [e_x[:], e_n[:], e_r[:], e_q[:]])
            one(TT(e_e[:], e_e[:], e_e[:], MUL))
        d(v.tensor_copy(s_E[0][:, :, 0], u_r[:]))
        one(v.tensor_copy(s_E[1][:, :, 0], u_i[:]))
        st = [s_t[:, 640 * q:640 * q + 640] for q in range(4)]
        for e in range(7):
            n = 1 << e
            step = min(n, 32)
            for c0 in range(0, n, step):
                tmp = [t[:, 0:PAIRS * step].rearrange("p (a b) -> p a b", b=step) for t in st]
                cmul([s_E[r][:, :, n + c0:n + c0 + step] for r in range(2)],
                     s_E[0][:, :, c0:c0 + step], s_E[1][:, :, c0:c0 + step],
                     wide(s_E[0][:, :, n - 1:n], step), wide(s_E[1][:, :, n - 1:n], step), tmp)
        dve.wait_ge(s("V_copied"), 4)
        for sign in (-1, 1):
            if sign == 1:
                for r in range(2):
                    for pr in range(PAIRS):
                        d(v.tensor_tensor_scan(s_V[r][:, pr, :], e_e[:, pr:pr + 1].to_broadcast([P, NC8]), s_V[r][:, pr, :],
                                               0.0, MUL, ADD))
                w()
                dve.wait_ge(s("V_full"), 4)
                for r in range(2):
                    d(v.memset(s_X[r][:, :, 0], 0.0))
            for q4 in range(4):
                q = slice(4 * q4, 4 * q4 + 4)
                tmp = [t[:, 0:512].rearrange("p (a b) -> p a b", b=NC8) for t in st]
                Er, Ei, Vr, Vi = s_E[0][:, q], s_E[1][:, q], s_V[0][:, q], s_V[1][:, q]
                d(TT(tmp[0], Er, Vr, MUL))
                d(TT(tmp[1], Ei, Vi, MUL))
                d(TT(tmp[2], Er, Vi, MUL))
                one(TT(tmp[3], Ei, Vr, MUL))
                if sign == -1:
                    d(TT(Vr, tmp[0], tmp[1], ADD))
                    one(TT(Vi, tmp[2], tmp[3], SUB))
                else:
                    d(TT(s_X[0][:, q, 1:NC8], tmp[0][:, :, 0:NC8 - 1], tmp[1][:, :, 0:NC8 - 1], SUB))
                    one(TT(s_X[1][:, q, 1:NC8], tmp[2][:, :, 0:NC8 - 1], tmp[3][:, :, 0:NC8 - 1], ADD))
        v.memset(junk[:], 0.0).then_inc(s("X_ready"), 1)
        dve.wait_ge(s("uP_in"), 16)
        dve.wait_ge(s("Yp_in"), 16)
        tiles.n += S5T

        def lo_gelu(t):
            dve.wait_ge(s("gelu_hi"), t + 1)
            TT(o_lo[:, t, :], s_Yp[:, t, :], o_hi[:, t, :].bitcast(F32), SUB).then_inc(s("gelu_split"), 1)
        for t in range(S5T):
            STT(s_Yp[:, t, :], s_uP2[:, t, :], cols[:, V_S5D + t:V_S5D + t + 1], s_Yp[:, t, :], MUL, ADD).then_inc(s("yd_ready"), 1)
            if t:
                lo_gelu(t - 1)
        lo_gelu(S5T - 1)
        for t in range(S5T):
            n = tiles.next()
            freed(n)
            TT(s_res[:, t, :], s_Yp[:, t, :], s_sig[:], MUL).then_inc(s("glu_out"), 1)
        for t in range(S5T):
            dve.wait_ge(s("s5_hi"), t + 1)
            vw = lambda x: x.rearrange("p (c j) -> p j c", j=LC)
            TT(vw(o_lo[:, t, :]), s_res[:, t, :].rearrange("p (j c) -> p j c", j=LC), vw(o_hi[:, t, :].bitcast(F32)),
               SUB).then_inc(s("s5_split"), 1)

        def merge(first, base=0):
            with dve.Fori(0, 2) as i:
                tiles.loop(i, 8)
                for j in (0, 2):
                    g0 = tiles.n
                    tiles.n += 2
                    for q in range(2):
                        n = tiles.next()
                        freed(g0 + q)
                        full(n)
                        m_out = M[:, bass.ds(i * 4 + (j + q), 1), :].rearrange("p a b -> p (a b)")
                        if first:
                            TT(m_out, acc[n % 2][:], m_sig[:, q, :], MUL).then_inc(acc_free[n % 2], 1)
                        else:
                            TT(m_t[:], acc[n % 2][:], m_sig[:, q, :], MUL).then_inc(acc_free[n % 2], 1)
                            freed(n)
                            TT(m_out, m_out, m_t[:], ADD).then_inc(s("merged_add"), 1)
                            dve.wait_ge(s("merged_add"), i * 4 + (base + j + q + 1))
            tiles.end(2)

        if last_stage >= 2:
            merge(True)

        if last_stage >= 3:
            tiles.n += 2
            with dve.Fori(0, GLA_PAIRS) as i:
                tiles.loop(i, 6)
                chain.loop(i, 17)
                v.tensor_copy(gkw_cur[:], gkw[:, bass.ds(i * P, P)]).then_inc(s("gkw_ready"), 1)
                dve.wait_ge(s("z_full"), i + 1)
                TS(g_kinv[:], pX[:], cols[:, bass.ds(V_GKB + i, 1)], None, ADD).then_inc(s("g_z"), 1)
                dve.wait_ge(s("g_ln"), i + 1)
                one(STT(g_kinv[:], g_kinv[:], 0.0, g_eb[:], ALU.min, SUB))
                for n in range(NCH):
                    t0 = n * GLA_CHUNK
                    ins = v.tensor_tensor_scan(g_S[:, t0:t0 + GLA_CHUNK], ones[:, 0:GLA_CHUNK], g_kinv[:, t0:t0 + GLA_CHUNK],
                                               0.0, MUL, ADD)
                ins.then_inc(s("g_S_ready"), 1)
                dve.wait_ge(s("g_S_ready"), i + 1)
                Sv = v3(g_S, NCH)
                TT(v3(g_kl, NCH), Sv[:, :, GLA_CHUNK - 1:GLA_CHUNK].to_broadcast([P, NCH, GLA_CHUNK]), Sv, SUB
                   ).then_inc(s("g_kx_ready"), 1)
                n = tiles.next()
                full(n)
                dve.wait_ge(s("g_klx"), i + 1)
                TT(g_kl[:], acc[n % 2][:], g_kl[:], MUL).then_inc(s("kl_ready"), 1)
                TT(g_kinv[:], acc[n % 2][:], g_kinv[:], MUL).then_inc(acc_free[n % 2], 1)
                n = tiles.next()
                full(n)
                STT(g_qd[:], acc[n % 2][:], GLA_DK ** -0.5, g_eb[:], MUL, MUL).then_inc(acc_free[n % 2], 1)
                tiles.n += 4
                one(v.memset(g_S0[:, 0, :], 0.0))
                for n in range(NCH - 1):
                    if n % 8 == 0:
                        dve.wait_ge(s("ds_full"), i * 2 + (n // 8 + 1))
                    ins = STT(g_S0[:, n + 1, :], g_S0[:, n, :], g_eb[:, 64 * n + 63:64 * n + 64],
                              [pX, pY][n // 8][:, ds_col(n):ds_col(n) + P], MUL, ADD)
                    if n < NCH - 2:
                        one(ins)
                ins.then_inc(s("S0_ready"), 1)
                one(v.memset(g_attn[:], 0.0))
                for hd in range(2):
                    dve.wait_ge(s("attn_full"), i * 2 + (hd + 1))
                    settle(dve)
                    v.copy_predicated(g_attn[:], gla_mask[:].unsqueeze(1).to_broadcast([P, 8, P]), v3(pX, 8)
                                      ).then_inc(s("attn_ready"), 1)
                    no = i * 2 + (hd + 1)
                    dve.wait_ge(s("g_ss_full"), no)
                    TS(g_rstd[:], pX[:], 1.0 / GLA_DV, EPS, MUL, ADD).then_inc(s("g_rstd_var"), 1)
                    dve.wait_ge(s("g_rstd_var"), no)
                    v.reciprocal(g_rstd[:], g_rstd[:]).then_inc(s("g_inv"), 1)
                    dve.wait_ge(s("g_rstd_ready"), no)
                    STT(g_sq[:], pY[:], cols[:, V_GLAG:V_GLAG + 1], g_rstd[:], MUL, MUL).then_inc(s("g_o_read"), 1)
                    dve.wait_ge(s("g_o_read"), no)
                    TT(g_sq[:], g_sq[:], g_sil[:], MUL).then_inc(s("g_y_ready"), 1)
                    dve.wait_ge(s("g_hi"), no)
                    slot = bass.ds(i * 2 + hd, 1)
                    TT(o_lo[:, slot, :].rearrange("p a b -> p (a b)"), g_sq[:],
                       o_hi[:, slot, :].rearrange("p a b -> p (a b)").bitcast(F32), SUB).then_inc(s("gla_split"), 1)
            tiles.end(GLA_PAIRS)
            chain.end(GLA_PAIRS)
            merge(False)

        if last_stage >= 4:
            dve.wait_ge(s("R_in"), 16)
            with dve.Fori(0, DH // 2) as i:
                tiles.loop(i, 38)
                chain.loop(i, 54)
                for hh in range(2):
                    one(TS(d_R[:], d_R[:], 0.25, None, MUL))
                    for qk in range(2):
                        no = i * 4 + (2 * hh + qk + 1)
                        n = tiles.next()
                        dve.wait_ge(s("d_ss_full"), no)
                        TS(d_rs[:], pX[:], 1.0 / DD, EPS, MUL, ADD).then_inc(s("d_var_read"), 1)
                        dve.wait_ge(s("d_var_read"), no)
                        v.reciprocal(d_rs[:], d_rs[:]).then_inc(s("d_inv"), 1)
                        dve.wait_ge(s("d_rstd_ready"), no)
                        full(n)
                        STT([d_q, d_k][qk][:], acc[n % 2][:], [qg[:], cols[:, V_KG:V_KG + 1]][qk], d_rs[:], MUL, MUL
                            ).then_inc(acc_free[n % 2], 1)
                        freed(n)
                    tiles.n += 1

                    def maxima(qb):
                        kw = (qb + 1) * QB
                        if qb >= 2:
                            dve.wait_ge(s("d_wT_full"), i * 16 + (8 * hh + qb - 1))
                        for j in range(2):
                            n = tiles.next()
                            full(n)
                            settle(dve)
                            v.tensor_tensor_reduce(out=d_s[:, qb % 2, j, 0:kw], in0=acc[n % 2][:, 0:kw],
                                                   in1=d_R[:, T - kw:T], scale=1.0, scalar=-3e38, op0=ADD, op1=ALU.max,
                                                   accum_out=mx[:, qb % 2, j:j + 1]).then_inc(acc_free[n % 2], 1)
                        freed(n)
                        TS(nmx[:, qb % 2, :], mx[:, qb % 2, :], -1.0, None, MUL).then_inc(s("d_mx_ready"), 1)

                    maxima(0)
                    for qb in range(NQB):
                        if qb + 1 < NQB:
                            maxima(qb + 1)
                        kw, b = (qb + 1) * QB, qb % 2
                        dve.wait_ge(s("d_p_ready"), i * 16 + (8 * hh + qb + 1))
                        one(v.reciprocal(rinv[:, b, :], rsum[:, b, :]))
                        one(TT(rinv[:, b, 1:2], rinv[:, b, 1:2], neg_lam[:], MUL))
                        one(TS(d_s[:, b, 1, 0:kw], d_s[:, b, 1, 0:kw], rinv[:, b, 1:2], None, MUL))
                        STT(d_s[:, b, 0, 0:kw], d_s[:, b, 0, 0:kw], rinv[:, b, 0:1], d_s[:, b, 1, 0:kw], MUL, ADD
                            ).then_inc(s("d_w_ready"), 1)
                        if qb % 4 == 3:
                            grp = qb // 4
                            no = i * 4 + (2 * hh + grp + 1)
                            dve.wait_ge(s("d_oss_full"), no)
                            one(TS(pY[:, HALF:T], pY[:, HALF:T], 1.0 / (2 * DD), EPS, MUL, ADD))
                            v.reciprocal(pY[:, HALF:T], pY[:, HALF:T]).then_inc(s("d_oinv"), 1)
                            dve.wait_ge(s("d_orstd"), no)
                            STT(o_sq[:], pY[:, 0:HALF], subg[:], o_sq[:], MUL, MUL).then_inc(s("d_o_read"), 1)
                            dve.wait_ge(s("d_hi"), no)
                            pos = (slice(None), bass.ds(i * 2 + hh, 1), slice(grp * HALF, (grp + 1) * HALF))
                            TT(o_lo[pos].rearrange("p a b -> p (a b)"), o_sq[:],
                               o_hi[pos].rearrange("p a b -> p (a b)").bitcast(F32), SUB).then_inc(s("diff_split"), 1)
            tiles.end(DH // 2)
            chain.end(DH // 2)
            merge(False, KD)

        if last_stage >= 5:
            for k in range(KD):
                dve.wait_ge(s("merged_hi"), k + 1)
                ins = TT(h_lo[:, k, :], M[:, k, :], h_hi[:, k, :].bitcast(F32), SUB)
            ins.then_inc(s("merged_split"), 1)
            dve.wait_ge(s("xT_in"), 16)
            with dve.Fori(0, 4) as i:
                tiles.loop(i, 2)
                for j in range(2):
                    n = tiles.next()
                    full(n)
                    mk_ = M[:, bass.ds(i * 2 + j, 1), :].rearrange("p a b -> p (a b)")
                    STT(mk_, acc[n % 2][:], mod[:, bass.ds(M_GT1 + j + i * 2, 1)], mk_, MUL, ADD).then_inc(acc_free[n % 2], 1)
            tiles.end(4)
            norm_head(2)
            norm_rest(2, M, scale2, M_SH2)

        if last_stage >= 6:
            def up(g, par):
                for c in range(2):
                    for ag in range(2):
                        n = tiles.next()
                        full(n)
                        dve.wait_ge(s("f_lin"), g * 4 + (2 * c + ag + 1))
                        buf = [f_a, f_g][ag][:, c, :]
                        ch = V_CONV + 22 * ag + g * 2 + c
                        one(STT(buf[:, 1:T], acc[n % 2][:, 0:T - 1], cols[:, bass.ds(ch + NT_FF, 1)], buf[:, 1:T], MUL, ADD))
                        STT(buf[:, 2:T], acc[n % 2][:, 0:T - 2], cols[:, bass.ds(ch, 1)], buf[:, 2:T], MUL, ADD
                            ).then_inc(acc_free[n % 2], 1)
                    freed(n)
                    dve.wait_ge(s("f_silu"), g * 2 + (c + 1))
                    TT(f_a[:, c, :], f_a[:, c, :], f_g[:, c, :], MUL).then_inc(s("f_prod"), 1)
                    dve.wait_ge(s("f_hi"), g * 2 + (c + 1))
                    TT(o_lo[:, 2 * par + c, :], f_a[:, c, :], o_hi[:, 2 * par + c, :].bitcast(F32), SUB).then_inc(s("act_split"), 1)

            def down():
                for m in range(KD):
                    n = tiles.next()
                    full(n)
                    STT(M[:, m, :], acc[n % 2][:], mod[:, M_GT2 + m:M_GT2 + m + 1], M[:, m, :], MUL, ADD).then_inc(acc_free[n % 2], 1)

            up(0, 0)
            with dve.Fori(0, (FG - 1) // 2) as i:
                tiles.loop(i, 24)
                chain.loop(i, 8)
                for q in range(2):
                    up(i * 2 + (q + 1), (q + 1) % 2)
                    down()
            tiles.end((FG - 1) // 2)
            chain.end((FG - 1) // 2)
            down()

    ctx.close()


_INS = ["x", "c", "ada_w", "ada_b", "norm1_g", "w_in", "gla_gk_w", "gla_gk_b", "gla_norm_g", "s5_lambda_re",
        "s5_lambda_im", "s5_b_re", "s5_b_im", "s5_c_re", "s5_c_im", "s5_d", "s5_log_dt", "s5_glu_w", "s5_glu_b",
        "diff_q_norm_g", "diff_k_norm_g", "diff_lambda_q1", "diff_lambda_k1", "diff_lambda_q2", "diff_lambda_k2",
        "diff_subln_g", "w_branch_gla", "w_branch_s5", "w_branch_diff", "w_out", "norm2_g", "ffn_w_up",
        "ffn_conv_w", "ffn_conv_b", "ffn_w_down"]


def kernel(**inputs):
    import numpy as np
    import concourse.bacc as bacc
    from concourse.bass_utils import run_bass_kernel_spmd

    nc = bacc.Bacc("TRN2", target_bir_lowering=False, num_devices=1)
    arrays, aps = {}, {}
    for name in _INS:
        arr = np.ascontiguousarray(inputs[name])
        arrays[f"in_{name}"] = arr
        aps[name] = nc.dram_tensor(f"in_{name}", arr.shape, mybir.dt.from_np(arr.dtype), kind="ExternalInput").ap()
    aps["out"] = nc.dram_tensor("out_0", (1, T, D), F32, kind="ExternalOutput").ap()
    build(nc, aps)
    r = run_bass_kernel_spmd(nc, [arrays], core_ids=[0])
    return r.results[0]["out_0"]
```

```python
import math

import concourse.bass as bass
from concourse import mybir
from contextlib import ExitStack

F32 = mybir.dt.float32
F32R = mybir.dt.float32r
I32 = mybir.dt.int32
ALU = mybir.AluOpType
ACT = mybir.ActivationFunctionType
AX = mybir.AxisListType

P = 128
D = 1024
T = 1024
KD = D // P
HALF = 512
GLA_HEADS, GLA_DK, GLA_DV, GLA_LR, GLA_CHUNK = 4, 64, 128, 16, 64
GLA_PAIRS = GLA_HEADS // 2
NCH = T // GLA_CHUNK
S5W, S5G, S5H, S5P = 512, 32, 16, 64
S5T = S5W // P
PAIRS = S5G // 2
LC = 8
NC8 = T // LC
GATE_AT = (2, 5)
DH, DD = 4, 64
QB = 128
NQB = T // QB
F = 2816
FG = F // 256
N_ROWS = 24
EPS = 1e-6
LAMBDA_INIT = 0.8 - 0.6 * math.exp(-0.3 * 0)

C_GQ = 0
C_GK = C_GQ + GLA_HEADS * GLA_DK
C_GV = C_GK + GLA_HEADS * GLA_DK
C_GR = C_GV + GLA_HEADS * GLA_DV
C_LR = C_GR + GLA_HEADS * GLA_DV
C_SU = C_LR + GLA_LR
C_DQ = C_SU + S5W
C_DK = C_DQ + DH * 2 * DD
C_DV = C_DK + DH * 2 * DD
C_GATE = C_DV + DH * 2 * DD

V_ADAB, V_N1, V_N2, V_C, V_GKB, V_S5D, V_GLUB, V_GLAG, V_SUBG, V_QG, V_KG, V_ROWS = (
    0, 48, 56, 64, 72, 74, 78, 82, 83, 84, 85, 86)
V_CONV = V_ROWS
NT_FF = 2 * F // P
V_CONVB = V_CONV + 3 * NT_FF
V_END = V_CONVB + NT_FF
M_SH1, M_SC1, M_GT1, M_SH2, M_SC2, M_GT2 = 0, 8, 16, 24, 32, 40


class Chain:

    def __init__(self, eng, sem):
        self.eng, self.sem, self.n, self.extra, self.base, self.per = eng, sem, 0, 0, 0, 0

    def loop(self, reg, per):
        self.base, self.per, self.extra = self.n, per, reg * per

    def end(self, count):
        assert self.n - self.base == self.per, (self.n - self.base, self.per)
        self.n, self.extra = self.base + self.per * count, 0

    def did(self, ins):
        ins.then_inc(self.sem, 1)
        self.n += 1

    def wait(self):
        self.eng.wait_ge(self.sem, self.extra + self.n)


class Count:

    def __init__(self):
        self.n, self.reg, self.per, self.base = 0, None, 0, 0

    def loop(self, reg, per):
        assert per % 2 == 0 and self.n % 2 == 0
        self.base, self.reg, self.per = self.n, reg, per

    def end(self, count):
        assert self.n - self.base == self.per, (self.n - self.base, self.per)
        self.n, self.reg = self.base + self.per * count, None

    def next(self):
        self.n += 1
        return self.n - 1

    def whole(self, n):
        return n + 1 if self.reg is None else self.reg * self.per + (n + 1)

    def half(self, n):
        return n // 2 + 1 if self.reg is None else self.reg * (self.per // 2) + (n // 2 + 1)


def build(nc, a, last_stage=99):
    w_in = a["w_in"][0]
    ctx = ExitStack()

    KB = 1024
    ctx.enter_context(nc.sbuf_tensor("slab", [P, 415 * 128], F32))
    BASE = 16512

    def at(name, shape, dt, off):
        return nc.alloc_sbuf_tensor_at(name, shape, dt, offset=BASE + off)

    small = [0]

    def const(name, shape, dt=F32):
        n = 4
        for s in shape[1:]:
            n *= s
        t = at(name, shape, dt, small[0])
        small[0] += (n + 31) // 32 * 32
        return t

    ident = const("ident", [P, P])
    ones = const("ones", [P, P])
    half_ones = const("half_ones", [P, P])
    gla_mask = const("gla_mask", [P, P], I32)
    cols = const("cols", [P, V_END])
    mod = const("mod", [P, 48])
    scale1 = const("scale1", [P, KD])
    scale2 = const("scale2", [P, KD])
    c_act = const("c_act", [P, KD])
    eps_col = const("eps_col", [P, 1])
    one_col = const("one_col", [P, 1])
    gkw = const("gkw", [GLA_LR, GLA_HEADS * GLA_DK])
    gkw_cur = const("gkw_cur", [GLA_LR, P])
    junk = const("junk", [P, 2])
    lam_in = const("lam_in", [DD, 4])
    lam_pr = const("lam_pr", [DD, 2])
    lam_e = const("lam_e", [P, 2])
    neg_lam = const("neg_lam", [P, 1])
    subg = const("subg", [P, 1])
    qg = const("qg", [P, 1])
    mx = const("mx", [P, 2, 2])
    nmx = const("nmx", [P, 2, 2])
    rsum = const("rsum", [P, 2, 2])
    rinv = const("rinv", [P, 2, 2])
    assert small[0] <= 6 * KB - 512, small[0]
    o_sq = at("o_sq", [P, HALF], F32, 6 * KB - 512)
    w_raw = at("w_raw", [P, 2, 8, P], F32, 8 * KB - 512)
    w_hi = at("w_hi", [P, 2, 8, P], F32R, 16 * KB - 512)
    w_lo = at("w_lo", [P, 2, 8, P], F32R, 24 * KB - 512)
    H0, O0, M0, A0 = 32 * KB - 512, 96 * KB - 512, 128 * KB - 512, 160 * KB - 512
    h_hi = at("h_hi", [P, KD, T], F32R, H0)
    h_lo = at("h_lo", [P, KD, T], F32R, H0 + 32 * KB)
    o_hi = at("o_hi", [P, 4, T], F32R, O0)
    o_lo = at("o_lo", [P, 4, T], F32R, O0 + 16 * KB)
    M = at("M", [P, KD, T], F32, M0)

    rows_a = at("rows_a", [P, P], F32, H0)
    rows_b = at("rows_b", [P, P], F32, H0 + 512)
    R0 = at("R0", [P, T], F32, H0 + 8 * KB)
    rows_c = at("rows_c", [P, P], F32, H0 + KB)
    x_tok = at("x_tok", [P, NQB, D], F32, O0)
    ada_v = a["ada_w"][0].rearrange("(k p) c -> p k c", p=P)
    ada_rings = [at(f"ada_ring{q}", [P, 2, KD, HALF], F32, (M0, A0)[q]) for q in range(2)]
    ada_sums = [at(f"ada_sum{q}", [P, 2, HALF], F32, (H0 + 16 * KB, A0 + 36 * KB)[q]) for q in range(2)]
    xT0 = at("xT0", [P, KD, T], F32, A0)
    n_tmp = at("n_tmp", [P, 2, T], F32, A0 + 36 * KB)
    n_rstd = at("n_rstd", [P, T], F32, O0 + 18 * KB)

    pA = ctx.enter_context(nc.psum_tensor("pA", [P, T], F32))
    pB = ctx.enter_context(nc.psum_tensor("pB", [P, T], F32))
    pX = ctx.enter_context(nc.psum_tensor("pX", [P, T], F32))
    pY = ctx.enter_context(nc.psum_tensor("pY", [P, T], F32))
    acc = [pA, pB]

    def sem(name):
        return ctx.enter_context(nc.semaphore(name))

    w_loaded = [sem("w_loaded0"), sem("w_loaded1")]
    w_hi_done = sem("w_hi_done")
    w_split = sem("w_split")
    w_started = sem("w_started")
    acc_full = [sem("acc_full0"), sem("acc_full1")]
    acc_free = [sem("acc_free0"), sem("acc_free1")]
    act_chain, dve_chain, pool_chain = sem("act_chain"), sem("dve_chain"), sem("pool_chain")

    settled = {e.engine: sem(f"settled_{n}") for n, e in
               (("sp", nc.sync), ("pool", nc.gpsimd), ("pe", nc.tensor), ("dve", nc.vector))}
    block = ctx.enter_context(nc.Block())
    S = {}
    total_units = [0]

    def s(name):
        if name not in S:
            S[name] = sem(name)
        return S[name]

    def settle(eng):
        eng.sem_inc(settled[eng.engine], 1)

    def ds_col(n):
        return HALF * (n % 2) + P * (n % 8 // 2)

    def v3(t, n):
        return t.rearrange("p (a b) -> p a b", a=n)

    def gemm(pe, units, tiles, new_unit, ks, rhs_hi, rhs_lo, ready=None):
        if new_unit:
            u = units.next()
            pe.wait_ge(w_split, units.whole(u))
        else:
            u = units.n - 1
        t = tiles.next()
        if t >= 2:
            pe.wait_ge(acc_free[t % 2], tiles.half(t) - 1)
        dst = acc[t % 2]
        n, total = 0, len(ks) * 6
        for k, w in ks:
            if ready is not None:
                pe.wait_ge(ready, k + 1)
            for wp, rp in ((w_hi, rhs_hi), (w_hi, rhs_lo), (w_lo, rhs_hi)):
                for hf in range(2):
                    ins = nc.tensor.matmul(dst[:, hf * HALF:(hf + 1) * HALF], wp[:, u % 2, w, :],
                                           rp[:, k, hf * HALF:(hf + 1) * HALF],
                                           start=(n < 2), stop=(n >= total - 2))
                    if n == 0 and new_unit:
                        ins.then_inc(w_started, 1)
                    n += 1
        ins.then_inc(acc_full[t % 2], 1)

    K8 = [(k, k) for k in range(8)]

    def gemm_h(pe, units, tiles, ready=None):
        gemm(pe, units, tiles, True, K8, h_hi, h_lo, ready)

    def load(sp, units, src, view):
        u = units.next()
        if u >= 2:
            sp.wait_ge(w_split, units.whole(u) - 2)
            settle(sp)
        sp.dma_start(view(w_raw[:, u % 2]), src).then_inc(w_loaded[u % 2], 16)

    def load_cols(sp, units, w, col):
        load(sp, units, w[:, bass.ds(col, P)].rearrange("(k p) c -> p k c", p=P), lambda t: t)

    def load_k4(sp, units, w, col):
        load(sp, units, w[:, bass.ds(col, 256)].rearrange("(k p) c -> p k c", p=P),
             lambda t: t.rearrange("p (k c) n -> p k (c n)", k=4))

    def load_down(sp, units, w, row, col):
        load(sp, units, w[bass.ds(row, 256), col:col + 512].rearrange("(k p) c -> p k c", p=P),
             lambda t: t.rearrange("p (k c) n -> p k (c n)", k=2))


    xT_dram = nc.dram_tensor("xT_scratch", (D, T), F32).ap()
    m_dram = nc.dram_tensor("merged_scratch", (D, T), F32).ap()
    R_dram = nc.dram_tensor("alibi_scratch", (P, T), F32).ap()
    u_dram = nc.dram_tensor("u_scratch", (S5W, T), F32).ap()
    y_dram = nc.dram_tensor("y_scratch", (S5W, T), F32).ap()

    rows_s = at("rows_s", [PAIRS, 3, P], F32, H0 + 2 * KB)
    dt_row = at("dt_row", [PAIRS, 2], F32, H0 + 4 * KB)
    s_G = [at(f"s_G{r}", [P, PAIRS, 9, S5H], F32, A0 + 9216 * r) for r in range(2)]
    s_U = at("s_U", [P, S5G, NC8], F32, A0 + 18 * KB)
    s_uP = at("s_uP", [P, S5T, LC, NC8], F32, M0 + 16 * KB)
    s_PT = [at(f"s_PT{r}", [P, PAIRS, P], F32, M0 + 8 * KB * r) for r in range(2)]
    s_Toep = at("s_Toep", [P, S5G, P], F32, M0 + 16 * KB)
    s_Ppre = [at(f"s_Ppre{r}", [P, PAIRS, P], F32, O0 + 8 * KB * r) for r in range(2)]
    s_K = at("s_K", [S5H, S5G, P], F32, O0)
    s_V = [at(f"s_V{r}", [P, PAIRS, NC8], F32, O0 + 8 * KB * r) for r in range(2)]
    s_E = [at(f"s_E{r}", [P, PAIRS, NC8], F32, O0 + 16 * KB + 8 * KB * r) for r in range(2)]
    s_t = at("s_t", [P, 4 * 512], F32, A0 + 36 * KB)
    s_Y = at("s_Y", [P, S5G, NC8], F32, O0 + 16 * KB)
    s_Yp = at("s_Yp", [P, S5T, T], F32, A0)
    s_uP2 = at("s_uP2", [P, S5T, T], F32, A0 + 18 * KB)
    s_sig = at("s_sig", [P, T], F32, A0 + 34 * KB)
    SM = A0 + 44 * KB

    small_end = [SM]

    def mk(name, shape, dt=F32):
        n = 4
        for x in shape[1:]:
            n *= x
        small_end[0] += (n + 31) // 32 * 32
        return at(name, shape, dt, small_end[0] - (n + 31) // 32 * 32)

    l_re, l_im, l_dt = mk("l_re", [P, PAIRS]), mk("l_im", [P, PAIRS]), mk("l_dt", [P, PAIRS])
    e_x, e_n, e_r, e_q, e_em, e_e = [mk(f"e_{i}", [P, PAIRS]) for i in range(6)]
    e_int = mk("e_int", [P, PAIRS], I32)
    th, sn, sh, cm = [mk(f"ph_{i}", [P, PAIRS]) for i in range(4)]
    cosv, cr, ci, inv = [mk(f"cc_{i}", [P, PAIRS]) for i in range(4)]
    wv_re, wv_im, mag8 = [mk(f"wv_{i}", [P, PAIRS]) for i in range(3)]
    Lp = [mk(f"Lp{r}", [P, PAIRS, 9]) for r in range(2)]
    assert small_end[0] <= A0 + 48 * KB
    s_LR = [at(f"s_LR{r}", [P, PAIRS, 8], F32, O0 + 24 * KB + 512 * r) for r in range(2)]
    s_B = [at(f"s_B{r}", [P, PAIRS, S5H], F32, O0 + 26 * KB + KB * r) for r in range(2)]
    s_Bb = [at(f"s_Bb{r}", [P, PAIRS, S5H], F32, A0 + 42 * KB + KB * r) for r in range(2)]
    s_C = [at(f"s_C{r}", [P, PAIRS, S5H], F32, O0 + 30 * KB + KB * r) for r in range(2)]
    c_rows = at("c_rows", [P, 2, 2, P], F32, O0 + 22 * KB)
    s_tt = at("s_tt", [P, 4, 2304 // 2], F32, A0 + 18 * KB)

    def blk(name, n, shape):
        return at(name, shape, F32, A0 + 4 * KB * n)
    g_lr = blk("g_lr", 0, [GLA_LR, T])
    g_S = blk("g_S", 1, [P, T])
    g_vT = blk("g_vT", 1, [P, T])
    g_rstd = blk("g_rstd", 1, [P, T])
    g_eb = blk("g_eb", 2, [P, T])
    g_kinv = blk("g_kinv", 3, [P, T])
    g_kl = blk("g_kl", 4, [P, T])
    g_attn = blk("g_attn", 4, [P, 8, P])
    g_qd = blk("g_qd", 5, [P, T])
    g_klT = blk("g_klT", 6, [P, 8, P])
    g_sq = blk("g_sq", 6, [P, T])
    g_S0 = blk("g_S0", 7, [P, NCH, P])
    g_v = blk("g_v", 9, [P, 2, 8, P])
    g_sil = blk("g_sil", 11, [P, T])

    d_R = blk("d_R", 0, [P, T])
    d_q = blk("d_q", 1, [P, T])
    d_k = blk("d_k", 2, [P, T])
    d_v = blk("d_v", 3, [P, 8, P])
    d_s = blk("d_s", 4, [P, 2, 2, T])
    d_tmp = blk("d_tmp", 4, [P, 2, T])
    d_wT = blk("d_wT", 8, [P, 8, 512])
    d_vT = blk("d_vT", 8, [P, T])
    d_rs = blk("d_rs", 9, [P, T])

    m_prev = blk("m_prev", 0, [P, KD, T])
    f_a = blk("f_a", 0, [P, 2, T])
    f_g = blk("f_g", 2, [P, 2, T])
    out_tok = blk("out_tok", 6, [P, 2, D])

    @block.sync
    def _(sp):
        units = Count()
        x_v = a["x"][0].rearrange("(n p) d -> p n d", p=P)
        for q in range(4):
            sp.dma_start(x_tok[:, 2 * q:2 * q + 2, :], x_v[:, 2 * q:2 * q + 2, :]).then_inc(s(f"x_in{q}"), 16)
        sp.wait_ge(s("rows_in"), 16 * N_ROWS)
        for n in range(4):
            if n >= 2:
                sp.wait_ge(s("ada_mult"), n - 1)
            sp.dma_start(ada_rings[0][:, n % 2], ada_v[:, :, n * HALF:(n + 1) * HALF]).then_inc(s(f"ada_in{n % 2}"), 16)
        sp.wait_ge(s("xT_copied"), KD)
        sp.dma_start(xT_dram.rearrange("(k p) t -> p k t", p=P), xT0[:]).then_inc(s("xT_stored"), 16)
        for r, nm in enumerate(("s5_b_re", "s5_b_im")):
            for gp in range(2):
                sp.dma_start(s_B[r][64 * gp:64 * gp + 64],
                             a[nm][0].rearrange("(r g) p h -> g p r h", g=2)[gp]).then_inc(s("s5_b_in"), 16)
        for r, nm in enumerate(("s5_c_re", "s5_c_im")):
            cv = a[nm][0].rearrange("(t r g) h p -> t g r h p", g=2, t=2)
            for t in range(2):
                for gp in range(2):
                    sp.dma_start(c_rows[:, r, t, 64 * gp:64 * gp + 64], cv[t, gp]).then_inc(s("s5_c_in"), 16)

        for t in range(S5T):
            load_cols(sp, units, w_in, C_SU + t * P)
        for g in range(2):
            load_cols(sp, units, w_in, C_GATE + D + g * P)
        for t in range(S5T):
            sp.wait_ge(acc_free[t % 2], t // 2 + 1)
            sp.dma_start(u_dram[t * P:(t + 1) * P, :], s_uP[:, t]).then_inc(s("u_out"), 16)
        sp.wait_ge(s("u_out"), 16 * S5T)
        sp.wait_ge(s("G_ready"), 1)
        u_v = u_dram.rearrange("(g h) (j c) -> j h g c", h=S5H, j=LC)
        for j in range(LC):
            sp.dma_start(s_U[16 * j:16 * j + 16], u_v[j]).then_inc(s("U_in"), 16)
        sp.wait_ge(s("K_copied"), 4)
        sp.wait_ge(s("Toep_zero"), 1)
        for j in range(LC):
            sp.dma_start(s_Toep[16 * j:16 * j + 16, :, 16 * j:P], s_K[:, :, 0:P - 16 * j]).then_inc(s("Toep_in"), 16)
        for g in range(2, 6):
            load_cols(sp, units, w_in, C_GATE + D + g * P)
        y_v = y_dram.rearrange("(g h) (j c) -> j h g c", h=S5H, j=LC)
        sp.wait_ge(s("Y_copied"), 4)
        for j in range(LC):
            sp.dma_start(y_v[j], s_Y[16 * j:16 * j + 16]).then_inc(s("y_out"), 16)
        for g in range(6, KD):
            load_cols(sp, units, w_in, C_GATE + D + g * P)
        sp.dma_start(s_uP2[:], u_dram.rearrange("(t p) n -> p t n", p=P)).then_inc(s("uP_in"), 16)
        sp.wait_ge(s("y_out"), 16 * LC)
        sp.dma_start(s_Yp[:], y_dram.rearrange("(t p) n -> p t n", p=P)).then_inc(s("Yp_in"), 16)
        load_k4(sp, units, a["s5_glu_w"][0], 0)
        load_k4(sp, units, a["s5_glu_w"][0], 256)

        def branch_loads(w):
            with sp.Fori(0, 2) as i:
                units.loop(i, 2)
                for j in (0, 2):
                    load_k4(sp, units, w, (i * 4 + j) * P)
            units.end(2)

        def gate_load(b, tile):
            load_cols(sp, units, w_in, C_GATE + b * D + tile * P)

        if last_stage >= 2:
            branch_loads(a["w_branch_s5"][0])
        if last_stage >= 3:
            load_cols(sp, units, w_in, C_LR)
            load_cols(sp, units, w_in, C_LR)
            with sp.Fori(0, GLA_PAIRS) as i:
                units.loop(i, 10)
                load_cols(sp, units, w_in, C_GK + i * P)
                load_cols(sp, units, w_in, C_GQ + i * P)
                load_cols(sp, units, w_in, C_GV + i * 256)
                load_cols(sp, units, w_in, C_GV + i * 256 + P)
                load_cols(sp, units, w_in, C_GR + i * 256)
                for f in range(3):
                    gate_load(0, i * 4 + f)
                load_cols(sp, units, w_in, C_GR + i * 256 + P)
                gate_load(0, i * 4 + 3)
            units.end(GLA_PAIRS)
            branch_loads(a["w_branch_gla"][0])
        if last_stage >= 4:
            sp.wait_ge(s("merged_add"), KD)
            sp.dma_start(d_R[:], R_dram).then_inc(s("R_in"), 16)
            with sp.Fori(0, DH // 2) as i:
                units.loop(i, 10)
                for hh in range(2):
                    for c in (C_DQ, C_DK, C_DV):
                        load_cols(sp, units, w_in, c + (i * 2 + hh) * P)
                    for f in range(2):
                        gate_load(2, i * 4 + (2 * hh + f))
            units.end(DH // 2)
            branch_loads(a["w_branch_diff"][0])
        if last_stage >= 5:
            with sp.Fori(0, 4) as i:
                units.loop(i, 2)
                for j in range(2):
                    load_cols(sp, units, a["w_out"][0], (i * 2 + j) * P)
            units.end(4)
        if last_stage >= 6:
            w_up, w_down = a["ffn_w_up"][0], a["ffn_w_down"][0]

            def up_loads(g):
                for c in (0, 1):
                    load_cols(sp, units, w_up, (g * 2 + c) * P)
                    load_cols(sp, units, w_up, (g * 2 + c) * P + F)

            def down_loads(g):
                load_down(sp, units, w_down, g * 256, 0)
                load_down(sp, units, w_down, g * 256, HALF)

            up_loads(0)
            with sp.Fori(0, (FG - 1) // 2) as i:
                units.loop(i, 12)
                for q in range(2):
                    up_loads(i * 2 + q + 1)
                    down_loads(i * 2 + q)
            units.end((FG - 1) // 2)
            down_loads(FG - 1)
        total_units[0] = units.n

        if last_stage >= 7:
            out_v = a["out"][0]
            for tt in range(NQB):
                sp.wait_ge(s("out_ready"), tt + 1)
                sp.dma_start(out_v[tt * P:(tt + 1) * P, :], out_tok[:, tt % 2]).then_inc(s(f"out_stored{tt % 2}"), 16)
            for q in range(2):
                sp.wait_ge(s(f"out_stored{q}"), 16 * (NQB // 2))

    @block.gpsimd
    def _(pool):
        g = nc.gpsimd
        chain = Chain(pool, pool_chain)
        d, w = chain.did, chain.wait
        d(g.memset(ident[:], 0.0))
        d(g.memset(ones[:], 1.0))
        d(g.memset(half_ones[:], 0.0))
        d(g.memset(eps_col[:], EPS))
        d(g.memset(one_col[:], 1.0))
        d(g.memset(gla_mask[:], 1))
        w()
        d(g.affine_select(out=ident[:], in_=ident[:], compare_op=ALU.not_equal, fill=1.0, base=0,
                          pattern=[[-1, P]], channel_multiplier=1))
        w()
        d(g.memset(half_ones[0:64, 0:64], 1.0))
        w()
        d(g.memset(half_ones[64:128, 64:128], 1.0))
        w()
        d(g.affine_select(out=gla_mask[:], in_=gla_mask[:], compare_op=ALU.is_ge, fill=0.0, base=0,
                          pattern=[[1, P]], channel_multiplier=-1))
        w()
        g.affine_select(out=gla_mask[:, 64:128], in_=gla_mask[:, 64:128], compare_op=ALU.is_ge, fill=0.0,
                        base=-64, pattern=[[0, 64]], channel_multiplier=1).then_inc(s("const_ready"), 1)
        d(g.iota(R0[:], [[1, T]], base=QB - T, channel_multiplier=-1, allow_small_or_imprecise_dtypes=True))
        w()
        d(g.affine_select(out=R0[:], in_=R0[:], compare_op=ALU.is_ge, fill=-1e30, base=T - QB,
                          pattern=[[-1, T]], channel_multiplier=1))
        w()
        pool.dma_start(R_dram, R0[:]).then_inc(s("R_stored"), 16)
        pool.wait_ge(s("R_stored"), 16)

        def split(n, extra_hi, slot):
            g.tensor_copy(w_hi[:, slot], w_raw[:, slot]).then_inc(w_hi_done, 1)
            pool.wait_ge(w_hi_done, extra_hi)
            g.tensor_tensor(w_lo[:, slot], w_raw[:, slot], w_hi[:, slot].bitcast(F32), ALU.subtract).then_inc(w_split, 1)

        for u in range(2):
            pool.wait_ge(w_loaded[u], 16)
            split(u, u + 1, u)
        with pool.Fori(0, (total_units[0] - 2) // 2) as i:
            for q in range(2):
                pool.wait_ge(w_loaded[q], i * 16 + 32)
                pool.wait_ge(w_started, i * 2 + (q + 2))
                settle(pool)
                split(None, i * 2 + (q + 3), q)

    @block.tensor
    def _(pe):
        units, tiles = Count(), Count()
        mm, tr = nc.tensor.matmul, nc.tensor.transpose
        s5_col = lambda q: HALF * (q % 2) + P * (q // 2)

        def col_sums(lhs, src, dst, ready, name):
            pe.wait_ge(s(ready[0]), ready[1])
            for hf in range(2):
                ins = mm(dst[:, hf * HALF:(hf + 1) * HALF], lhs[:], src[:, hf * HALF:(hf + 1) * HALF],
                         start=True, stop=True)
            ins.then_inc(s(name), 1)

        def norm_sums(tag):
            for k in range(KD):
                pe.wait_ge(s(f"sq_ready{tag}"), k + 1)
                for hf in range(2):
                    ins = mm(pY[:, hf * HALF:(hf + 1) * HALF], ones[:], n_tmp[:, k % 2, hf * HALF:(hf + 1) * HALF],
                             start=(k == 0), stop=(k == KD - 1))
                ins.then_inc(s(f"sq_summed{tag}"), 1)

        pe.wait_ge(s("const_ready"), 1)
        pe.wait_ge(s("rows_in"), 16 * N_ROWS)
        tr(pA[:, 0:V_ROWS], rows_a[0:V_ROWS, :], ident[0:V_ROWS, 0:V_ROWS])
        tr(pA[:, 128:256], rows_b[:], ident[:])
        tr(pA[:, 256:304], rows_c[0:48, :], ident[0:48, 0:48])
        tr(pA[:, 320:336], rows_s[:, 0, :], ident[0:PAIRS, 0:PAIRS])
        tr(pA[:, 336:352], rows_s[:, 1, :], ident[0:PAIRS, 0:PAIRS])
        pe.wait_ge(s("dt_rows"), 1)
        tr(pA[:, 352:368], rows_s[:, 2, :], ident[0:PAIRS, 0:PAIRS])
        mm(pA[:, 368:370], ones[0:DD, :], lam_pr[:], start=True, stop=True).then_inc(s("rows_T"), 1)
        for q in range(4):
            pe.wait_ge(s(f"x_in{q}"), 16)
        for k in range(KD):
            if k >= 2:
                pe.wait_ge(s("xT_copied"), k - 1)
            for tt in range(NQB):
                ins = tr([pX, pY][k % 2][:, tt * P:(tt + 1) * P], x_tok[:, tt, k * P:(k + 1) * P], ident[:])
            ins.then_inc(s("xT_full"), 1)
        pe.wait_ge(s("xT_copied"), KD)
        norm_sums(1)
        pe.wait_ge(s("cols_ready"), 1)

        def ada_cols(n, dst):
            pe.wait_ge(s("ada_mult"), n + 1)
            for c in range(4):
                ins = mm(dst[:, 4 * n + c:4 * n + c + 1], ada_sums[n // 4 > 0][:, n % 2, c * P:(c + 1) * P],
                         ones[:, 0:1], start=True, stop=True)
            ins.then_inc(s("ada_used"), 1)

        for n in range(4):
            ada_cols(n, pA)

        pe.wait_ge(s("mod_ready"), 1)
        for t in range(S5T):
            gemm_h(pe, units, tiles, s("h_ready1") if t == 0 else None)
        pe.wait_ge(s("s5_c_in"), 16 * 8)
        for r in range(2):
            for t in range(2):
                ins = tr(pX[:, (2 * r + t) * P:(2 * r + t + 1) * P], c_rows[:, r, t, :], ident[:])
        ins.then_inc(s("C_T"), 1)
        for g in range(2):
            gemm_h(pe, units, tiles)
        for r in range(2):
            pe.wait_ge(s("Ppre_ready"), 1)
            pe.wait_ge(s("C_copied"), 1)
            if r:
                pe.wait_ge(s("PT_copied"), 2)
            for pr in range(PAIRS):
                ins = tr([pX, pY][pr // 8][:, (pr % 8) * P:(pr % 8 + 1) * P], s_Ppre[r][:, pr, :], ident[:])
                if pr % 8 == 7:
                    ins.then_inc(s("PT_full"), 1)
        pe.wait_ge(s("G_ready"), 1)
        for rnd in range(4):
            pe.wait_ge(s("PT_copied"), 4)
            if rnd >= 2:
                pe.wait_ge(s("K_copied"), rnd - 1)
            for q in range(8):
                gr = rnd * 8 + q
                pr, gp = gr // 2, gr % 2
                for r in range(2):
                    ins = mm([pX, pY][rnd % 2][0:S5H, s5_col(q):s5_col(q) + P], s_Bb[r][64 * gp:64 * gp + 64, pr, :],
                             s_G[r][64 * gp:64 * gp + 64, pr, 0:8, :].rearrange("p a b -> p (a b)"),
                             start=(r == 0), stop=(r == 1))
            ins.then_inc(s("K_full"), 1)
        pe.wait_ge(s("U_in"), 16 * LC)
        pe.wait_ge(s("K_copied"), 4)
        for r in range(2):
            for half in range(2):
                if r:
                    pe.wait_ge(s("V_copied"), half + 1)
                for pr in range(8 * half, 8 * half + 8):
                    for gp in range(2):
                        ins = mm([pX, pY][half][64 * gp:64 * gp + 64, (pr % 8) * P:(pr % 8 + 1) * P],
                                 s_PT[r][:, pr, 64 * gp:64 * gp + 64], s_U[:, 2 * pr + gp, :], start=True, stop=True)
                ins.then_inc(s("V_full"), 1)
        for g in range(2, 6):
            gemm_h(pe, units, tiles)
        pe.wait_ge(s("X_ready"), 1)
        pe.wait_ge(s("Toep_in"), 16 * LC)
        pe.wait_ge(s("V_copied"), 4)
        for rnd in range(4):
            if rnd >= 2:
                pe.wait_ge(s("Y_copied"), rnd - 1)
            for q in range(8):
                gr = rnd * 8 + q
                pr, gp = gr // 2, gr % 2
                dst = [pX, pY][rnd % 2][:, s5_col(q):s5_col(q) + P]
                mm(dst, s_Toep[:, gr, :], s_U[:, gr, :], start=True, stop=False)
                for r in range(2):
                    ins = mm([pX, pY][rnd % 2][:, s5_col(q) + 1:s5_col(q) + P],
                             s_G[r][64 * gp:64 * gp + 64, pr, 1:9, :].rearrange("p a b -> p (a b)"),
                             s_V[r][64 * gp:64 * gp + 64, pr, 0:NC8 - 1], start=False, stop=(r == 1))
            ins.then_inc(s("Y_full"), 1)
        for g in range(6, KD):
            gemm_h(pe, units, tiles)
        pe.wait_ge(s("gelu_split"), S5T)
        for t in range(4):
            gemm(pe, units, tiles, t % 2 == 0, [(k, 2 * k + t % 2) for k in range(4)], o_hi, o_lo)

        def merge(ready, count):
            pe.wait_ge(s(ready), count)
            with pe.Fori(0, 2) as i:
                units.loop(i, 2)
                tiles.loop(i, 4)
                for j in range(4):
                    gemm(pe, units, tiles, j % 2 == 0, [(k, 2 * k + j % 2) for k in range(4)], o_hi, o_lo)
            units.end(2)
            tiles.end(2)

        if last_stage >= 2:
            pe.wait_ge(s("s5_split"), S5T)
            for j in range(KD):
                gemm(pe, units, tiles, j % 2 == 0, [(k, 2 * k + j % 2) for k in range(4)], o_hi, o_lo)
                if j:
                    ada_cols(3 + j, pX)
            ada_cols(3 + KD, pX)

        if last_stage >= 3:
            gemm_h(pe, units, tiles)
            gemm(pe, units, tiles, True, [(0, 0)], h_hi, h_lo)
            pe.wait_ge(acc_free[0], tiles.half(tiles.n - 2))
            with pe.Fori(0, GLA_PAIRS) as i:
                units.loop(i, 10)
                tiles.loop(i, 10)
                pe.wait_ge(s("gkw_ready"), i + 1)
                for hf in range(2):
                    ins = mm(pX[:, hf * HALF:(hf + 1) * HALF], gkw_cur[:], g_lr[:, hf * HALF:(hf + 1) * HALF],
                             start=True, stop=True)
                ins.then_inc(s("z_full"), 1)
                gemm_h(pe, units, tiles)
                gemm_h(pe, units, tiles)
                gemm_h(pe, units, tiles)
                t_v = tiles.n - 1
                pe.wait_ge(s("kl_ready"), i + 1)
                for tb in range(8):
                    ins = tr(pX[:, tb * P:(tb + 1) * P], g_kl[:, tb * P:(tb + 1) * P], ident[:])
                ins.then_inc(s("klT_full"), 1)
                for hd in range(2):
                    if hd == 0:
                        gemm_h(pe, units, tiles)
                    else:
                        gemm_h(pe, units, tiles)
                    pe.wait_ge(acc_free[(t_v + hd) % 2], tiles.half(t_v + hd))
                    if hd:
                        pe.wait_ge(s("v_copied"), i * 2 + 1)
                    for tb in range(8):
                        ins = tr(pY[:, tb * P:(tb + 1) * P], g_vT[:, tb * P:(tb + 1) * P], ident[:])
                    ins.then_inc(s("v_full"), 1)
                pe.wait_ge(s("klT_copied"), i + 1)
                pe.wait_ge(s("v_copied"), i * 2 + 2)
                settle(pe)
                for n in range(NCH - 1):
                    tb, hb = n // 2, 64 * (n % 2)
                    for hd in range(2):
                        ins = mm([pX, pY][n // 8][64 * hd:64 * hd + 64, ds_col(n):ds_col(n) + P],
                                 g_klT[hb:hb + 64, tb, 64 * hd:64 * hd + 64], g_v[hb:hb + 64, hd, tb, :],
                                 start=True, stop=True)
                    if n % 8 == 7 or n == NCH - 2:
                        ins.then_inc(s("ds_full"), 1)
                gemm_h(pe, units, tiles)
                pe.wait_ge(s("S0_ready"), i + 1)
                for hd in range(2):
                    r0 = 64 * hd
                    if hd:
                        pe.wait_ge(s("g_rstd_ready"), i * 2 + 1)
                    for tb in range(8):
                        ins = mm(pX[:, tb * P:(tb + 1) * P], g_kinv[r0:r0 + 64, tb * P:(tb + 1) * P],
                                 g_qd[r0:r0 + 64, tb * P:(tb + 1) * P], start=True, stop=True)
                    ins.then_inc(s("attn_full"), 1)
                    gemm_h(pe, units, tiles)
                    pe.wait_ge(s("attn_ready"), i * 2 + (hd + 1))
                    if hd:
                        pe.wait_ge(s("g_o_read"), i * 2 + 1)
                    for tb in range(8):
                        mm(pY[:, tb * P:(tb + 1) * P], g_v[:, hd, tb, :], g_attn[:, tb, :], start=True, stop=False)
                        for c in range(2):
                            t0 = tb * P + 64 * c
                            ins = mm(pY[:, t0:t0 + 64], g_S0[r0:r0 + 64, 2 * tb + c, :], g_qd[r0:r0 + 64, t0:t0 + 64],
                                     start=False, stop=(c == 1))
                    ins.then_inc(s("g_o_full"), 1)
                    col_sums(ones, g_sq, pX, ("g_sq_ready", i * 2 + (hd + 1)), "g_ss_full")
                    gemm_h(pe, units, tiles)
            units.end(GLA_PAIRS)
            tiles.end(GLA_PAIRS)
            merge("gla_split", GLA_HEADS)

        if last_stage >= 4:
            with pe.Fori(0, DH // 2) as i:
                units.loop(i, 10)
                tiles.loop(i, 42)
                for hh in range(2):
                    for qk in range(2):
                        gemm_h(pe, units, tiles)
                        t_k = tiles.n - 1
                        pe.wait_ge(s("d_sq_ready"), i * 4 + (2 * hh + qk + 1))
                        if hh or qk:
                            pe.wait_ge(s("d_rstd_ready"), i * 4 + (2 * hh + qk))
                        for hf in range(2):
                            ins = mm(pX[:, hf * HALF:(hf + 1) * HALF], half_ones[:], d_tmp[:, 0, hf * HALF:(hf + 1) * HALF],
                                     start=True, stop=True)
                        ins.then_inc(s("d_ss_full"), 1)
                    gemm_h(pe, units, tiles)
                    t_v = tiles.n - 1
                    pe.wait_ge(acc_free[t_v % 2], tiles.half(t_v))
                    for tb in range(8):
                        ins = tr(pY[:, tb * P:(tb + 1) * P], d_vT[:, tb * P:(tb + 1) * P], ident[:])
                    ins.then_inc(s("d_v_full"), 1)
                    pe.wait_ge(acc_free[t_k % 2], tiles.half(t_k))

                    def scores(qb):
                        kw = (qb + 1) * QB
                        for j in range(2):
                            t = tiles.next()
                            pe.wait_ge(acc_free[t % 2], tiles.half(t) - 1)
                            for c0 in range(0, kw, HALF):
                                c1 = min(kw, c0 + HALF)
                                ins = mm(acc[t % 2][:, c0:c1], d_q[64 * j:64 * j + 64, qb * QB:(qb + 1) * QB],
                                         d_k[64 * j:64 * j + 64, c0:c1], start=True, stop=True)
                            ins.then_inc(acc_full[t % 2], 1)

                    def weights_T(qb):
                        pe.wait_ge(s("d_w_ready"), i * 16 + (8 * hh + qb + 1))
                        if hh == 0 and qb == 0:
                            pe.wait_ge(s("d_rstd_ready"), i * 4 + 2)
                        elif qb == 0:
                            pe.wait_ge(s("d_rstd_ready"), i * 4 + 4)
                        else:
                            pe.wait_ge(s("d_wT_copied"), i * 16 + (8 * hh + qb))
                        for kb in range(qb + 1):
                            ins = tr(pX[:, kb * P:(kb + 1) * P], d_s[:, qb % 2, 0, kb * P:(kb + 1) * P], ident[:])
                        ins.then_inc(s("d_wT_full"), 1)

                    def values(grp):
                        pe.wait_ge(s("d_wT_copied"), i * 16 + (8 * hh + 4 * grp + 4))
                        if grp:
                            pe.wait_ge(s("d_o_read"), i * 4 + (2 * hh + 1))
                        else:
                            pe.wait_ge(s("d_v_copied"), i * 2 + (hh + 1))
                        nkb = 4 * grp + 4
                        for kb in range(nkb):
                            c0 = max(0, kb - 4 * grp) * P
                            ins = mm(pY[:, c0:HALF], d_v[:, kb, :], d_wT[:, kb, c0:HALF], start=(kb == 0), stop=(kb == nkb - 1))
                        ins.then_inc(s("d_o_full"), 1)
                        pe.wait_ge(s("d_osq_ready"), i * 4 + (2 * hh + grp + 1))
                        mm(pY[:, HALF:T], ones[:], o_sq[:], start=True, stop=True).then_inc(s("d_oss_full"), 1)

                    scores(0)
                    for qb in range(NQB):
                        if qb + 1 < NQB:
                            scores(qb + 1)
                        if qb in GATE_AT:
                            gemm_h(pe, units, tiles)
                        weights_T(qb)
                        if qb % 4 == 3:
                            values(qb // 4)
            units.end(DH // 2)
            tiles.end(DH // 2)
            merge("diff_split", 2 * DH)

        if last_stage >= 5:
            pe.wait_ge(s("merged_split"), 1)
            with pe.Fori(0, 4) as i:
                units.loop(i, 2)
                tiles.loop(i, 2)
                for j in range(2):
                    gemm_h(pe, units, tiles)
            units.end(4)
            tiles.end(4)
            norm_sums(2)

        if last_stage >= 6:
            pe.wait_ge(s("h_ready2"), KD)

            def down(q, g):
                pe.wait_ge(s("act_split"), g * 2 + 2)
                for n in range(2):
                    for m in range(4):
                        gemm_down(pe, units, tiles, m, q)

            def gemm_down(pe, units, tiles, m, q):
                gemm(pe, units, tiles, m == 0, [(2 * q + k, 4 * k + m) for k in range(2)], o_hi, o_lo)

            for t in range(4):
                gemm_h(pe, units, tiles)
            with pe.Fori(0, (FG - 1) // 2) as i:
                units.loop(i, 12)
                tiles.loop(i, 24)
                for q in range(2):
                    for t in range(4):
                        gemm_h(pe, units, tiles)
                    down(q, i * 2 + q)
            units.end((FG - 1) // 2)
            tiles.end((FG - 1) // 2)
            down(0, FG - 1)

        if last_stage >= 7:
            for q in range(2):
                pe.wait_ge(acc_free[q], tiles.half(tiles.n - 2))
            for tt in range(NQB):
                if tt >= 2:
                    pe.wait_ge(s("out_ready"), tt - 1)
                for k in range(KD):
                    ins = tr([pX, pY][tt % 2][:, k * P:(k + 1) * P], M[:, k, tt * P:(tt + 1) * P], ident[:])
                ins.then_inc(s("out_full"), 1)

    @block.scalar
    def _(act):
        units, tiles = Count(), Count()
        act_ = nc.scalar.activation
        chain = Chain(act, act_chain)
        d, w = chain.did, chain.wait

        def full(t):
            act.wait_ge(acc_full[t % 2], tiles.half(t))

        def rows(v, n):
            return a[v][0].rearrange("(m p) -> m p", m=n)

        def row_in(dst, src):
            act.dma_start(dst, src).then_inc(s("rows_in"), 16)

        row_in(rows_a[V_ADAB:V_N1, :], rows("ada_b", 48))
        row_in(rows_a[V_N1:V_N2, :], rows("norm1_g", 8))
        row_in(rows_a[V_N2:V_C, :], rows("norm2_g", 8))
        row_in(rows_a[V_C:V_GKB, :], rows("c", 8))
        row_in(rows_a[V_GKB:V_S5D, :], rows("gla_gk_b", 2))
        row_in(rows_a[V_S5D:V_GLUB, :], rows("s5_d", 4))
        row_in(rows_a[V_GLUB:V_GLAG, :], rows("s5_glu_b", 4))
        row_in(rows_a[V_GLAG:V_SUBG, :], rows("gla_norm_g", 1))
        row_in(rows_a[V_SUBG:V_QG, :], rows("diff_subln_g", 1))
        for j in range(2):
            row_in(rows_a[V_QG:V_KG, DD * j:DD * j + DD], rows("diff_q_norm_g", 1))
            row_in(rows_a[V_KG:V_ROWS, DD * j:DD * j + DD], rows("diff_k_norm_g", 1))
        cw = a["ffn_conv_w"][0].rearrange("w (m p) -> (w m) p", p=P)
        row_in(rows_b[:], cw[0:P])
        row_in(rows_c[0:4, :], cw[P:3 * NT_FF])
        row_in(rows_c[4:48, :], rows("ffn_conv_b", NT_FF))
        for r, nm in enumerate(("s5_lambda_re", "s5_lambda_im")):
            row_in(rows_s[:, r, :], a[nm][0].rearrange("(r g) p -> r (g p)", g=2))
        row_in(dt_row[:], a["s5_log_dt"][0].rearrange("(r g) -> r g", g=2))
        row_in(gkw[:], a["gla_gk_w"][0])
        for q, nm in enumerate(("diff_lambda_q1", "diff_lambda_k1", "diff_lambda_q2", "diff_lambda_k2")):
            row_in(lam_in[:, q:q + 1], a[nm][0].rearrange("(p o) -> p o", o=1))

        act.wait_ge(s("rows_T"), 1)
        act_(cols[:, 0:V_ROWS], pA[:, 0:V_ROWS], ACT.Copy)
        act_(cols[:, V_CONV:V_CONV + P], pA[:, 128:256], ACT.Copy)
        act_(cols[:, V_CONV + P:V_END], pA[:, 256:304], ACT.Copy)
        act_(l_re[:], pA[:, 320:336], ACT.Copy)
        act_(l_im[:], pA[:, 336:352], ACT.Copy)
        act_(l_dt[:], pA[:, 352:368], ACT.Copy)
        act_(lam_e[:], pA[:, 368:370], ACT.Exp).then_inc(s("cols_ready"), 1)
        act.wait_ge(s("cols_ready"), 1)
        act_(c_act[:], cols[:, V_C:V_C + KD], ACT.Silu).then_inc(s("c_ready"), 1)

        for k in range(KD):
            act.wait_ge(s("xT_full"), k + 1)
            act_(xT0[:, k, :], [pX, pY][k % 2][:], ACT.Copy).then_inc(s("xT_copied"), 1)

        def norm_squares(tag, X, ready):
            for k in range(KD):
                if ready is not None:
                    ready(k)
                if k >= 2:
                    act.wait_ge(s(f"sq_summed{tag}"), k - 1)
                act_(n_tmp[:, k % 2, :], X[:, k, :], ACT.Square).then_inc(s(f"sq_ready{tag}"), 1)

        def norm_rstd(tag):
            act.wait_ge(s(f"sq_summed{tag}"), KD)
            d(act_(n_rstd[:], pY[:], ACT.Ln, scale=1.0 / D, bias=eps_col[:]))
            w()
            act_(n_rstd[:], n_rstd[:], ACT.Exp, scale=-0.5).then_inc(s(f"nrm_rstd{tag}"), 1)

        def norm_hi(tag, k):
            act.wait_ge(s(f"nrm_t{tag}"), k + 1)
            act_(h_hi[:, k, :], n_tmp[:, k % 2, :], ACT.Copy).then_inc(s(f"nrm_hi{tag}"), 1)

        norm_squares(1, xT0, lambda k: act.wait_ge(s("xT_copied"), k + 1))
        norm_rstd(1)

        act.wait_ge(s("angle_ready"), 1)
        act_(sn[:], th[:], ACT.Sin)
        act_(sh[:], th[:], ACT.Sin, scale=0.5).then_inc(s("sines"), 1)
        act.wait_ge(s("R_stored"), 16)
        for k in range(KD):
            norm_hi(1, k)
        for t in range(S5T):
            n = tiles.next()
            full(n)
            act_(s_uP[:, t], acc[n % 2].rearrange("p (c j) -> p j c", j=LC), ACT.Copy).then_inc(acc_free[n % 2], 1)
        act.wait_ge(s("C_T"), 1)
        act_(s_C[0].rearrange("p a b -> p (a b)"), pX[:, 0:256], ACT.Copy)
        act_(s_C[1].rearrange("p a b -> p (a b)"), pX[:, 256:512], ACT.Copy).then_inc(s("C_copied"), 1)
        for n in range(4):
            act.wait_ge(s("PT_full"), n + 1)
            act_(s_PT[n // 2][:, 8 * (n % 2):8 * (n % 2) + 8, :].rearrange("p a b -> p (a b)"), [pX, pY][n % 2][:],
                 ACT.Copy).then_inc(s("PT_copied"), 1)
        for n in range(4):
            act.wait_ge(s("K_full"), n + 1)
            act_(s_K[:, 8 * n:8 * n + 8, :].rearrange("p (r g) b -> p g r b", g=2),
                 [pX, pY][n % 2][0:S5H, :].rearrange("p (g r b) -> p g r b", g=2, b=P),
                 ACT.Copy).then_inc(s("K_copied"), 1)

        def gate(g):
            n = tiles.next()
            full(n)
            act_(M[:, g, :], acc[n % 2][:], ACT.Sigmoid).then_inc(acc_free[n % 2], 1)

        act.wait_ge(s("Toep_in"), 16 * LC)
        for n in range(4):
            act.wait_ge(s("V_full"), n + 1)
            act_(s_V[n // 2][:, 8 * (n % 2):8 * (n % 2) + 8, :].rearrange("p a b -> p (a b)"), [pX, pY][n % 2][:],
                 ACT.Copy).then_inc(s("V_copied"), 1)
        for g in range(4):
            gate(g)
        for n in range(4):
            act.wait_ge(s("Y_full"), n + 1)
            act_(s_Y[:, 8 * n:8 * n + 8, :].rearrange("p (r g) b -> p g r b", g=2),
                 [pX, pY][n % 2][:].rearrange("p (g r b) -> p g r b", g=2, b=P),
                 ACT.Copy).then_inc(s("Y_copied"), 1)
        for g in range(4, KD):
            gate(g)
        for t in range(S5T):
            act.wait_ge(s("yd_ready"), t + 1)
            d(act_(s_Yp[:, t, :], s_Yp[:, t, :], ACT.Gelu_apprx_tanh))
            w()
            act_(o_hi[:, t, :], s_Yp[:, t, :], ACT.Copy).then_inc(s("gelu_hi"), 1)
        for t in range(S5T):
            n = tiles.next()
            full(n)
            if t:
                act.wait_ge(s("glu_out"), t)
            act_(s_sig[:], acc[n % 2][:], ACT.Sigmoid, bias=cols[:, V_GLUB + t:V_GLUB + t + 1]).then_inc(acc_free[n % 2], 1)
        for t in range(S5T):
            act.wait_ge(s("glu_out"), S5T)
            act_(o_hi[:, t, :].rearrange("p (c j) -> p j c", j=LC), s_Yp[:, t, :].rearrange("p (j c) -> p j c", j=LC),
                 ACT.Copy).then_inc(s("s5_hi"), 1)

        def merged_out(adds):
            if adds:
                act.wait_ge(s("merged_add"), adds)
            else:
                for q in range(2):
                    act.wait_ge(acc_free[q], tiles.half(tiles.n - 2 + q))
            act.dma_start(m_dram.rearrange("(k p) t -> p k t", p=P), M[:]).then_inc(s("M_out"), 16)

        def merge(split, count):
            act.wait_ge(s(split), count)
            for q in range(4):
                act.dma_start(m_prev[:, 2 * q:2 * q + 2, :], m_dram.rearrange("(k p) t -> p k t", p=P)[:, 2 * q:2 * q + 2, :]
                              ).then_inc(s(f"M_in{q}"), 16)
            tiles.n += KD

        def gate_reg(tile):
            n = tiles.next()
            full(n)
            act_(M[:, bass.ds(tile, 1), :].rearrange("p a b -> p (a b)"), acc[n % 2][:], ACT.Sigmoid
                 ).then_inc(acc_free[n % 2], 1)

        tiles.n += KD
        if last_stage >= 2:
            act.wait_ge(s("s5_split"), S5T)
            for n in range(4, 12):
                act.wait_ge(s("ada_mult"), max(4, n - 1))
                act.dma_start(ada_rings[1][:, n % 2], ada_v[:, :, n * HALF:(n + 1) * HALF]).then_inc(s(f"ada_in{n % 2}"), 16)
        if last_stage >= 3:
            merged_out(0)

        if last_stage >= 3:
            n = tiles.next()
            full(n)
            act_(g_lr[:], acc[n % 2][0:GLA_LR, :], ACT.Copy).then_inc(acc_free[n % 2], 1)
            n = tiles.next()
            full(n)
            act_(junk[:], acc[n % 2][:, 0:2], ACT.Copy).then_inc(acc_free[n % 2], 1)
            act.wait_ge(s("M_out"), 16)
            with act.Fori(0, GLA_PAIRS) as i:
                tiles.loop(i, 10)
                chain.loop(i, 4)
                act.wait_ge(s("g_z"), i + 1)
                d(act_(g_eb[:], g_kinv[:], ACT.Abs))
                w()
                d(act_(g_eb[:], g_eb[:], ACT.Exp, scale=-1.0))
                w()
                act_(g_eb[:], g_eb[:], ACT.Ln, bias=one_col[:]).then_inc(s("g_ln"), 1)
                act.wait_ge(s("g_S_ready"), i + 1)
                act_(g_eb[:], g_S[:], ACT.Exp, scale=1.0 / 16)
                act_(g_kinv[:], g_S[:], ACT.Exp, scale=-1.0 / 16).then_inc(s("g_exps"), 1)
                act.wait_ge(s("g_kx_ready"), i + 1)
                act_(g_kl[:], g_kl[:], ACT.Exp, scale=1.0 / 16).then_inc(s("g_klx"), 1)
                tiles.n += 2
                n = tiles.next()
                full(n)
                act_(g_vT[:], acc[n % 2][:], ACT.Copy).then_inc(acc_free[n % 2], 1)
                act.wait_ge(s("klT_full"), i + 1)
                act_(g_klT.rearrange("p a b -> p (a b)"), pX[:], ACT.Copy).then_inc(s("klT_copied"), 1)
                act.wait_ge(s("v_full"), i * 2 + 1)
                act_(g_v[:, 0].rearrange("p a b -> p (a b)"), pY[:], ACT.Copy).then_inc(s("v_copied"), 1)
                n = tiles.next()
                full(n)
                act_(g_vT[:], acc[n % 2][:], ACT.Copy).then_inc(acc_free[n % 2], 1)
                n = tiles.next()
                full(n)
                act_(g_sil[:], acc[n % 2][:], ACT.Silu).then_inc(acc_free[n % 2], 1)
                act.wait_ge(s("v_full"), i * 2 + 2)
                act_(g_v[:, 1].rearrange("p a b -> p (a b)"), pY[:], ACT.Copy).then_inc(s("v_copied"), 1)
                gate_reg(i * 4)
                for hd in range(2):
                    if hd == 0:
                        gate_reg(i * 4 + 1)
                    else:
                        n = tiles.next()
                        full(n)
                        act_(g_sil[:], acc[n % 2][:], ACT.Silu).then_inc(acc_free[n % 2], 1)
                        act.wait_ge(s("gla_split"), i * 2 + 1)
                    act.wait_ge(s("g_o_full"), i * 2 + (hd + 1))
                    act_(g_sq[:], pY[:], ACT.Square).then_inc(s("g_sq_ready"), 1)
                    act.wait_ge(s("g_ss_full"), i * 2 + (hd + 1))
                    d(act_(g_rstd[:], pX[:], ACT.Ln, scale=1.0 / GLA_DV, bias=eps_col[:]))
                    w()
                    act_(g_rstd[:], g_rstd[:], ACT.Exp, scale=-0.5).then_inc(s("g_rstd_ready"), 1)
                    act.wait_ge(s("g_y_ready"), i * 2 + (hd + 1))
                    act_(o_hi[:, bass.ds(i * 2 + hd, 1), :].rearrange("p a b -> p (a b)"), g_sq[:], ACT.Copy).then_inc(s("g_hi"), 1)
                    gate_reg(i * 4 + (2 + hd))
            tiles.end(GLA_PAIRS)
            chain.end(GLA_PAIRS)
            merge("gla_split", GLA_HEADS)
            merged_out(KD)

        if last_stage >= 4:
            act.wait_ge(s("M_out"), 32)
            with act.Fori(0, DH // 2) as i:
                tiles.loop(i, 42)
                chain.loop(i, 4)
                for hh in range(2):
                    for qk in range(2):
                        n = tiles.next()
                        full(n)
                        if qk:
                            act.wait_ge(s("d_ss_full"), i * 4 + (2 * hh + 1))
                        act_(d_tmp[:, 0, :], acc[n % 2][:], ACT.Square).then_inc(s("d_sq_ready"), 1)
                        act.wait_ge(s("d_ss_full"), i * 4 + (2 * hh + qk + 1))
                        if qk:
                            act.wait_ge(acc_free[(n - 1) % 2], tiles.half(n - 1))
                        act_(d_rs[:], pX[:], ACT.Sqrt, scale=1.0 / DD, bias=eps_col[:]).then_inc(s("d_rstd_ready"), 1)
                    n = tiles.next()
                    full(n)
                    act_(d_vT[:], acc[n % 2][:], ACT.Copy).then_inc(acc_free[n % 2], 1)
                    act.wait_ge(s("d_v_full"), i * 2 + (hh + 1))
                    act_(d_v.rearrange("p a b -> p (a b)"), pY[:], ACT.Copy).then_inc(s("d_v_copied"), 1)

                    def exps(qb):
                        tiles.n += 2
                        kw = (qb + 1) * QB
                        act.wait_ge(s("d_mx_ready"), i * 16 + (8 * hh + qb + 1))
                        for j in range(2):
                            ins = act_(d_s[:, qb % 2, j, 0:kw], d_s[:, qb % 2, j, 0:kw], ACT.Exp,
                                       bias=nmx[:, qb % 2, j:j + 1], accum_out=rsum[:, qb % 2, j:j + 1])
                        ins.then_inc(s("d_p_ready"), 1)

                    exps(0)
                    for qb in range(NQB):
                        if qb + 1 < NQB:
                            exps(qb + 1)
                        if qb in GATE_AT:
                            gate_reg(i * 4 + (2 * hh + GATE_AT.index(qb)))
                        act.wait_ge(s("d_wT_full"), i * 16 + (8 * hh + qb + 1))
                        act_(d_wT[:, 0:qb + 1, (qb % 4) * QB:(qb % 4 + 1) * QB],
                             pX[:, 0:(qb + 1) * QB].rearrange("p (a b) -> p a b", b=QB), ACT.Copy).then_inc(s("d_wT_copied"), 1)
                        if qb % 4 == 3:
                            grp = qb // 4
                            no = i * 4 + (2 * hh + grp + 1)
                            act.wait_ge(s("d_o_full"), no)
                            act_(o_sq[:], pY[:, 0:HALF], ACT.Square).then_inc(s("d_osq_ready"), 1)
                            act.wait_ge(s("d_oss_full"), no)
                            d(act_(o_sq[:], pY[:, HALF:T], ACT.Ln, scale=1.0 / (2 * DD), bias=eps_col[:]))
                            w()
                            act_(o_sq[:], o_sq[:], ACT.Exp, scale=-0.5).then_inc(s("d_orstd"), 1)
                            act.wait_ge(s("d_o_read"), no)
                            act_(o_hi[:, bass.ds(i * 2 + hh, 1), grp * HALF:(grp + 1) * HALF].rearrange("p a b -> p (a b)"),
                                 o_sq[:], ACT.Copy).then_inc(s("d_hi"), 1)
            tiles.end(DH // 2)
            chain.end(DH // 2)
            merge("diff_split", 2 * DH)

        if last_stage >= 5:
            for k in range(KD):
                act.wait_ge(s("merged_add"), 2 * KD)
                act_(h_hi[:, k, :], M[:, k, :], ACT.Copy).then_inc(s("merged_hi"), 1)
            act.wait_ge(s("merged_split"), 1)
            act.dma_start(M[:], xT_dram.rearrange("(k p) t -> p k t", p=P)).then_inc(s("xT_in"), 16)
            first = tiles.n
            tiles.n += 8
            norm_squares(2, M, lambda k: act.wait_ge(acc_free[(first + k) % 2], tiles.half(first + k)))
            norm_rstd(2)
            for k in range(KD):
                norm_hi(2, k)

        if last_stage >= 6:
            def up(g, par, start):
                for c in range(2):
                    for ag in range(2):
                        n = tiles.next()
                        full(n)
                        buf = [f_a, f_g][ag]
                        if ag == 0 and not start:
                            act.wait_ge(s("act_split"), (g - 1) * 2 + (c + 1))
                        ch = V_CONV + 2 * NT_FF + 22 * ag + g * 2 + c
                        chb = V_CONVB + 22 * ag + g * 2 + c
                        act_(buf[:, c, :], acc[n % 2][:], ACT.Identity, scale=cols[:, bass.ds(ch, 1)],
                             bias=cols[:, bass.ds(chb, 1)]).then_inc(s("f_lin"), 1)
                        if ag == 0:
                            act.wait_ge(acc_free[n % 2], tiles.half(n))
                            act_(f_a[:, c, :], f_a[:, c, :], ACT.Silu).then_inc(s("f_silu"), 1)
                    act.wait_ge(s("f_prod"), g * 2 + (c + 1))
                    act_(o_hi[:, 2 * par + c, :], f_a[:, c, :], ACT.Copy).then_inc(s("f_hi"), 1)

            up(0, 0, True)
            with act.Fori(0, (FG - 1) // 2) as i:
                tiles.loop(i, 24)
                for q in range(2):
                    up(i * 2 + (q + 1), (q + 1) % 2, False)
                    tiles.n += 8
            tiles.end((FG - 1) // 2)
            tiles.n += 8

        if last_stage >= 7:
            for tt in range(NQB):
                act.wait_ge(s("out_full"), tt + 1)
                if tt >= 2:
                    act.wait_ge(s(f"out_stored{tt % 2}"), 16 * (tt // 2))
                act_(out_tok[:, tt % 2, :], [pX, pY][tt % 2][:], ACT.Copy).then_inc(s("out_ready"), 1)

    @block.vector
    def _(dve):
        v = nc.vector
        tiles = Count()
        chain = Chain(dve, dve_chain)
        d, w = chain.did, chain.wait
        TT, TS, STT = v.tensor_tensor, v.tensor_scalar, v.scalar_tensor_tensor
        MUL, ADD, SUB = ALU.mult, ALU.add, ALU.subtract

        def one(ins):
            d(ins)
            w()

        def full(t):
            dve.wait_ge(acc_full[t % 2], tiles.half(t))

        def freed(t):
            dve.wait_ge(acc_free[t % 2], tiles.half(t))

        dve.wait_ge(s("rows_in"), 16 * N_ROWS)
        d(TT(lam_pr[:, 0:1], lam_in[:, 0:1], lam_in[:, 1:2], MUL))
        d(TT(lam_pr[:, 1:2], lam_in[:, 2:3], lam_in[:, 3:4], MUL))
        v.tensor_copy(rows_s[:, 2, :].rearrange("p (g q) -> p g q", g=2),
                      dt_row[:].unsqueeze(2).to_broadcast([PAIRS, 2, S5P])).then_inc(s("dt_rows"), 1)
        dve.wait_ge(s("cols_ready"), 1)
        one(STT(neg_lam[:], lam_e[:, 1:2], LAMBDA_INIT, lam_e[:, 0:1], SUB, SUB))
        d(TS(subg[:], cols[:, V_SUBG:V_SUBG + 1], 1.0 - LAMBDA_INIT, None, MUL))
        d(TS(qg[:], cols[:, V_QG:V_QG + 1], DD ** -0.5, None, MUL))

        def norm_rest(tag, X, scale, shift):
            def lo(k):
                dve.wait_ge(s(f"nrm_hi{tag}"), k + 1)
                TT(h_lo[:, k, :], n_tmp[:, k % 2, :], h_hi[:, k, :].bitcast(F32), SUB).then_inc(s(f"h_ready{tag}"), 1)
            for k in range(KD):
                if k >= 2:
                    dve.wait_ge(s(f"h_ready{tag}"), k - 1)
                one(TT(n_tmp[:, k % 2, :], X[:, k, :], n_rstd[:], MUL))
                TS(n_tmp[:, k % 2, :], n_tmp[:, k % 2, :], scale[:, k:k + 1], mod[:, shift + k:shift + k + 1],
                   MUL, ADD).then_inc(s(f"nrm_t{tag}"), 1)
                if k:
                    lo(k - 1)
            lo(KD - 1)

        def expm1(out_m1, out_e, x):
            one(TS(e_x[:], x, -87.3, 88.7, ALU.max, ALU.min))
            one(TS(e_n[:], e_x[:], 1.0 / math.log(2.0), 12582912.0, MUL, ADD))
            one(TS(e_n[:], e_n[:], 12582912.0, None, SUB))
            one(STT(e_r[:], e_n[:], -0.693145751953125, e_x[:], MUL, ADD))
            one(STT(e_r[:], e_n[:], -1.4286068203094172e-06, e_r[:], MUL, ADD))
            one(TS(e_q[:], e_r[:], 1.0 / 8, 1.0, MUL, ADD))
            for k in range(7, 1, -1):
                one(STT(e_q[:], e_q[:], 1.0 / k, e_r[:], MUL, MUL))
                one(TS(e_q[:], e_q[:], 1.0, None, ADD))
            one(TT(e_q[:], e_q[:], e_r[:], MUL))
            one(TS(e_n[:], e_n[:], 127.0, 8388608.0, ADD, MUL))
            one(v.tensor_copy(e_int[:], e_n[:]))
            two_n = e_int[:].bitcast(F32)
            one(TT(e_q[:], e_q[:], two_n, MUL))
            one(TT(out_e, e_q[:], two_n, ADD))
            one(STT(out_m1, two_n, 1.0, e_q[:], SUB, ADD))

        def cmul(oi, ar, ai, br, bi, tmp):
            d(TT(tmp[0], ar, br, MUL))
            d(TT(tmp[1], ai, bi, MUL))
            d(TT(tmp[2], ar, bi, MUL))
            one(TT(tmp[3], ai, br, MUL))
            d(TT(oi[0], tmp[0], tmp[1], SUB))
            one(TT(oi[1], tmp[2], tmp[3], ADD))

        expm1(e_em[:], l_dt[:], l_dt[:])
        one(TT(th[:], l_im[:], l_dt[:], MUL))
        one(TS(sn[:], th[:], 1.0 / (2 * math.pi), 12582912.0, MUL, ADD))
        one(TS(sn[:], sn[:], 12582912.0, None, SUB))
        for c in (-6.28125, -0.0019340515136718750, -1.2556659146e-06):
            one(STT(th[:], sn[:], c, th[:], MUL, ADD))
        TS(th[:], th[:], -3.1415925, 3.1415925, ALU.max, ALU.min).then_inc(s("angle_ready"), 1)

        dve.wait_ge(s("c_ready"), 1)

        def ada_mult(n):
            ring, out = ada_rings[n >= 4][:, n % 2], ada_sums[n >= 4][:, n % 2, :]
            dve.wait_ge(s(f"ada_in{n % 2}"), 16 * (n // 2 + 1))
            if n % 4 >= 2 or n >= 8:
                dve.wait_ge(s("ada_used"), n - 1)
            one(TS(out, ring[:, 0, :], c_act[:, 0:1], None, MUL))
            for k in range(1, KD):
                ins = STT(out, ring[:, k, :], c_act[:, k:k + 1], out, MUL, ADD)
                if k < KD - 1:
                    one(ins)
            ins.then_inc(s("ada_mult"), 1)

        for n in range(4):
            ada_mult(n)
        dve.wait_ge(s("ada_used"), 4)
        one(TT(mod[:, 0:16], pA[:, 0:16], cols[:, V_ADAB:V_ADAB + 16], ADD))
        STT(scale1[:], mod[:, M_SC1:M_SC1 + 8], 1.0, cols[:, V_N1:V_N1 + 8], ADD, MUL).then_inc(s("mod_ready"), 1)
        dve.wait_ge(s("mod_ready"), 1)
        dve.wait_ge(s("nrm_rstd1"), 1)
        norm_rest(1, xT0, scale1, M_SH1)

        one(TT(cosv[:], l_re[:], l_dt[:], MUL))
        expm1(e_em[:], e_e[:], cosv[:])
        dve.wait_ge(s("sines"), 1)
        one(TT(cm[:], sh[:], sh[:], MUL))
        one(TS(cm[:], cm[:], -2.0, None, MUL))
        one(TS(cosv[:], cm[:], 1.0, None, ADD))
        one(TT(cr[:], e_e[:], cm[:], MUL))
        one(TT(cr[:], cr[:], e_em[:], ADD))
        one(TT(ci[:], e_e[:], sn[:], MUL))
        L = [Lp[0], Lp[1]]
        dve.wait_ge(s("xT_stored"), 16)
        d(v.memset(L[0][:, :, 0], 1.0))
        d(v.memset(L[1][:, :, 0], 0.0))
        d(TS(L[0][:, :, 1], cr[:], 1.0, None, ADD))
        one(v.tensor_copy(L[1][:, :, 1], ci[:]))

        def small_tmp(n):
            return [s_tt[:, q, 0:PAIRS * n].rearrange("p (a b) -> p a b", b=n) for q in range(4)]

        def wide(t, n):
            return t.to_broadcast([P, PAIRS, n])

        for n in (1, 2, 4):
            cmul([L[r][:, :, n + 1:2 * n + 1] for r in range(2)], L[0][:, :, 1:n + 1], L[1][:, :, 1:n + 1],
                 wide(L[0][:, :, n:n + 1], n), wide(L[1][:, :, n:n + 1], n), small_tmp(n))
        one(TT(inv[:], l_re[:], l_re[:], MUL))
        one(TT(wv_re[:], l_im[:], l_im[:], MUL))
        one(TT(inv[:], inv[:], wv_re[:], ADD))
        one(v.reciprocal(inv[:], inv[:]))
        d(TT(e_x[:], cr[:], l_re[:], MUL))
        d(TT(e_n[:], ci[:], l_im[:], MUL))
        d(TT(e_r[:], ci[:], l_re[:], MUL))
        one(TT(e_q[:], cr[:], l_im[:], MUL))
        d(TT(wv_re[:], e_x[:], e_n[:], ADD))
        one(TT(wv_im[:], e_r[:], e_q[:], SUB))
        d(TT(wv_re[:], wv_re[:], inv[:], MUL))
        one(TT(wv_im[:], wv_im[:], inv[:], MUL))
        dve.wait_ge(s("s5_b_in"), 16 * 4)
        dve.wait_ge(s("xT_full"), KD)
        cmul([s_Bb[0][:], s_Bb[1][:]], s_B[0][:], s_B[1][:], wv_re[:].unsqueeze(2).to_broadcast([P, PAIRS, S5H]),
             wv_im[:].unsqueeze(2).to_broadcast([P, PAIRS, S5H]), small_tmp(S5H))
        for r in range(2):
            for j in range(LC):
                d(v.tensor_copy(s_LR[r][:, :, j], L[r][:, :, LC - 1 - j]))
        w()
        HP = PAIRS // 2
        for hp in range(2):
            q = slice(hp * HP, hp * HP + HP)
            sh4 = [P, HP, LC, S5H]
            tmp = [s_tt[:, n, 0:1024].rearrange("p (a b c) -> p a b c", a=HP, b=LC) for n in range(4)]
            cmul([s_Ppre[r][:, q, :].rearrange("p a (b c) -> p a b c", b=LC) for r in range(2)],
                 s_Bb[0][:, q, :].unsqueeze(2).to_broadcast(sh4), s_Bb[1][:, q, :].unsqueeze(2).to_broadcast(sh4),
                 s_LR[0][:, q, :].unsqueeze(3).to_broadcast(sh4), s_LR[1][:, q, :].unsqueeze(3).to_broadcast(sh4), tmp)
        v.memset(junk[:], 0.0).then_inc(s("Ppre_ready"), 1)
        dve.wait_ge(s("C_copied"), 1)
        for hp in range(2):
            q = slice(hp * HP, hp * HP + HP)
            sh4 = [P, HP, 9, S5H]
            tmp = [s_tt[:, n, :].rearrange("p (a b c) -> p a b c", a=HP, b=9) for n in range(4)]
            ins4 = [(s_C[r][:, q, :].unsqueeze(2).to_broadcast(sh4)) for r in range(2)]
            lam4 = [(L[r][:, q, :].unsqueeze(3).to_broadcast(sh4)) for r in range(2)]
            d(TT(tmp[0], ins4[0], lam4[0], MUL))
            d(TT(tmp[1], ins4[1], lam4[1], MUL))
            d(TT(tmp[2], ins4[0], lam4[1], MUL))
            one(TT(tmp[3], ins4[1], lam4[0], MUL))
            d(TT(s_G[0][:, q], tmp[0], tmp[1], SUB))
            one(STT(s_G[1][:, q].rearrange("p a b c -> p (a b c)"), s_tt[:, 2, :], -1.0, s_tt[:, 3, :], MUL, SUB))
        v.memset(junk[:], 0.0).then_inc(s("G_ready"), 1)

        dve.wait_ge(s("u_out"), 16 * S5T)
        v.memset(s_Toep[:], 0.0).then_inc(s("Toep_zero"), 1)
        u_r, u_i = cosv, sn
        for sq in range(3):
            cmul([u_r[:], u_i[:]], u_r[:], u_i[:], u_r[:], u_i[:], [e_x[:], e_n[:], e_r[:], e_q[:]])
            one(TT(e_e[:], e_e[:], e_e[:], MUL))
        d(v.tensor_copy(s_E[0][:, :, 0], u_r[:]))
        one(v.tensor_copy(s_E[1][:, :, 0], u_i[:]))
        st = [s_t[:, 512 * q:512 * q + 512] for q in range(4)]
        for e in range(7):
            n = 1 << e
            step = min(n, 16)
            for c0 in range(0, n, step):
                tmp = [s_t[:, 256 * m:256 * m + PAIRS * step].rearrange("p (a b) -> p a b", b=step) for m in range(4)]
                cmul([s_E[r][:, :, n + c0:n + c0 + step] for r in range(2)],
                     s_E[0][:, :, c0:c0 + step], s_E[1][:, :, c0:c0 + step],
                     wide(s_E[0][:, :, n - 1:n], step), wide(s_E[1][:, :, n - 1:n], step), tmp)
        dve.wait_ge(s("V_copied"), 4)
        for sign in (-1, 1):
            if sign == 1:
                for r in range(2):
                    for pr in range(PAIRS):
                        d(v.tensor_tensor_scan(s_V[r][:, pr, :], e_e[:, pr:pr + 1].to_broadcast([P, NC8]), s_V[r][:, pr, :],
                                               0.0, MUL, ADD))
                w()
            for q4 in range(4):
                q = slice(4 * q4, 4 * q4 + 4)
                tmp = [t[:, 0:512].rearrange("p (a b) -> p a b", b=NC8) for t in st]
                Er, Ei, Vr, Vi = s_E[0][:, q], s_E[1][:, q], s_V[0][:, q], s_V[1][:, q]
                d(TT(tmp[0], Er, Vr, MUL))
                d(TT(tmp[1], Ei, Vi, MUL))
                d(TT(tmp[2], Er, Vi, MUL))
                one(TT(tmp[3], Ei, Vr, MUL))
                if sign == -1:
                    d(TT(Vr, tmp[0], tmp[1], ADD))
                    one(TT(Vi, tmp[2], tmp[3], SUB))
                else:
                    d(TT(Vr, tmp[0], tmp[1], SUB))
                    one(TT(Vi, tmp[2], tmp[3], ADD))
        v.memset(junk[:], 0.0).then_inc(s("X_ready"), 1)
        dve.wait_ge(s("uP_in"), 16)
        dve.wait_ge(s("Yp_in"), 16)
        tiles.n += S5T + KD

        def lo_gelu(t):
            dve.wait_ge(s("gelu_hi"), t + 1)
            TT(o_lo[:, t, :], s_Yp[:, t, :], o_hi[:, t, :].bitcast(F32), SUB).then_inc(s("gelu_split"), 1)
        for t in range(S5T):
            STT(s_Yp[:, t, :], s_uP2[:, t, :], cols[:, V_S5D + t:V_S5D + t + 1], s_Yp[:, t, :], MUL, ADD).then_inc(s("yd_ready"), 1)
            if t:
                lo_gelu(t - 1)
        lo_gelu(S5T - 1)
        for t in range(S5T):
            n = tiles.next()
            freed(n)
            TT(s_Yp[:, t, :], s_Yp[:, t, :], s_sig[:], MUL).then_inc(s("glu_out"), 1)
        for t in range(S5T):
            dve.wait_ge(s("s5_hi"), t + 1)
            vw = lambda x: x.rearrange("p (c j) -> p j c", j=LC)
            TT(vw(o_lo[:, t, :]), s_Yp[:, t, :].rearrange("p (j c) -> p j c", j=LC), vw(o_hi[:, t, :].bitcast(F32)),
               SUB).then_inc(s("s5_split"), 1)

        def merge(base):
            for q in range(2):
                freed(tiles.n - 2 + q)
            for j in range(KD):
                n = tiles.next()
                full(n)
                TT(M[:, j, :], acc[n % 2][:], M[:, j, :], MUL).then_inc(acc_free[n % 2], 1)
                freed(n)
                if j % 2 == 0:
                    dve.wait_ge(s(f"M_in{j // 2}"), 16 * (base // KD + 1))
                TT(M[:, j, :], M[:, j, :], m_prev[:, j, :], ADD).then_inc(s("merged_add"), 1)

        if last_stage >= 2:
            for q in range(2):
                freed(tiles.n - 2 + q)
            for j in range(KD):
                n = tiles.next()
                full(n)
                TT(M[:, j, :], acc[n % 2][:], M[:, j, :], MUL).then_inc(acc_free[n % 2], 1)
                ada_mult(4 + j)
            dve.wait_ge(s("ada_used"), 12)
            one(TT(mod[:, 16:48], pX[:, 16:48], cols[:, V_ADAB + 16:V_ADAB + 48], ADD))
            STT(scale2[:], mod[:, M_SC2:M_SC2 + 8], 1.0, cols[:, V_N2:V_N2 + 8], ADD, MUL).then_inc(s("mod_ready"), 1)

        if last_stage >= 3:
            tiles.n += 2
            with dve.Fori(0, GLA_PAIRS) as i:
                tiles.loop(i, 10)
                chain.loop(i, 17)
                v.tensor_copy(gkw_cur[:], gkw[:, bass.ds(i * P, P)]).then_inc(s("gkw_ready"), 1)
                dve.wait_ge(s("z_full"), i + 1)
                TS(g_kinv[:], pX[:], cols[:, bass.ds(V_GKB + i, 1)], None, ADD).then_inc(s("g_z"), 1)
                dve.wait_ge(s("g_ln"), i + 1)
                one(STT(g_kinv[:], g_kinv[:], 0.0, g_eb[:], ALU.min, SUB))
                for n in range(NCH):
                    t0 = n * GLA_CHUNK
                    ins = v.tensor_tensor_scan(g_S[:, t0:t0 + GLA_CHUNK], ones[:, 0:GLA_CHUNK], g_kinv[:, t0:t0 + GLA_CHUNK],
                                               0.0, MUL, ADD)
                ins.then_inc(s("g_S_ready"), 1)
                dve.wait_ge(s("g_S_ready"), i + 1)
                Sv = v3(g_S, NCH)
                TT(v3(g_kl, NCH), Sv[:, :, GLA_CHUNK - 1:GLA_CHUNK].to_broadcast([P, NCH, GLA_CHUNK]), Sv, SUB
                   ).then_inc(s("g_kx_ready"), 1)
                n = tiles.next()
                full(n)
                dve.wait_ge(s("g_klx"), i + 1)
                TT(g_kl[:], acc[n % 2][:], g_kl[:], MUL).then_inc(s("kl_ready"), 1)
                TT(g_kinv[:], acc[n % 2][:], g_kinv[:], MUL).then_inc(acc_free[n % 2], 1)
                n = tiles.next()
                full(n)
                STT(g_qd[:], acc[n % 2][:], GLA_DK ** -0.5, g_eb[:], MUL, MUL).then_inc(acc_free[n % 2], 1)
                tiles.n += 8
                one(v.memset(g_S0[:, 0, :], 0.0))
                for n in range(NCH - 1):
                    if n % 8 == 0:
                        dve.wait_ge(s("ds_full"), i * 2 + (n // 8 + 1))
                    ins = STT(g_S0[:, n + 1, :], g_S0[:, n, :], g_eb[:, 64 * n + 63:64 * n + 64],
                              [pX, pY][n // 8][:, ds_col(n):ds_col(n) + P], MUL, ADD)
                    if n < NCH - 2:
                        one(ins)
                ins.then_inc(s("S0_ready"), 1)
                one(v.memset(g_attn[:], 0.0))
                for hd in range(2):
                    dve.wait_ge(s("attn_full"), i * 2 + (hd + 1))
                    settle(dve)
                    v.copy_predicated(g_attn[:], gla_mask[:].unsqueeze(1).to_broadcast([P, 8, P]), v3(pX, 8)
                                      ).then_inc(s("attn_ready"), 1)
                    no = i * 2 + (hd + 1)
                    dve.wait_ge(s("g_rstd_ready"), no)
                    STT(g_sq[:], pY[:], cols[:, V_GLAG:V_GLAG + 1], g_rstd[:], MUL, MUL).then_inc(s("g_o_read"), 1)
                    dve.wait_ge(s("g_o_read"), no)
                    TT(g_sq[:], g_sq[:], g_sil[:], MUL).then_inc(s("g_y_ready"), 1)
                    dve.wait_ge(s("g_hi"), no)
                    slot = bass.ds(i * 2 + hd, 1)
                    TT(o_lo[:, slot, :].rearrange("p a b -> p (a b)"), g_sq[:],
                       o_hi[:, slot, :].rearrange("p a b -> p (a b)").bitcast(F32), SUB).then_inc(s("gla_split"), 1)
            tiles.end(GLA_PAIRS)
            chain.end(GLA_PAIRS)
            merge(0)

        if last_stage >= 4:
            dve.wait_ge(s("R_in"), 16)
            with dve.Fori(0, DH // 2) as i:
                tiles.loop(i, 42)
                chain.loop(i, 54)
                for hh in range(2):
                    one(TS(d_R[:], d_R[:], 0.25, None, MUL))
                    for qk in range(2):
                        no = i * 4 + (2 * hh + qk + 1)
                        n = tiles.next()
                        dve.wait_ge(s("d_rstd_ready"), no)
                        one(v.reciprocal(d_rs[:], d_rs[:]))
                        full(n)
                        STT([d_q, d_k][qk][:], acc[n % 2][:], [qg[:], cols[:, V_KG:V_KG + 1]][qk], d_rs[:], MUL, MUL
                            ).then_inc(acc_free[n % 2], 1)
                        freed(n)
                    tiles.n += 1

                    def maxima(qb):
                        kw = (qb + 1) * QB
                        if qb >= 2:
                            dve.wait_ge(s("d_wT_full"), i * 16 + (8 * hh + qb - 1))
                        for j in range(2):
                            n = tiles.next()
                            full(n)
                            settle(dve)
                            v.tensor_tensor_reduce(out=d_s[:, qb % 2, j, 0:kw], in0=acc[n % 2][:, 0:kw],
                                                   in1=d_R[:, T - kw:T], scale=1.0, scalar=-3e38, op0=ADD, op1=ALU.max,
                                                   accum_out=mx[:, qb % 2, j:j + 1]).then_inc(acc_free[n % 2], 1)
                        freed(n)
                        TS(nmx[:, qb % 2, :], mx[:, qb % 2, :], -1.0, None, MUL).then_inc(s("d_mx_ready"), 1)

                    maxima(0)
                    for qb in range(NQB):
                        if qb + 1 < NQB:
                            maxima(qb + 1)
                        if qb in GATE_AT:
                            tiles.n += 1
                        kw, b = (qb + 1) * QB, qb % 2
                        dve.wait_ge(s("d_p_ready"), i * 16 + (8 * hh + qb + 1))
                        one(v.reciprocal(rinv[:, b, :], rsum[:, b, :]))
                        one(TT(rinv[:, b, 1:2], rinv[:, b, 1:2], neg_lam[:], MUL))
                        one(TS(d_s[:, b, 1, 0:kw], d_s[:, b, 1, 0:kw], rinv[:, b, 1:2], None, MUL))
                        STT(d_s[:, b, 0, 0:kw], d_s[:, b, 0, 0:kw], rinv[:, b, 0:1], d_s[:, b, 1, 0:kw], MUL, ADD
                            ).then_inc(s("d_w_ready"), 1)
                        if qb % 4 == 3:
                            grp = qb // 4
                            no = i * 4 + (2 * hh + grp + 1)
                            dve.wait_ge(s("d_orstd"), no)
                            STT(o_sq[:], pY[:, 0:HALF], subg[:], o_sq[:], MUL, MUL).then_inc(s("d_o_read"), 1)
                            dve.wait_ge(s("d_hi"), no)
                            pos = (slice(None), bass.ds(i * 2 + hh, 1), slice(grp * HALF, (grp + 1) * HALF))
                            TT(o_lo[pos].rearrange("p a b -> p (a b)"), o_sq[:],
                               o_hi[pos].rearrange("p a b -> p (a b)").bitcast(F32), SUB).then_inc(s("diff_split"), 1)
            tiles.end(DH // 2)
            chain.end(DH // 2)
            merge(KD)

        if last_stage >= 5:
            for k in range(KD):
                dve.wait_ge(s("merged_hi"), k + 1)
                ins = TT(h_lo[:, k, :], M[:, k, :], h_hi[:, k, :].bitcast(F32), SUB)
            ins.then_inc(s("merged_split"), 1)
            dve.wait_ge(s("xT_in"), 16)
            with dve.Fori(0, 4) as i:
                tiles.loop(i, 2)
                for j in range(2):
                    n = tiles.next()
                    full(n)
                    mk_ = M[:, bass.ds(i * 2 + j, 1), :].rearrange("p a b -> p (a b)")
                    STT(mk_, acc[n % 2][:], mod[:, bass.ds(M_GT1 + j + i * 2, 1)], mk_, MUL, ADD).then_inc(acc_free[n % 2], 1)
            tiles.end(4)
            dve.wait_ge(s("nrm_rstd2"), 1)
            norm_rest(2, M, scale2, M_SH2)

        if last_stage >= 6:
            def up(g, par):
                for c in range(2):
                    for ag in range(2):
                        n = tiles.next()
                        full(n)
                        dve.wait_ge(s("f_lin"), g * 4 + (2 * c + ag + 1))
                        buf = [f_a, f_g][ag][:, c, :]
                        ch = V_CONV + 22 * ag + g * 2 + c
                        one(STT(buf[:, 1:T], acc[n % 2][:, 0:T - 1], cols[:, bass.ds(ch + NT_FF, 1)], buf[:, 1:T], MUL, ADD))
                        STT(buf[:, 2:T], acc[n % 2][:, 0:T - 2], cols[:, bass.ds(ch, 1)], buf[:, 2:T], MUL, ADD
                            ).then_inc(acc_free[n % 2], 1)
                    freed(n)
                    dve.wait_ge(s("f_silu"), g * 2 + (c + 1))
                    TT(f_a[:, c, :], f_a[:, c, :], f_g[:, c, :], MUL).then_inc(s("f_prod"), 1)
                    dve.wait_ge(s("f_hi"), g * 2 + (c + 1))
                    TT(o_lo[:, 2 * par + c, :], f_a[:, c, :], o_hi[:, 2 * par + c, :].bitcast(F32), SUB).then_inc(s("act_split"), 1)

            def down():
                for m in range(KD):
                    n = tiles.next()
                    full(n)
                    STT(M[:, m, :], acc[n % 2][:], mod[:, M_GT2 + m:M_GT2 + m + 1], M[:, m, :], MUL, ADD).then_inc(acc_free[n % 2], 1)

            up(0, 0)
            with dve.Fori(0, (FG - 1) // 2) as i:
                tiles.loop(i, 24)
                chain.loop(i, 8)
                for q in range(2):
                    up(i * 2 + (q + 1), (q + 1) % 2)
                    down()
            tiles.end((FG - 1) // 2)
            chain.end((FG - 1) // 2)
            down()

    ctx.close()


_INS = ["x", "c", "ada_w", "ada_b", "norm1_g", "w_in", "gla_gk_w", "gla_gk_b", "gla_norm_g", "s5_lambda_re",
        "s5_lambda_im", "s5_b_re", "s5_b_im", "s5_c_re", "s5_c_im", "s5_d", "s5_log_dt", "s5_glu_w", "s5_glu_b",
        "diff_q_norm_g", "diff_k_norm_g", "diff_lambda_q1", "diff_lambda_k1", "diff_lambda_q2", "diff_lambda_k2",
        "diff_subln_g", "w_branch_gla", "w_branch_s5", "w_branch_diff", "w_out", "norm2_g", "ffn_w_up",
        "ffn_conv_w", "ffn_conv_b", "ffn_w_down"]


def kernel(**inputs):
    import numpy as np
    import concourse.bacc as bacc
    from concourse.bass_utils import run_bass_kernel_spmd

    nc = bacc.Bacc("TRN2", target_bir_lowering=False, num_devices=1)
    arrays, aps = {}, {}
    for name in _INS:
        arr = np.ascontiguousarray(inputs[name])
        arrays[f"in_{name}"] = arr
        aps[name] = nc.dram_tensor(f"in_{name}", arr.shape, mybir.dt.from_np(arr.dtype), kind="ExternalInput").ap()
    aps["out"] = nc.dram_tensor("out_0", (1, T, D), F32, kind="ExternalOutput").ap()
    build(nc, aps)
    r = run_bass_kernel_spmd(nc, [arrays], core_ids=[0])
    return r.results[0]["out_0"]
```

```python
import math

import concourse.bass as bass
from concourse import mybir
from contextlib import ExitStack

F32 = mybir.dt.float32
F32R = mybir.dt.float32r
I32 = mybir.dt.int32
ALU = mybir.AluOpType
ACT = mybir.ActivationFunctionType

P = 128
D = 1024
T = 1024
KD = D // P
HALF = 512
GLA_HEADS, GLA_DK, GLA_DV, GLA_LR, GLA_CHUNK = 4, 64, 128, 16, 64
GLA_PAIRS = GLA_HEADS // 2
NCH = T // GLA_CHUNK
S5W, S5G, S5H, S5P = 512, 32, 16, 64
S5T = S5W // P
PAIRS = S5G // 2
LC = 8
NC8 = T // LC
GATE_AT = (3, 7)
DH, DD = 4, 64
QB = 128
NQB = T // QB
STEPS = NQB + 5
F = 2816
FG = F // 256
N_ROWS = 24
EPS = 1e-6
LAMBDA_INIT = 0.8 - 0.6 * math.exp(-0.3 * 0)

C_GQ = 0
C_GK = C_GQ + GLA_HEADS * GLA_DK
C_GV = C_GK + GLA_HEADS * GLA_DK
C_GR = C_GV + GLA_HEADS * GLA_DV
C_LR = C_GR + GLA_HEADS * GLA_DV
C_SU = C_LR + GLA_LR
C_DQ = C_SU + S5W
C_DK = C_DQ + DH * 2 * DD
C_DV = C_DK + DH * 2 * DD
C_GATE = C_DV + DH * 2 * DD

V_ADAB, V_N1, V_N2, V_C, V_GKB, V_S5D, V_GLUB, V_GLAG, V_SUBG, V_QG, V_KG, V_ROWS = (
    0, 48, 56, 64, 72, 74, 78, 82, 83, 84, 85, 86)
V_CONV = V_ROWS
NT_FF = 2 * F // P
V_CONVB = V_CONV + 3 * NT_FF
V_END = V_CONVB + NT_FF
M_SH1, M_SC1, M_GT1, M_SH2, M_SC2, M_GT2 = 0, 8, 16, 24, 32, 40


class Chain:

    def __init__(self, eng, sem):
        self.eng, self.sem, self.n, self.extra, self.base, self.per = eng, sem, 0, 0, 0, 0

    def loop(self, reg, per):
        self.base, self.per, self.extra = self.n, per, reg * per

    def end(self, count):
        assert self.n - self.base == self.per, (self.n - self.base, self.per)
        self.n, self.extra = self.base + self.per * count, 0

    def did(self, ins):
        ins.then_inc(self.sem, 1)
        self.n += 1

    def wait(self):
        self.eng.wait_ge(self.sem, self.extra + self.n)


class Count:

    def __init__(self):
        self.n, self.reg, self.per, self.base = 0, None, 0, 0

    def loop(self, reg, per):
        assert per % 2 == 0 and self.n % 2 == 0
        self.base, self.reg, self.per = self.n, reg, per

    def end(self, count):
        assert self.n - self.base == self.per, (self.n - self.base, self.per)
        self.n, self.reg = self.base + self.per * count, None

    def next(self):
        self.n += 1
        return self.n - 1

    def whole(self, n):
        return n + 1 if self.reg is None else self.reg * self.per + (n + 1)

    def half(self, n):
        return n // 2 + 1 if self.reg is None else self.reg * (self.per // 2) + (n // 2 + 1)


def build(nc, a):
    w_in = a["w_in"][0]
    ctx = ExitStack()

    KB = 1024
    ctx.enter_context(nc.sbuf_tensor("slab", [P, 415 * 128], F32))
    BASE = 16512

    def at(name, shape, dt, off):
        return nc.alloc_sbuf_tensor_at(name, shape, dt, offset=BASE + off)

    small = [0]

    def const(name, shape, dt=F32):
        n = 4
        for s in shape[1:]:
            n *= s
        t = at(name, shape, dt, small[0])
        small[0] += (n + 31) // 32 * 32
        return t

    ident = const("ident", [P, P])
    ones = const("ones", [P, P])
    half_ones = const("half_ones", [P, P])
    gla_mask = const("gla_mask", [P, P], I32)
    cols = const("cols", [P, V_END])
    mod = const("mod", [P, 48])
    scale1 = const("scale1", [P, KD])
    scale2 = const("scale2", [P, KD])
    c_act = const("c_act", [P, KD])
    eps_col = const("eps_col", [P, 1])
    one_col = const("one_col", [P, 1])
    gkw = const("gkw", [GLA_LR, GLA_HEADS * GLA_DK])
    gkw_cur = const("gkw_cur", [GLA_LR, P])
    junk = const("junk", [P, 2])
    lam_in = const("lam_in", [DD, 4])
    lam_pr = const("lam_pr", [DD, 2])
    lam_e = const("lam_e", [P, 2])
    neg_lam = const("neg_lam", [P, 1])
    subg = const("subg", [P, 1])
    qg = const("qg", [P, 1])
    mx = const("mx", [P, 2, 2])
    nmx = const("nmx", [P, 2, 2])
    rsum = const("rsum", [P, 2, 2])
    rinv = const("rinv", [P, 2, 2])
    assert small[0] <= 6 * KB - 512, small[0]
    o_sq = at("o_sq", [P, HALF], F32, 6 * KB - 512)
    w_raw = at("w_raw", [P, 2, 8, P], F32, 8 * KB - 512)
    w_hi = at("w_hi", [P, 2, 8, P], F32R, 16 * KB - 512)
    w_lo = at("w_lo", [P, 2, 8, P], F32R, 24 * KB - 512)
    H0, O0, M0, A0 = 32 * KB - 512, 96 * KB - 512, 128 * KB - 512, 160 * KB - 512
    h_hi = at("h_hi", [P, KD, T], F32R, H0)
    h_lo = at("h_lo", [P, KD, T], F32R, H0 + 32 * KB)
    o_hi = at("o_hi", [P, 4, T], F32R, O0)
    o_lo = at("o_lo", [P, 4, T], F32R, O0 + 16 * KB)
    M = at("M", [P, KD, T], F32, M0)

    rows_a = at("rows_a", [P, P], F32, H0)
    rows_b = at("rows_b", [P, P], F32, H0 + 512)
    R0 = at("R0", [P, T], F32, H0 + 8 * KB)
    rows_c = at("rows_c", [P, P], F32, H0 + KB)
    x_tok = at("x_tok", [P, NQB, D], F32, O0)
    ada_v = a["ada_w"][0].rearrange("(k p) c -> p k c", p=P)
    ada_first = [at(f"ada_first{q}", [P, 2, KD, HALF], F32, (M0, H0 + 32 * KB)[q]) for q in range(2)]
    ada_ring = at("ada_ring", [P, 2, KD, HALF], F32, A0)
    ada_sums = [at(f"ada_sum{q}", [P, 4, HALF], F32, (H0 + 16 * KB, A0 + 38 * KB)[q]) for q in range(2)]
    xT0 = at("xT0", [P, KD, T], F32, A0)
    n_tmp = at("n_tmp", [P, 2, T], F32, A0 + 36 * KB)
    sq_sum = at("sq_sum", [P, T], F32, O0)
    n_rstd = at("n_rstd", [P, T], F32, O0 + 18 * KB)

    pA = ctx.enter_context(nc.psum_tensor("pA", [P, T], F32))
    pB = ctx.enter_context(nc.psum_tensor("pB", [P, T], F32))
    pX = ctx.enter_context(nc.psum_tensor("pX", [P, T], F32))
    pY = ctx.enter_context(nc.psum_tensor("pY", [P, T], F32))
    acc = [pA, pB]

    def sem(name):
        return ctx.enter_context(nc.semaphore(name))

    w_loaded = [sem("w_loaded0"), sem("w_loaded1")]
    w_hi_done = sem("w_hi_done")
    w_split = sem("w_split")
    w_started = sem("w_started")
    acc_full = [sem("acc_full0"), sem("acc_full1")]
    acc_free = [sem("acc_free0"), sem("acc_free1")]
    act_chain, dve_chain, pool_chain = sem("act_chain"), sem("dve_chain"), sem("pool_chain")

    settled = {e.engine: sem(f"settled_{n}") for n, e in
               (("sp", nc.sync), ("pool", nc.gpsimd), ("pe", nc.tensor), ("dve", nc.vector))}
    block = ctx.enter_context(nc.Block())
    S = {}
    total_units = [0]

    def s(name):
        if name not in S:
            S[name] = sem(name)
        return S[name]

    def settle(eng):
        eng.sem_inc(settled[eng.engine], 1)

    def ds_col(n):
        return HALF * (n % 2) + P * (n % 8 // 2)

    def v3(t, n):
        return t.rearrange("p (a b) -> p a b", a=n)

    def gemm(pe, units, tiles, new_unit, ks, rhs_hi, rhs_lo, ready=None, mid=None, mid_at=1, per_chunk=1):
        if new_unit:
            u = units.next()
            pe.wait_ge(w_split, units.whole(u))
        else:
            u = units.n - 1
        t = tiles.next()
        if t >= 2:
            pe.wait_ge(acc_free[t % 2], tiles.half(t) - 1)
        dst = acc[t % 2]
        n, total = 0, len(ks) * 6
        for k, w in ks:
            if ready is not None:
                pe.wait_ge(ready, (k + 1) * per_chunk)
            if mid is not None and k == mid_at:
                mid()
            for wp, rp in ((w_hi, rhs_hi), (w_hi, rhs_lo), (w_lo, rhs_hi)):
                for hf in range(2):
                    ins = nc.tensor.matmul(dst[:, hf * HALF:(hf + 1) * HALF], wp[:, u % 2, w, :],
                                           rp[:, k, hf * HALF:(hf + 1) * HALF],
                                           start=(n < 2), stop=(n >= total - 2))
                    if n == 0 and new_unit:
                        ins.then_inc(w_started, 1)
                    n += 1
        ins.then_inc(acc_full[t % 2], 1)

    K8 = [(k, k) for k in range(8)]

    def gemm_h(pe, units, tiles, ready=None, mid=None, mid_at=1):
        gemm(pe, units, tiles, True, K8, h_hi, h_lo, ready, mid, mid_at)

    def load(sp, units, src, view):
        u = units.next()
        if u >= 2:
            sp.wait_ge(w_split, units.whole(u) - 2)
            settle(sp)
        sp.dma_start(view(w_raw[:, u % 2]), src).then_inc(w_loaded[u % 2], 16)

    def load_cols(sp, units, w, col):
        load(sp, units, w[:, bass.ds(col, P)].rearrange("(k p) c -> p k c", p=P), lambda t: t)

    def load_k4(sp, units, w, col):
        load(sp, units, w[:, bass.ds(col, 256)].rearrange("(k p) c -> p k c", p=P),
             lambda t: t.rearrange("p (k c) n -> p k (c n)", k=4))

    def load_down(sp, units, w, row, col):
        load(sp, units, w[bass.ds(row, 256), col:col + 512].rearrange("(k p) c -> p k c", p=P),
             lambda t: t.rearrange("p (k c) n -> p k (c n)", k=2))

    xT_dram = nc.dram_tensor("xT_scratch", (D, T), F32).ap()
    m_dram = nc.dram_tensor("merged_scratch", (D, T), F32).ap()
    R_dram = nc.dram_tensor("alibi_scratch", (P, T), F32).ap()
    u_dram = nc.dram_tensor("u_scratch", (S5W, T), F32).ap()
    y_dram = nc.dram_tensor("y_scratch", (S5W, T), F32).ap()

    rows_s = at("rows_s", [PAIRS, 3, P], F32, H0 + 2 * KB)
    dt_row = at("dt_row", [PAIRS, 2], F32, H0 + 4 * KB)
    s_G = [at(f"s_G{r}", [P, PAIRS, 9, S5H], F32, A0 + 9216 * r) for r in range(2)]
    s_U = at("s_U", [P, S5G, NC8], F32, A0 + 18 * KB)
    s_uP = at("s_uP", [P, S5T, LC, NC8], F32, M0 + 16 * KB)
    s_PT = [at(f"s_PT{r}", [P, PAIRS, P], F32, M0 + 8 * KB * r) for r in range(2)]
    s_Toep = at("s_Toep", [P, S5G, P], F32, M0 + 16 * KB)
    s_Ppre = [at(f"s_Ppre{r}", [P, PAIRS, P], F32, O0 + 8 * KB * r) for r in range(2)]
    s_K = at("s_K", [S5H, S5G, P], F32, O0)
    s_V = [at(f"s_V{r}", [P, PAIRS, NC8], F32, O0 + 8 * KB * r) for r in range(2)]
    s_E = [at(f"s_E{r}", [P, PAIRS, NC8], F32, O0 + 16 * KB + 8 * KB * r) for r in range(2)]
    s_t = at("s_t", [P, 4 * 512], F32, A0 + 36 * KB)
    s_Y = at("s_Y", [P, S5G, NC8], F32, O0 + 16 * KB)
    s_Yp = at("s_Yp", [P, S5T, T], F32, A0)
    s_uP2 = at("s_uP2", [P, S5T, T], F32, A0 + 18 * KB)
    s_sig = at("s_sig", [P, T], F32, A0 + 34 * KB)
    SM = A0 + 44 * KB

    small_end = [SM]

    def mk(name, shape, dt=F32):
        n = 4
        for x in shape[1:]:
            n *= x
        small_end[0] += (n + 31) // 32 * 32
        return at(name, shape, dt, small_end[0] - (n + 31) // 32 * 32)

    l_re, l_im, l_dt = mk("l_re", [P, PAIRS]), mk("l_im", [P, PAIRS]), mk("l_dt", [P, PAIRS])
    e_x, e_n, e_r, e_q, e_em, e_e = [mk(f"e_{i}", [P, PAIRS]) for i in range(6)]
    e_int = mk("e_int", [P, PAIRS], I32)
    th, sn, sh, cm = [mk(f"ph_{i}", [P, PAIRS]) for i in range(4)]
    cosv, cr, ci, inv = [mk(f"cc_{i}", [P, PAIRS]) for i in range(4)]
    wv_re, wv_im = [mk(f"wv_{i}", [P, PAIRS]) for i in range(2)]
    Lp = [mk(f"Lp{r}", [P, PAIRS, 9]) for r in range(2)]
    assert small_end[0] <= A0 + 48 * KB
    s_LR = [at(f"s_LR{r}", [P, PAIRS, 8], F32, O0 + 24 * KB + 512 * r) for r in range(2)]
    s_B = [at(f"s_B{r}", [P, PAIRS, S5H], F32, O0 + 26 * KB + KB * r) for r in range(2)]
    s_Bb = [at(f"s_Bb{r}", [P, PAIRS, S5H], F32, A0 + 42 * KB + KB * r) for r in range(2)]
    s_C = [at(f"s_C{r}", [P, PAIRS, S5H], F32, O0 + 30 * KB + KB * r) for r in range(2)]
    c_rows = at("c_rows", [P, 2, 2, P], F32, O0 + 22 * KB)
    s_tt = at("s_tt", [P, 4, 2304 // 2], F32, A0 + 18 * KB)

    def blk(name, n, shape):
        return at(name, shape, F32, A0 + 4 * KB * n)
    g_lr = blk("g_lr", 0, [GLA_LR, T])
    g_S = blk("g_S", 1, [P, T])
    g_vT = blk("g_vT", 1, [P, T])
    g_rstd = blk("g_rstd", 1, [P, T])
    g_eb = blk("g_eb", 2, [P, T])
    g_kinv = blk("g_kinv", 3, [P, T])
    g_kl = blk("g_kl", 4, [P, T])
    g_attn = blk("g_attn", 4, [P, 8, P])
    g_qd = blk("g_qd", 5, [P, T])
    g_klT = blk("g_klT", 6, [P, 8, P])
    g_sq = blk("g_sq", 6, [P, T])
    g_S0 = blk("g_S0", 7, [P, NCH, P])
    g_v = blk("g_v", 9, [P, 2, 8, P])
    g_sil = blk("g_sil", 11, [P, T])

    d_R = blk("d_R", 0, [P, T])
    d_q = blk("d_q", 1, [P, T])
    d_k = blk("d_k", 2, [P, T])
    d_v = blk("d_v", 3, [P, 8, P])
    d_s = blk("d_s", 4, [P, 2, 2, T])
    d_tmp = blk("d_tmp", 4, [P, 2, T])
    d_w = blk("d_w", 10, [P, 2, T])
    d_wT = blk("d_wT", 8, [P, 2, 8, P])
    d_vT = blk("d_vT", 8, [P, T])
    d_rs = blk("d_rs", 9, [P, T])

    m_prev = blk("m_prev", 0, [P, KD, T])
    f_a = blk("f_a", 0, [P, 2, T])
    f_g = blk("f_g", 2, [P, 2, T])
    f_raw = blk("f_raw", 4, [P, 2, T])
    out_tok = blk("out_tok", 6, [P, 2, D])

    @block.sync
    def _(sp):
        units = Count()
        x_v = a["x"][0].rearrange("(n p) d -> p n d", p=P)
        for q in range(4):
            sp.dma_start(x_tok[:, 2 * q:2 * q + 2, :], x_v[:, 2 * q:2 * q + 2, :]).then_inc(s(f"x_in{q}"), 16)
        sp.wait_ge(s("rows_in"), 16 * N_ROWS)
        for n in range(4):
            sp.dma_start(ada_first[n // 2][:, n % 2], ada_v[:, :, n * HALF:(n + 1) * HALF]).then_inc(s(f"ada_first{n}"), 16)
        for t in range(2):
            load_cols(sp, units, w_in, C_SU + t * P)
        sp.wait_ge(s("xT_copied"), KD)
        sp.dma_start(xT_dram.rearrange("(k p) t -> p k t", p=P), xT0[:]).then_inc(s("xT_stored"), 16)
        for r, nm in enumerate(("s5_b_re", "s5_b_im")):
            for gp in range(2):
                sp.dma_start(s_B[r][64 * gp:64 * gp + 64],
                             a[nm][0].rearrange("(r g) p h -> g p r h", g=2)[gp]).then_inc(s("s5_b_in"), 16)
        for r, nm in enumerate(("s5_c_re", "s5_c_im")):
            cv = a[nm][0].rearrange("(t r g) h p -> t g r h p", g=2, t=2)
            for t in range(2):
                for gp in range(2):
                    sp.dma_start(c_rows[:, r, t, 64 * gp:64 * gp + 64], cv[t, gp]).then_inc(s("s5_c_in"), 16)

        for t in range(2, S5T):
            load_cols(sp, units, w_in, C_SU + t * P)
        for g in range(2):
            load_cols(sp, units, w_in, C_GATE + D + g * P)
        for t in range(S5T):
            sp.wait_ge(acc_free[t % 2], t // 2 + 1)
            sp.dma_start(u_dram[t * P:(t + 1) * P, :], s_uP[:, t]).then_inc(s("u_out"), 16)
        sp.wait_ge(s("u_out"), 16 * S5T)
        sp.wait_ge(s("G_ready"), 1)
        u_v = u_dram.rearrange("(g h) (j c) -> j h g c", h=S5H, j=LC)
        for j in range(LC):
            sp.dma_start(s_U[16 * j:16 * j + 16], u_v[j]).then_inc(s("U_in"), 16)
        sp.wait_ge(s("K_copied"), 4)
        sp.wait_ge(s("Toep_zero"), 1)
        for j in range(LC):
            sp.dma_start(s_Toep[16 * j:16 * j + 16, :, 16 * j:P], s_K[:, :, 0:P - 16 * j]).then_inc(s("Toep_in"), 16)
        for g in range(2, KD):
            load_cols(sp, units, w_in, C_GATE + D + g * P)
        load_k4(sp, units, a["s5_glu_w"][0], 0)
        y_v = y_dram.rearrange("(g h) (j c) -> j h g c", h=S5H, j=LC)
        for h in range(2):
            sp.wait_ge(s("Y_copied"), 2 * h + 2)
            for j in range(LC):
                sp.dma_start(y_v[j][:, 16 * h:16 * h + 16], s_Y[16 * j:16 * j + 16, 16 * h:16 * h + 16]
                             ).then_inc(s(f"y_out{h}"), 16)
        sp.dma_start(s_uP2[:], u_dram.rearrange("(t p) n -> p t n", p=P)).then_inc(s("uP_in"), 16)
        for h in range(2):
            sp.wait_ge(s(f"y_out{h}"), 16 * LC)
            sp.dma_start(s_Yp[:, 2 * h:2 * h + 2], y_dram.rearrange("(t p) n -> p t n", p=P)[:, 2 * h:2 * h + 2]
                         ).then_inc(s(f"Yp_in{h}"), 16)
        load_k4(sp, units, a["s5_glu_w"][0], 256)

        def branch_loads(w):
            with sp.Fori(0, 2) as i:
                units.loop(i, 2)
                for j in (0, 2):
                    load_k4(sp, units, w, (i * 4 + j) * P)
            units.end(2)

        def gate_load(b, tile):
            load_cols(sp, units, w_in, C_GATE + b * D + tile * P)

        branch_loads(a["w_branch_s5"][0])
        load_cols(sp, units, w_in, C_LR)
        load_cols(sp, units, w_in, C_LR)
        with sp.Fori(0, GLA_PAIRS) as i:
            units.loop(i, 10)
            load_cols(sp, units, w_in, C_GK + i * P)
            load_cols(sp, units, w_in, C_GQ + i * P)
            load_cols(sp, units, w_in, C_GV + i * 256)
            load_cols(sp, units, w_in, C_GV + i * 256 + P)
            load_cols(sp, units, w_in, C_GR + i * 256)
            for f in range(3):
                gate_load(0, i * 4 + f)
            load_cols(sp, units, w_in, C_GR + i * 256 + P)
            gate_load(0, i * 4 + 3)
        units.end(GLA_PAIRS)
        branch_loads(a["w_branch_gla"][0])
        with sp.Fori(0, DH // 2) as i:
            units.loop(i, 10)
            for hh in range(2):
                for c in (C_DQ, C_DK, C_DV):
                    load_cols(sp, units, w_in, c + (i * 2 + hh) * P)
                for f in range(2):
                    gate_load(2, i * 4 + (2 * hh + f))
        units.end(DH // 2)
        branch_loads(a["w_branch_diff"][0])
        with sp.Fori(0, 4) as i:
            units.loop(i, 2)
            for j in range(2):
                load_cols(sp, units, a["w_out"][0], (i * 2 + j) * P)
        units.end(4)
        w_up, w_down = a["ffn_w_up"][0], a["ffn_w_down"][0]

        def up_loads(g):
            for c in (0, 1):
                load_cols(sp, units, w_up, (g * 2 + c) * P)
                load_cols(sp, units, w_up, (g * 2 + c) * P + F)

        def down_load(g, n):
            load_down(sp, units, w_down, g * 256, n * HALF)

        up_loads(0)
        with sp.Fori(0, (FG - 1) // 2) as i:
            units.loop(i, 12)
            for q in range(2):
                for c in (0, 1):
                    load_cols(sp, units, w_up, ((i * 2 + q + 1) * 2 + c) * P)
                    down_load(i * 2 + q, c)
                    load_cols(sp, units, w_up, ((i * 2 + q + 1) * 2 + c) * P + F)
        units.end((FG - 1) // 2)
        for n in range(2):
            down_load(FG - 1, n)
        total_units[0] = units.n

        out_v = a["out"][0]
        for tt in range(NQB):
            sp.wait_ge(s("out_ready"), tt + 1)
            sp.dma_start(out_v[tt * P:(tt + 1) * P, :], out_tok[:, tt % 2]).then_inc(s(f"out_stored{tt % 2}"), 16)
        for q in range(2):
            sp.wait_ge(s(f"out_stored{q}"), 16 * (NQB // 2))

    @block.gpsimd
    def _(pool):
        g = nc.gpsimd
        chain = Chain(pool, pool_chain)
        d, w = chain.did, chain.wait
        d(g.memset(ident[:], 0.0))
        d(g.memset(ones[:], 1.0))
        d(g.memset(half_ones[:], 0.0))
        d(g.memset(eps_col[:], EPS))
        d(g.memset(one_col[:], 1.0))
        d(g.memset(gla_mask[:], 1))
        w()
        d(g.affine_select(out=ident[:], in_=ident[:], compare_op=ALU.not_equal, fill=1.0, base=0,
                          pattern=[[-1, P]], channel_multiplier=1))
        w()
        d(g.memset(half_ones[0:64, 0:64], 1.0))
        w()
        d(g.memset(half_ones[64:128, 64:128], 1.0))
        w()
        d(g.affine_select(out=gla_mask[:], in_=gla_mask[:], compare_op=ALU.is_ge, fill=0.0, base=0,
                          pattern=[[1, P]], channel_multiplier=-1))
        w()
        g.affine_select(out=gla_mask[:, 64:128], in_=gla_mask[:, 64:128], compare_op=ALU.is_ge, fill=0.0,
                        base=-64, pattern=[[0, 64]], channel_multiplier=1).then_inc(s("const_ready"), 1)
        d(g.iota(R0[:], [[1, T]], base=QB - T, channel_multiplier=-1, allow_small_or_imprecise_dtypes=True))
        w()
        d(g.affine_select(out=R0[:], in_=R0[:], compare_op=ALU.is_ge, fill=-1e30, base=T - QB,
                          pattern=[[-1, T]], channel_multiplier=1))
        w()
        pool.dma_start(R_dram, R0[:]).then_inc(s("R_stored"), 16)
        pool.wait_ge(s("R_stored"), 16)

        def split(hi_count, slot):
            g.tensor_copy(w_hi[:, slot], w_raw[:, slot]).then_inc(w_hi_done, 1)
            pool.wait_ge(w_hi_done, hi_count)
            g.tensor_tensor(w_lo[:, slot], w_raw[:, slot], w_hi[:, slot].bitcast(F32), ALU.subtract).then_inc(w_split, 1)

        for u in range(2):
            pool.wait_ge(w_loaded[u], 16)
            split(u + 1, u)
        with pool.Fori(0, (total_units[0] - 2) // 2) as i:
            for q in range(2):
                pool.wait_ge(w_loaded[q], i * 16 + 32)
                pool.wait_ge(w_started, i * 2 + (q + 2))
                settle(pool)
                split(i * 2 + (q + 3), q)

    @block.tensor
    def _(pe):
        units, tiles = Count(), Count()
        mm, tr = nc.tensor.matmul, nc.tensor.transpose
        s5_col = lambda q: HALF * (q % 2) + P * (q // 2)

        def col_sums(lhs, src, dst, ready, name):
            pe.wait_ge(s(ready[0]), ready[1])
            for hf in range(2):
                ins = mm(dst[:, hf * HALF:(hf + 1) * HALF], lhs[:], src[:, hf * HALF:(hf + 1) * HALF],
                         start=True, stop=True)
            ins.then_inc(s(name), 1)

        pe.wait_ge(s("const_ready"), 1)
        pe.wait_ge(s("rows_in"), 16 * N_ROWS)
        tr(pA[:, 0:V_ROWS], rows_a[0:V_ROWS, :], ident[0:V_ROWS, 0:V_ROWS])
        tr(pA[:, 128:256], rows_b[:], ident[:])
        tr(pA[:, 256:304], rows_c[0:48, :], ident[0:48, 0:48])
        tr(pA[:, 320:336], rows_s[:, 0, :], ident[0:PAIRS, 0:PAIRS])
        tr(pA[:, 336:352], rows_s[:, 1, :], ident[0:PAIRS, 0:PAIRS])
        pe.wait_ge(s("dt_rows"), 1)
        tr(pA[:, 352:368], rows_s[:, 2, :], ident[0:PAIRS, 0:PAIRS])
        mm(pA[:, 368:370], ones[0:DD, :], lam_pr[:], start=True, stop=True).then_inc(s("rows_T"), 1)
        for q in range(4):
            pe.wait_ge(s(f"x_in{q}"), 16)
        for k in range(KD):
            if k >= 2:
                pe.wait_ge(s("xT_copied"), k - 1)
            for tt in range(NQB):
                ins = tr([pX, pY][k % 2][:, tt * P:(tt + 1) * P], x_tok[:, tt, k * P:(k + 1) * P], ident[:])
            ins.then_inc(s("xT_full"), 1)
        pe.wait_ge(s("xT_copied"), KD)
        for k in range(KD):
            pe.wait_ge(s("sq_ready"), k + 1)
            for hf in range(2):
                ins = mm(pY[:, hf * HALF:(hf + 1) * HALF], ones[:], n_tmp[:, k % 2, hf * HALF:(hf + 1) * HALF],
                         start=(k == 0), stop=(k == KD - 1))
            ins.then_inc(s("sq_summed"), 1)
        pe.wait_ge(s("cols_ready"), 1)

        def ada_cols(n, dst):
            pe.wait_ge(s("ada_mult"), n + 1)
            for c in range(4):
                ins = mm(dst[:, 4 * n + c:4 * n + c + 1], ada_sums[n >= 4][:, n % 4, c * P:(c + 1) * P],
                         ones[:, 0:1], start=True, stop=True)
            ins.then_inc(s("ada_used"), 1)

        for n in range(4):
            ada_cols(n, pA)

        pe.wait_ge(s("mod_ready"), 1)
        def c_T():
            pe.wait_ge(s("s5_c_in"), 16 * 8)
            for r in range(2):
                for t in range(2):
                    ins = tr(pX[:, (2 * r + t) * P:(2 * r + t + 1) * P], c_rows[:, r, t, :], ident[:])
            ins.then_inc(s("C_T"), 1)

        for t in range(S5T):
            gemm_h(pe, units, tiles, s("h_ready1") if t == 0 else None, c_T if t == 2 else None)

        def tables_T(r):
            pe.wait_ge(s("Ppre_ready"), 1)
            pe.wait_ge(s("C_copied"), 1)
            if r:
                pe.wait_ge(s("PT_copied"), 2)
            for pr in range(PAIRS):
                ins = tr([pX, pY][pr // 8][:, (pr % 8) * P:(pr % 8 + 1) * P], s_Ppre[r][:, pr, :], ident[:])
                if pr % 8 == 7:
                    ins.then_inc(s("PT_full"), 1)

        gemm_h(pe, units, tiles, mid=lambda: tables_T(0))
        tables_T(1)
        pe.wait_ge(s("G_ready"), 1)
        for rnd in range(4):
            pe.wait_ge(s("PT_copied"), 4)
            if rnd >= 2:
                pe.wait_ge(s("K_copied"), rnd - 1)
            for q in range(8):
                gr = rnd * 8 + q
                pr, gp = gr // 2, gr % 2
                for r in range(2):
                    ins = mm([pX, pY][rnd % 2][0:S5H, s5_col(q):s5_col(q) + P], s_Bb[r][64 * gp:64 * gp + 64, pr, :],
                             s_G[r][64 * gp:64 * gp + 64, pr, 0:8, :].rearrange("p a b -> p (a b)"),
                             start=(r == 0), stop=(r == 1))
            ins.then_inc(s("K_full"), 1)
        gemm_h(pe, units, tiles)
        pe.wait_ge(s("U_in"), 16 * LC)
        for r in range(2):
            for half in range(2):
                if r:
                    pe.wait_ge(s("V_copied"), half + 1)
                else:
                    pe.wait_ge(s("K_copied"), half + 3)
                for pr in range(8 * half, 8 * half + 8):
                    for gp in range(2):
                        ins = mm([pX, pY][half][64 * gp:64 * gp + 64, (pr % 8) * P:(pr % 8 + 1) * P],
                                 s_PT[r][:, pr, 64 * gp:64 * gp + 64], s_U[:, 2 * pr + gp, :], start=True, stop=True)
                ins.then_inc(s("V_full"), 1)
        for g in range(2, 6):
            gemm_h(pe, units, tiles)
        pe.wait_ge(s("X_ready"), 1)
        pe.wait_ge(s("Toep_in"), 16 * LC)
        pe.wait_ge(s("V_copied"), 4)
        for rnd in range(4):
            if rnd >= 2:
                pe.wait_ge(s("Y_copied"), rnd - 1)
            for q in range(8):
                gr = rnd * 8 + q
                pr, gp = gr // 2, gr % 2
                dst = [pX, pY][rnd % 2][:, s5_col(q):s5_col(q) + P]
                mm(dst, s_Toep[:, gr, :], s_U[:, gr, :], start=True, stop=False)
                for r in range(2):
                    ins = mm([pX, pY][rnd % 2][:, s5_col(q) + 1:s5_col(q) + P],
                             s_G[r][64 * gp:64 * gp + 64, pr, 1:9, :].rearrange("p a b -> p (a b)"),
                             s_V[r][64 * gp:64 * gp + 64, pr, 0:NC8 - 1], start=False, stop=(r == 1))
            ins.then_inc(s("Y_full"), 1)
        for g in range(6, KD):
            gemm_h(pe, units, tiles)
        for t in range(4):
            gemm(pe, units, tiles, t % 2 == 0, [(k, 2 * k + t % 2) for k in range(4)], o_hi, o_lo,
                 s("gelu_split") if t == 0 else None)

        def merge(split, per_chunk):
            with pe.Fori(0, 2) as i:
                units.loop(i, 2)
                tiles.loop(i, 4)
                for j in range(4):
                    gemm(pe, units, tiles, j % 2 == 0, [(k, 2 * k + j % 2) for k in range(4)], o_hi, o_lo,
                         s(split) if j == 0 else None, per_chunk=per_chunk)
            units.end(2)
            tiles.end(2)

        for j in range(KD):
            gemm(pe, units, tiles, j % 2 == 0, [(k, 2 * k + j % 2) for k in range(4)], o_hi, o_lo,
                 s("s5_split") if j == 0 else None)
            ada_cols(4 + j, pX)

        gemm_h(pe, units, tiles)
        gemm(pe, units, tiles, True, [(0, 0)], h_hi, h_lo)
        pe.wait_ge(acc_free[0], tiles.half(tiles.n - 2))
        with pe.Fori(0, GLA_PAIRS) as i:
            units.loop(i, 10)
            tiles.loop(i, 10)
            pe.wait_ge(s("gkw_ready"), i + 1)
            for hf in range(2):
                ins = mm(pX[:, hf * HALF:(hf + 1) * HALF], gkw_cur[:], g_lr[:, hf * HALF:(hf + 1) * HALF],
                         start=True, stop=True)
            ins.then_inc(s("z_full"), 1)
            gemm_h(pe, units, tiles)
            gemm_h(pe, units, tiles)
            gemm_h(pe, units, tiles)
            t_v = tiles.n - 1
            pe.wait_ge(s("kl_ready"), i + 1)
            for tb in range(8):
                ins = tr(pX[:, tb * P:(tb + 1) * P], g_kl[:, tb * P:(tb + 1) * P], ident[:])
            ins.then_inc(s("klT_full"), 1)
            for hd in range(2):
                def values_T():
                    pe.wait_ge(acc_free[(t_v + hd) % 2], tiles.half(t_v + hd))
                    if hd:
                        pe.wait_ge(s("v_copied"), i * 2 + 1)
                    for tb in range(8):
                        ins = tr(pY[:, tb * P:(tb + 1) * P], g_vT[:, tb * P:(tb + 1) * P], ident[:])
                    ins.then_inc(s("v_full"), 1)

                gemm_h(pe, units, tiles, mid=values_T, mid_at=4)
            pe.wait_ge(s("klT_copied"), i + 1)
            pe.wait_ge(s("v_copied"), i * 2 + 2)
            settle(pe)
            for n in range(NCH - 1):
                tb, hb = n // 2, 64 * (n % 2)
                for hd in range(2):
                    ins = mm([pX, pY][n // 8][64 * hd:64 * hd + 64, ds_col(n):ds_col(n) + P],
                             g_klT[hb:hb + 64, tb, 64 * hd:64 * hd + 64], g_v[hb:hb + 64, hd, tb, :],
                             start=True, stop=True)
                if n % 8 == 7 or n == NCH - 2:
                    ins.then_inc(s("ds_full"), 1)
            gemm_h(pe, units, tiles)
            pe.wait_ge(s("S0_ready"), i + 1)
            for hd in range(2):
                r0 = 64 * hd
                if hd:
                    pe.wait_ge(s("g_rstd_ready"), i * 2 + 1)
                for tb in range(8):
                    ins = mm(pX[:, tb * P:(tb + 1) * P], g_kinv[r0:r0 + 64, tb * P:(tb + 1) * P],
                             g_qd[r0:r0 + 64, tb * P:(tb + 1) * P], start=True, stop=True)
                ins.then_inc(s("attn_full"), 1)
                gemm_h(pe, units, tiles)
                pe.wait_ge(s("attn_ready"), i * 2 + (hd + 1))
                if hd:
                    pe.wait_ge(s("g_o_read"), i * 2 + 1)
                for tb in range(8):
                    mm(pY[:, tb * P:(tb + 1) * P], g_v[:, hd, tb, :], g_attn[:, tb, :], start=True, stop=False)
                    for c in range(2):
                        t0 = tb * P + 64 * c
                        ins = mm(pY[:, t0:t0 + 64], g_S0[r0:r0 + 64, 2 * tb + c, :], g_qd[r0:r0 + 64, t0:t0 + 64],
                                 start=False, stop=(c == 1))
                ins.then_inc(s("g_o_full"), 1)
                gemm_h(pe, units, tiles, mid=lambda:
                       col_sums(ones, g_sq, pX, ("g_sq_ready", i * 2 + (hd + 1)), "g_ss_full"))
        units.end(GLA_PAIRS)
        tiles.end(GLA_PAIRS)
        merge("gla_split", 1)

        with pe.Fori(0, DH // 2) as i:
            units.loop(i, 10)
            tiles.loop(i, 42)
            for hh in range(2):
                def qk_sums(qk):
                    pe.wait_ge(s("d_sq_ready"), i * 4 + (2 * hh + qk + 1))
                    if hh or qk:
                        pe.wait_ge(s("d_rstd_ready"), i * 4 + (2 * hh + qk))
                    for hf in range(2):
                        ins = mm(pX[:, hf * HALF:(hf + 1) * HALF], half_ones[:], d_tmp[:, 0, hf * HALF:(hf + 1) * HALF],
                                 start=True, stop=True)
                    ins.then_inc(s("d_ss_full"), 1)

                gemm_h(pe, units, tiles)
                gemm_h(pe, units, tiles, mid=lambda: qk_sums(0))
                gemm_h(pe, units, tiles, mid=lambda: qk_sums(1))
                t_v = tiles.n - 1
                pe.wait_ge(s("d_qk_ready"), i * 4 + (2 * hh + 2))

                n8, n2 = i * 16 + 8 * hh, i * 4 + 2 * hh

                def scores(qb):
                    kw = (qb + 1) * QB
                    for j in range(2):
                        t = tiles.next()
                        pe.wait_ge(acc_free[t % 2], tiles.half(t) - 1)
                        for c0 in range(0, kw, HALF):
                            c1 = min(kw, c0 + HALF)
                            ins = mm(acc[t % 2][:, c0:c1], d_q[64 * j:64 * j + 64, qb * QB:(qb + 1) * QB],
                                     d_k[64 * j:64 * j + 64, c0:c1], start=True, stop=True)
                        ins.then_inc(acc_full[t % 2], 1)

                def weights_T(qb):
                    pe.wait_ge(s("d_w_ready"), n8 + (qb + 1))
                    if qb == 0:
                        pe.wait_ge(s("d_rstd_ready"), n2 + 2)
                    else:
                        pe.wait_ge(s("d_wT_copied"), n8 + qb)
                    for kb in range(qb + 1):
                        ins = tr(pX[:, kb * P:(kb + 1) * P], d_w[:, qb % 2, kb * P:(kb + 1) * P], ident[:])
                    ins.then_inc(s("d_wT_full"), 1)

                def values(qb):
                    pe.wait_ge(s("d_wT_copied"), n8 + (qb + 1))
                    if qb == 0:
                        pe.wait_ge(s("d_v_copied"), i * 2 + (hh + 1))
                    if qb == 4:
                        pe.wait_ge(s("d_orstd"), n2 + 1)
                    for kb in range(qb + 1):
                        ins = mm(pY[:, qb * P:(qb + 1) * P], d_v[:, kb, :], d_wT[:, qb % 2, kb, :],
                                 start=(kb == 0), stop=(kb == qb))
                    ins.then_inc(s("d_pv"), 1)

                def out_sums(grp):
                    pe.wait_ge(s("d_osq_ready"), n2 + (grp + 1))
                    if grp:
                        pe.wait_ge(s("d_o_read"), n2 + 1)
                    c0 = HALF * (1 - grp)
                    mm(pY[:, c0:c0 + HALF], ones[:], o_sq[:], start=True, stop=True).then_inc(s("d_oss_full"), 1)

                for q in range(STEPS):
                    if q < NQB:
                        scores(q)
                    if q == 0:
                        pe.wait_ge(acc_free[t_v % 2], tiles.half(t_v))
                        for tb in range(8):
                            ins = tr(pY[:, tb * P:(tb + 1) * P], d_vT[:, tb * P:(tb + 1) * P], ident[:])
                        ins.then_inc(s("d_v_full"), 1)
                    if q in (7, 11):
                        out_sums(q // 8)
                    if q in GATE_AT:
                        gemm_h(pe, units, tiles)
                    if 2 <= q < NQB + 2:
                        weights_T(q - 2)
                    if 3 <= q < NQB + 3:
                        values(q - 3)
        units.end(DH // 2)
        tiles.end(DH // 2)
        merge("diff_split", 2)

        for t in range(KD):
            gemm_h(pe, units, tiles, s("merged_split") if t == 0 else None)
        col_sums(ones, sq_sum, pY, ("sq_added", KD - 1), "n_ss_full")

        def down(q):
            for m in range(4):
                gemm(pe, units, tiles, m == 0, [(2 * q + k, 4 * k + m) for k in range(2)], o_hi, o_lo)

        for t in range(4):
            gemm_h(pe, units, tiles, s("h_ready2") if t == 0 else None)
        with pe.Fori(0, (FG - 1) // 2) as i:
            units.loop(i, 12)
            tiles.loop(i, 24)
            for q in range(2):
                for c in range(2):
                    gemm_h(pe, units, tiles)
                    if c == 0:
                        pe.wait_ge(s("act_split"), i * 4 + (2 * q + 2))
                    down(q)
                    gemm_h(pe, units, tiles)
        units.end((FG - 1) // 2)
        tiles.end((FG - 1) // 2)
        pe.wait_ge(s("act_split"), 2 * FG)
        down(0)
        down(0)

        for q in range(2):
            pe.wait_ge(acc_free[q], tiles.half(tiles.n - 2))
        for tt in range(NQB):
            if tt >= 2:
                pe.wait_ge(s("out_ready"), tt - 1)
            for k in range(KD):
                ins = tr([pX, pY][tt % 2][:, k * P:(k + 1) * P], M[:, k, tt * P:(tt + 1) * P], ident[:])
            ins.then_inc(s("out_full"), 1)

    @block.scalar
    def _(act):
        units, tiles = Count(), Count()
        act_ = nc.scalar.activation
        chain = Chain(act, act_chain)
        d, w = chain.did, chain.wait

        def full(t):
            act.wait_ge(acc_full[t % 2], tiles.half(t))

        def rows(v, n):
            return a[v][0].rearrange("(m p) -> m p", m=n)

        def row_in(dst, src):
            act.dma_start(dst, src).then_inc(s("rows_in"), 16)

        row_in(rows_a[V_ADAB:V_N1, :], rows("ada_b", 48))
        row_in(rows_a[V_N1:V_N2, :], rows("norm1_g", 8))
        row_in(rows_a[V_N2:V_C, :], rows("norm2_g", 8))
        row_in(rows_a[V_C:V_GKB, :], rows("c", 8))
        row_in(rows_a[V_GKB:V_S5D, :], rows("gla_gk_b", 2))
        row_in(rows_a[V_S5D:V_GLUB, :], rows("s5_d", 4))
        row_in(rows_a[V_GLUB:V_GLAG, :], rows("s5_glu_b", 4))
        row_in(rows_a[V_GLAG:V_SUBG, :], rows("gla_norm_g", 1))
        row_in(rows_a[V_SUBG:V_QG, :], rows("diff_subln_g", 1))
        for j in range(2):
            row_in(rows_a[V_QG:V_KG, DD * j:DD * j + DD], rows("diff_q_norm_g", 1))
            row_in(rows_a[V_KG:V_ROWS, DD * j:DD * j + DD], rows("diff_k_norm_g", 1))
        cw = a["ffn_conv_w"][0].rearrange("w (m p) -> (w m) p", p=P)
        row_in(rows_b[:], cw[0:P])
        row_in(rows_c[0:4, :], cw[P:3 * NT_FF])
        row_in(rows_c[4:48, :], rows("ffn_conv_b", NT_FF))
        for r, nm in enumerate(("s5_lambda_re", "s5_lambda_im")):
            row_in(rows_s[:, r, :], a[nm][0].rearrange("(r g) p -> r (g p)", g=2))
        row_in(dt_row[:], a["s5_log_dt"][0].rearrange("(r g) -> r g", g=2))
        row_in(gkw[:], a["gla_gk_w"][0])
        for q, nm in enumerate(("diff_lambda_q1", "diff_lambda_k1", "diff_lambda_q2", "diff_lambda_k2")):
            row_in(lam_in[:, q:q + 1], a[nm][0].rearrange("(p o) -> p o", o=1))

        act.wait_ge(s("rows_T"), 1)
        act_(cols[:, 0:V_ROWS], pA[:, 0:V_ROWS], ACT.Copy)
        act_(cols[:, V_CONV:V_CONV + P], pA[:, 128:256], ACT.Copy)
        act_(cols[:, V_CONV + P:V_END], pA[:, 256:304], ACT.Copy)
        act_(l_re[:], pA[:, 320:336], ACT.Copy)
        act_(l_im[:], pA[:, 336:352], ACT.Copy)
        act_(l_dt[:], pA[:, 352:368], ACT.Copy)
        act_(lam_e[:], pA[:, 368:370], ACT.Exp).then_inc(s("cols_ready"), 1)
        act.wait_ge(s("cols_ready"), 1)
        act_(c_act[:], cols[:, V_C:V_C + KD], ACT.Silu).then_inc(s("c_ready"), 1)

        for k in range(KD):
            act.wait_ge(s("xT_full"), k + 1)
            act_(xT0[:, k, :], [pX, pY][k % 2][:], ACT.Copy).then_inc(s("xT_copied"), 1)

        def norm_rstd(sums, count):
            act.wait_ge(s(sums), count)
            d(act_(n_rstd[:], pY[:], ACT.Ln, scale=1.0 / D, bias=eps_col[:]))
            w()
            act_(n_rstd[:], n_rstd[:], ACT.Exp, scale=-0.5).then_inc(s("nrm_rstd"), 1)

        def norm_hi(tag, k, scale, shift):
            act.wait_ge(s(f"nrm_t{tag}"), k + 1)
            d(act_(h_hi[:, k, :], n_tmp[:, k % 2, :], ACT.Identity, scale=scale[:, k:k + 1],
                   bias=mod[:, shift + k:shift + k + 1]))
            w()
            act_(n_tmp[:, k % 2, :], n_tmp[:, k % 2, :], ACT.Identity, scale=scale[:, k:k + 1],
                 bias=mod[:, shift + k:shift + k + 1]).then_inc(s(f"nrm_hi{tag}"), 1)

        for k in range(KD):
            act.wait_ge(s("xT_copied"), k + 1)
            if k >= 2:
                act.wait_ge(s("sq_summed"), k - 1)
            act_(n_tmp[:, k % 2, :], xT0[:, k, :], ACT.Square).then_inc(s("sq_ready"), 1)
        norm_rstd("sq_summed", KD)

        act.wait_ge(s("angle_ready"), 1)
        act_(sn[:], th[:], ACT.Sin)
        act_(sh[:], th[:], ACT.Sin, scale=0.5).then_inc(s("sines"), 1)
        act.wait_ge(s("R_stored"), 16)
        for k in range(KD):
            norm_hi(1, k, scale1, M_SH1)
        for t in range(S5T):
            n = tiles.next()
            full(n)
            act_(s_uP[:, t], acc[n % 2].rearrange("p (c j) -> p j c", j=LC), ACT.Copy).then_inc(acc_free[n % 2], 1)
            if t == 1:
                act.wait_ge(s("C_T"), 1)
                act_(s_C[0].rearrange("p a b -> p (a b)"), pX[:, 0:256], ACT.Copy)
                act_(s_C[1].rearrange("p a b -> p (a b)"), pX[:, 256:512], ACT.Copy).then_inc(s("C_copied"), 1)
        for n in range(4):
            act.wait_ge(s("PT_full"), n + 1)
            act_(s_PT[n // 2][:, 8 * (n % 2):8 * (n % 2) + 8, :].rearrange("p a b -> p (a b)"), [pX, pY][n % 2][:],
                 ACT.Copy).then_inc(s("PT_copied"), 1)
        for n in range(4):
            act.wait_ge(s("K_full"), n + 1)
            act_(s_K[:, 8 * n:8 * n + 8, :].rearrange("p (r g) b -> p g r b", g=2),
                 [pX, pY][n % 2][0:S5H, :].rearrange("p (g r b) -> p g r b", g=2, b=P),
                 ACT.Copy).then_inc(s("K_copied"), 1)

        def gate(g):
            n = tiles.next()
            full(n)
            act_(M[:, g, :], acc[n % 2][:], ACT.Sigmoid).then_inc(acc_free[n % 2], 1)

        act.wait_ge(s("Toep_in"), 16 * LC)
        for n in range(4):
            act.wait_ge(s("V_full"), n + 1)
            act_(s_V[n // 2][:, 8 * (n % 2):8 * (n % 2) + 8, :].rearrange("p a b -> p (a b)"), [pX, pY][n % 2][:],
                 ACT.Copy).then_inc(s("V_copied"), 1)
            if n in (1, 2):
                gate(n - 1)
        for g in range(2, 4):
            gate(g)
        for n in range(4):
            act.wait_ge(s("Y_full"), n + 1)
            act_(s_Y[:, 8 * n:8 * n + 8, :].rearrange("p (r g) b -> p g r b", g=2),
                 [pX, pY][n % 2][:].rearrange("p (g r b) -> p g r b", g=2, b=P),
                 ACT.Copy).then_inc(s("Y_copied"), 1)
        for g in range(4, KD - 1):
            gate(g)
        for t in range(S5T):
            act.wait_ge(s("yd_ready"), t + 1)
            d(act_(s_Yp[:, t, :], s_Yp[:, t, :], ACT.Gelu_apprx_tanh))
            w()
            act_(o_hi[:, t, :], s_Yp[:, t, :], ACT.Copy).then_inc(s("gelu_hi"), 1)
        gate(KD - 1)

        def ada_load(n):
            if n >= 6:
                act.wait_ge(s("ada_mult"), n - 1)
            act.dma_start(ada_ring[:, (n + 1) % 2], ada_v[:, :, n * HALF:(n + 1) * HALF]).then_inc(s(f"ada_in{n % 2}"), 16)

        ada_load(4)
        for t in range(S5T):
            n = tiles.next()
            full(n)
            if t:
                act.wait_ge(s("glu_out"), t)
            act_(s_sig[:], acc[n % 2][:], ACT.Sigmoid, bias=cols[:, V_GLUB + t:V_GLUB + t + 1]).then_inc(acc_free[n % 2], 1)
        for t in range(S5T):
            act.wait_ge(s("glu_out"), t + 1)
            act_(o_hi[:, t, :].rearrange("p (c j) -> p j c", j=LC), s_Yp[:, t, :].rearrange("p (j c) -> p j c", j=LC),
                 ACT.Copy).then_inc(s("s5_hi"), 1)

        def merged_out(adds):
            if adds:
                act.wait_ge(s("merged_add"), adds)
                act.dma_start(d_R[:], R_dram).then_inc(s("R_in"), 16)
            else:
                for q in range(2):
                    act.wait_ge(acc_free[q], tiles.half(tiles.n - 2 + q))
            act.dma_start(m_dram.rearrange("(k p) t -> p k t", p=P), M[:]).then_inc(s("M_out"), 16)

        def merge(split, count):
            act.wait_ge(s(split), count)
            for q in range(4):
                act.dma_start(m_prev[:, 2 * q:2 * q + 2, :], m_dram.rearrange("(k p) t -> p k t", p=P)[:, 2 * q:2 * q + 2, :]
                              ).then_inc(s(f"M_in{q}"), 16)
            tiles.n += KD

        def gate_reg(tile):
            n = tiles.next()
            full(n)
            act_(M[:, bass.ds(tile, 1), :].rearrange("p a b -> p (a b)"), acc[n % 2][:], ACT.Sigmoid
                 ).then_inc(acc_free[n % 2], 1)

        tiles.n += KD
        act.wait_ge(s("s5_split"), S5T)
        for n in range(5, 12):
            ada_load(n)
        merged_out(0)

        n = tiles.next()
        full(n)
        act_(g_lr[:], acc[n % 2][0:GLA_LR, :], ACT.Copy).then_inc(acc_free[n % 2], 1)
        n = tiles.next()
        full(n)
        act_(junk[:], acc[n % 2][:, 0:2], ACT.Copy).then_inc(acc_free[n % 2], 1)
        with act.Fori(0, GLA_PAIRS) as i:
            tiles.loop(i, 10)
            chain.loop(i, 4)
            act.wait_ge(s("g_z"), i + 1)
            d(act_(g_eb[:], g_kinv[:], ACT.Abs))
            w()
            d(act_(g_eb[:], g_eb[:], ACT.Exp, scale=-1.0))
            w()
            act_(g_eb[:], g_eb[:], ACT.Ln, bias=one_col[:]).then_inc(s("g_ln"), 1)
            act.wait_ge(s("g_S_ready"), i + 1)
            act_(g_eb[:], g_S[:], ACT.Exp, scale=1.0 / 16)
            act_(g_kinv[:], g_S[:], ACT.Exp, scale=-1.0 / 16).then_inc(s("g_exps"), 1)
            act.wait_ge(s("g_kx_ready"), i + 1)
            act_(g_kl[:], g_kl[:], ACT.Exp, scale=1.0 / 16).then_inc(s("g_klx"), 1)
            tiles.n += 2
            n = tiles.next()
            full(n)
            act_(g_vT[:], acc[n % 2][:], ACT.Copy).then_inc(acc_free[n % 2], 1)
            act.wait_ge(s("klT_full"), i + 1)
            act_(g_klT.rearrange("p a b -> p (a b)"), pX[:], ACT.Copy).then_inc(s("klT_copied"), 1)
            act.wait_ge(s("v_full"), i * 2 + 1)
            act_(g_v[:, 0].rearrange("p a b -> p (a b)"), pY[:], ACT.Copy).then_inc(s("v_copied"), 1)
            n = tiles.next()
            full(n)
            act_(g_vT[:], acc[n % 2][:], ACT.Copy).then_inc(acc_free[n % 2], 1)
            n = tiles.next()
            full(n)
            act_(g_sil[:], acc[n % 2][:], ACT.Silu).then_inc(acc_free[n % 2], 1)
            act.wait_ge(s("v_full"), i * 2 + 2)
            act_(g_v[:, 1].rearrange("p a b -> p (a b)"), pY[:], ACT.Copy).then_inc(s("v_copied"), 1)
            act.wait_ge(s("M_out"), 16)
            gate_reg(i * 4)
            for hd in range(2):
                if hd == 0:
                    gate_reg(i * 4 + 1)
                else:
                    n = tiles.next()
                    full(n)
                    act_(g_sil[:], acc[n % 2][:], ACT.Silu).then_inc(acc_free[n % 2], 1)
                    act.wait_ge(s("gla_split"), i * 2 + 1)
                act.wait_ge(s("g_o_full"), i * 2 + (hd + 1))
                act_(g_sq[:], pY[:], ACT.Square).then_inc(s("g_sq_ready"), 1)
                act.wait_ge(s("g_ss_full"), i * 2 + (hd + 1))
                d(act_(g_rstd[:], pX[:], ACT.Ln, scale=1.0 / GLA_DV, bias=eps_col[:]))
                w()
                act_(g_rstd[:], g_rstd[:], ACT.Exp, scale=-0.5).then_inc(s("g_rstd_ready"), 1)
                act.wait_ge(s("g_y_ready"), i * 2 + (hd + 1))
                act_(o_hi[:, bass.ds(i * 2 + hd, 1), :].rearrange("p a b -> p (a b)"), g_sq[:], ACT.Copy).then_inc(s("g_hi"), 1)
                gate_reg(i * 4 + (2 + hd))
        tiles.end(GLA_PAIRS)
        chain.end(GLA_PAIRS)
        merge("gla_split", GLA_HEADS)
        merged_out(KD)

        with act.Fori(0, DH // 2) as i:
            tiles.loop(i, 42)
            chain.loop(i, 8)
            for hh in range(2):
                for qk in range(2):
                    n = tiles.next()
                    full(n)
                    if qk:
                        act.wait_ge(s("d_ss_full"), i * 4 + (2 * hh + 1))
                    act_(d_tmp[:, 0, :], acc[n % 2][:], ACT.Square).then_inc(s("d_sq_ready"), 1)
                    act.wait_ge(s("d_var"), i * 4 + (2 * hh + qk + 1))
                    d(act_(d_rs[:], d_tmp[:, 1, :], ACT.Ln))
                    w()
                    act_(d_rs[:], d_rs[:], ACT.Exp, scale=-0.5).then_inc(s("d_rstd_ready"), 1)
                n = tiles.next()
                full(n)
                act_(d_vT[:], acc[n % 2][:], ACT.Copy).then_inc(acc_free[n % 2], 1)
                act.wait_ge(s("d_v_full"), i * 2 + (hh + 1))
                act_(d_v.rearrange("p a b -> p (a b)"), pY[:], ACT.Copy).then_inc(s("d_v_copied"), 1)

                n8, n2 = i * 16 + 8 * hh, i * 4 + 2 * hh

                for q in range(STEPS):
                    grp = (q - 6) // 4
                    if q < NQB:
                        tiles.n += 2
                        kw = (q + 1) * QB
                        act.wait_ge(s("d_mx_ready"), n8 + (q + 1))
                        for j in range(2):
                            ins = act_(d_s[:, q % 2, j, 0:kw], d_s[:, q % 2, j, 0:kw], ACT.Exp,
                                       bias=nmx[:, q % 2, j:j + 1], accum_out=rsum[:, q % 2, j:j + 1])
                        ins.then_inc(s("d_p_ready"), 1)
                    if q in (7, 11):
                        c0 = HALF * (1 - grp)
                        act.wait_ge(s("d_oss_full"), n2 + (grp + 1))
                        d(act_(o_sq[:], pY[:, c0:c0 + HALF], ACT.Ln, scale=1.0 / (2 * DD), bias=eps_col[:]))
                        w()
                        act_(o_sq[:], o_sq[:], ACT.Exp, scale=-0.5).then_inc(s("d_orstd"), 1)
                    if q in GATE_AT:
                        act.wait_ge(s("M_out"), 32)
                        gate_reg(i * 4 + (2 * hh + GATE_AT.index(q)))
                    if 2 <= q < NQB + 2:
                        b = q - 2
                        act.wait_ge(s("d_wT_full"), n8 + (b + 1))
                        if b >= 2:
                            act.wait_ge(s("d_pv"), n8 + (b - 1))
                        act_(d_wT[:, b % 2, 0:b + 1, :], pX[:, 0:(b + 1) * QB].rearrange("p (a b) -> p a b", b=QB),
                             ACT.Copy).then_inc(s("d_wT_copied"), 1)
                    if q in (6, 10):
                        act.wait_ge(s("d_pv"), n8 + (4 * grp + 4))
                        if grp:
                            act.wait_ge(s("diff_split"), n2 + 1)
                        act_(o_sq[:], pY[:, grp * HALF:(grp + 1) * HALF], ACT.Square).then_inc(s("d_osq_ready"), 1)
                    if q in (8, 12):
                        act.wait_ge(s("d_o_read"), n2 + (grp + 1))
                        act_(o_hi[:, bass.ds(i * 2 + hh, 1), grp * HALF:(grp + 1) * HALF].rearrange("p a b -> p (a b)"),
                             o_sq[:], ACT.Copy).then_inc(s("d_hi"), 1)
        tiles.end(DH // 2)
        chain.end(DH // 2)
        merge("diff_split", 2 * DH)

        for k in range(KD):
            act.wait_ge(s("merged_add"), KD + k + 1)
            act_(h_hi[:, k, :], M[:, k, :], ACT.Copy).then_inc(s("merged_hi"), 1)
        act.wait_ge(s("merged_split"), KD)
        act.dma_start(M[:], xT_dram.rearrange("(k p) t -> p k t", p=P)).then_inc(s("xT_in"), 16)
        for k in range(KD):
            n = tiles.next()
            if k >= 2:
                act.wait_ge(s("sq_added"), max(1, k - 2))
            act.wait_ge(acc_free[n % 2], tiles.half(n))
            act_(n_tmp[:, k % 2, :], M[:, k, :], ACT.Square).then_inc(s("sq2_ready"), 1)
        norm_rstd("n_ss_full", 1)
        for k in range(KD):
            norm_hi(2, k, scale2, M_SH2)

        def up(g, par, start):
            for c in range(2):
                for ag in range(2):
                    n = tiles.next()
                    if ag == 0 and not start:
                        tiles.n += 4
                    full(n)
                    buf = [f_a, f_g][ag]
                    if ag == 0 and not start:
                        act.wait_ge(s("act_split"), (g - 1) * 2 + (c + 1))
                    ch = V_CONV + 2 * NT_FF + 22 * ag + g * 2 + c
                    chb = V_CONVB + 22 * ag + g * 2 + c
                    if not start or c:
                        act.wait_ge(s("f_conv"), g * 4 + (2 * c + ag - 1))
                    act_(f_raw[:, ag, :], acc[n % 2][:], ACT.Copy).then_inc(acc_free[n % 2], 1)
                    act.wait_ge(acc_free[n % 2], tiles.half(n))
                    act_(buf[:, c, :], f_raw[:, ag, :], ACT.Identity, scale=cols[:, bass.ds(ch, 1)],
                         bias=cols[:, bass.ds(chb, 1)]).then_inc(s("f_lin"), 1)
                    if ag == 0:
                        act.wait_ge(s("f_conv"), g * 4 + (2 * c + 1))
                        act_(f_a[:, c, :], f_a[:, c, :], ACT.Silu).then_inc(s("f_silu"), 1)
                act.wait_ge(s("f_prod"), g * 2 + (c + 1))
                act_(o_hi[:, 2 * par + c, :], f_a[:, c, :], ACT.Copy).then_inc(s("f_hi"), 1)

        up(0, 0, True)
        with act.Fori(0, (FG - 1) // 2) as i:
            tiles.loop(i, 24)
            for q in range(2):
                up(i * 2 + (q + 1), (q + 1) % 2, False)
        tiles.end((FG - 1) // 2)
        tiles.n += 8

        for tt in range(NQB):
            act.wait_ge(s("out_full"), tt + 1)
            if tt >= 2:
                act.wait_ge(s(f"out_stored{tt % 2}"), 16 * (tt // 2))
            act_(out_tok[:, tt % 2, :], [pX, pY][tt % 2][:], ACT.Copy).then_inc(s("out_ready"), 1)

    @block.vector
    def _(dve):
        v = nc.vector
        tiles = Count()
        chain = Chain(dve, dve_chain)
        d, w = chain.did, chain.wait
        TT, TS, STT = v.tensor_tensor, v.tensor_scalar, v.scalar_tensor_tensor
        MUL, ADD, SUB = ALU.mult, ALU.add, ALU.subtract

        def one(ins):
            d(ins)
            w()

        def full(t):
            dve.wait_ge(acc_full[t % 2], tiles.half(t))

        def freed(t):
            dve.wait_ge(acc_free[t % 2], tiles.half(t))

        dve.wait_ge(s("rows_in"), 16 * N_ROWS)
        d(TT(lam_pr[:, 0:1], lam_in[:, 0:1], lam_in[:, 1:2], MUL))
        d(TT(lam_pr[:, 1:2], lam_in[:, 2:3], lam_in[:, 3:4], MUL))
        v.tensor_copy(rows_s[:, 2, :].rearrange("p (g q) -> p g q", g=2),
                      dt_row[:].unsqueeze(2).to_broadcast([PAIRS, 2, S5P])).then_inc(s("dt_rows"), 1)
        dve.wait_ge(s("cols_ready"), 1)
        one(STT(neg_lam[:], lam_e[:, 1:2], LAMBDA_INIT, lam_e[:, 0:1], SUB, SUB))
        d(TS(subg[:], cols[:, V_SUBG:V_SUBG + 1], 1.0 - LAMBDA_INIT, None, MUL))
        d(TS(qg[:], cols[:, V_QG:V_QG + 1], DD ** -0.5, None, MUL))

        def norm_rest(tag, X):
            def lo(k):
                dve.wait_ge(s(f"nrm_hi{tag}"), k + 1)
                TT(h_lo[:, k, :], n_tmp[:, k % 2, :], h_hi[:, k, :].bitcast(F32), SUB).then_inc(s(f"h_ready{tag}"), 1)
            for k in range(KD):
                if k >= 2:
                    dve.wait_ge(s(f"h_ready{tag}"), k - 1)
                TT(n_tmp[:, k % 2, :], X[:, k, :], n_rstd[:], MUL).then_inc(s(f"nrm_t{tag}"), 1)
                if k:
                    lo(k - 1)
            lo(KD - 1)

        def expm1(out_m1, out_e, x):
            one(TS(e_x[:], x, -87.3, 88.7, ALU.max, ALU.min))
            one(TS(e_n[:], e_x[:], 1.0 / math.log(2.0), 12582912.0, MUL, ADD))
            one(TS(e_n[:], e_n[:], 12582912.0, None, SUB))
            one(STT(e_r[:], e_n[:], -0.693145751953125, e_x[:], MUL, ADD))
            one(STT(e_r[:], e_n[:], -1.4286068203094172e-06, e_r[:], MUL, ADD))
            one(TS(e_q[:], e_r[:], 1.0 / 8, 1.0, MUL, ADD))
            for k in range(7, 1, -1):
                one(STT(e_q[:], e_q[:], 1.0 / k, e_r[:], MUL, MUL))
                one(TS(e_q[:], e_q[:], 1.0, None, ADD))
            one(TT(e_q[:], e_q[:], e_r[:], MUL))
            one(TS(e_n[:], e_n[:], 127.0, 8388608.0, ADD, MUL))
            one(v.tensor_copy(e_int[:], e_n[:]))
            two_n = e_int[:].bitcast(F32)
            one(TT(e_q[:], e_q[:], two_n, MUL))
            one(TT(out_e, e_q[:], two_n, ADD))
            one(STT(out_m1, two_n, 1.0, e_q[:], SUB, ADD))

        def cmul(oi, ar, ai, br, bi, tmp):
            d(TT(tmp[0], ar, br, MUL))
            d(TT(tmp[1], ai, bi, MUL))
            d(TT(tmp[2], ar, bi, MUL))
            one(TT(tmp[3], ai, br, MUL))
            d(TT(oi[0], tmp[0], tmp[1], SUB))
            one(TT(oi[1], tmp[2], tmp[3], ADD))

        expm1(e_em[:], l_dt[:], l_dt[:])
        one(TT(th[:], l_im[:], l_dt[:], MUL))
        one(TS(sn[:], th[:], 1.0 / (2 * math.pi), 12582912.0, MUL, ADD))
        one(TS(sn[:], sn[:], 12582912.0, None, SUB))
        for c in (-6.28125, -0.0019340515136718750, -1.2556659146e-06):
            one(STT(th[:], sn[:], c, th[:], MUL, ADD))
        TS(th[:], th[:], -3.1415925, 3.1415925, ALU.max, ALU.min).then_inc(s("angle_ready"), 1)

        dve.wait_ge(s("c_ready"), 1)

        def ada_mult(n):
            ring, out = ada_ring[:, (n + 1) % 2] if n >= 4 else ada_first[n // 2][:, n % 2], ada_sums[n >= 4][:, n % 4, :]
            if n < 4:
                dve.wait_ge(s(f"ada_first{n}"), 16)
            else:
                dve.wait_ge(s(f"ada_in{n % 2}"), 16 * (n // 2 - 1))
            if n >= 8:
                dve.wait_ge(s("ada_used"), n - 3)
            one(TS(out, ring[:, 0, :], c_act[:, 0:1], None, MUL))
            for k in range(1, KD):
                ins = STT(out, ring[:, k, :], c_act[:, k:k + 1], out, MUL, ADD)
                if k < KD - 1:
                    one(ins)
            ins.then_inc(s("ada_mult"), 1)

        for n in range(4):
            ada_mult(n)
        dve.wait_ge(s("ada_used"), 4)
        one(TT(mod[:, 0:16], pA[:, 0:16], cols[:, V_ADAB:V_ADAB + 16], ADD))
        STT(scale1[:], mod[:, M_SC1:M_SC1 + 8], 1.0, cols[:, V_N1:V_N1 + 8], ADD, MUL).then_inc(s("mod_ready"), 1)
        dve.wait_ge(s("mod_ready"), 1)
        dve.wait_ge(s("nrm_rstd"), 1)
        norm_rest(1, xT0)

        one(TT(cosv[:], l_re[:], l_dt[:], MUL))
        expm1(e_em[:], e_e[:], cosv[:])
        dve.wait_ge(s("sines"), 1)
        one(TT(cm[:], sh[:], sh[:], MUL))
        one(TS(cm[:], cm[:], -2.0, None, MUL))
        one(TS(cosv[:], cm[:], 1.0, None, ADD))
        one(TT(cr[:], e_e[:], cm[:], MUL))
        one(TT(cr[:], cr[:], e_em[:], ADD))
        one(TT(ci[:], e_e[:], sn[:], MUL))
        L = [Lp[0], Lp[1]]
        dve.wait_ge(s("xT_stored"), 16)
        d(v.memset(L[0][:, :, 0], 1.0))
        d(v.memset(L[1][:, :, 0], 0.0))
        d(TS(L[0][:, :, 1], cr[:], 1.0, None, ADD))
        one(v.tensor_copy(L[1][:, :, 1], ci[:]))

        def small_tmp(n):
            return [s_tt[:, q, 0:PAIRS * n].rearrange("p (a b) -> p a b", b=n) for q in range(4)]

        def wide(t, n):
            return t.to_broadcast([P, PAIRS, n])

        for n in (1, 2, 4):
            cmul([L[r][:, :, n + 1:2 * n + 1] for r in range(2)], L[0][:, :, 1:n + 1], L[1][:, :, 1:n + 1],
                 wide(L[0][:, :, n:n + 1], n), wide(L[1][:, :, n:n + 1], n), small_tmp(n))
        one(TT(inv[:], l_re[:], l_re[:], MUL))
        one(TT(wv_re[:], l_im[:], l_im[:], MUL))
        one(TT(inv[:], inv[:], wv_re[:], ADD))
        one(v.reciprocal(inv[:], inv[:]))
        d(TT(e_x[:], cr[:], l_re[:], MUL))
        d(TT(e_n[:], ci[:], l_im[:], MUL))
        d(TT(e_r[:], ci[:], l_re[:], MUL))
        one(TT(e_q[:], cr[:], l_im[:], MUL))
        d(TT(wv_re[:], e_x[:], e_n[:], ADD))
        one(TT(wv_im[:], e_r[:], e_q[:], SUB))
        d(TT(wv_re[:], wv_re[:], inv[:], MUL))
        one(TT(wv_im[:], wv_im[:], inv[:], MUL))
        dve.wait_ge(s("s5_b_in"), 16 * 4)
        dve.wait_ge(s("xT_full"), KD)
        cmul([s_Bb[0][:], s_Bb[1][:]], s_B[0][:], s_B[1][:], wv_re[:].unsqueeze(2).to_broadcast([P, PAIRS, S5H]),
             wv_im[:].unsqueeze(2).to_broadcast([P, PAIRS, S5H]), small_tmp(S5H))
        for r in range(2):
            for j in range(LC):
                d(v.tensor_copy(s_LR[r][:, :, j], L[r][:, :, LC - 1 - j]))
        w()
        HP = PAIRS // 2
        for hp in range(2):
            q = slice(hp * HP, hp * HP + HP)
            sh4 = [P, HP, LC, S5H]
            tmp = [s_tt[:, n, 0:1024].rearrange("p (a b c) -> p a b c", a=HP, b=LC) for n in range(4)]
            cmul([s_Ppre[r][:, q, :].rearrange("p a (b c) -> p a b c", b=LC) for r in range(2)],
                 s_Bb[0][:, q, :].unsqueeze(2).to_broadcast(sh4), s_Bb[1][:, q, :].unsqueeze(2).to_broadcast(sh4),
                 s_LR[0][:, q, :].unsqueeze(3).to_broadcast(sh4), s_LR[1][:, q, :].unsqueeze(3).to_broadcast(sh4), tmp)
        v.memset(junk[:], 0.0).then_inc(s("Ppre_ready"), 1)
        dve.wait_ge(s("C_copied"), 1)
        for hp in range(2):
            q = slice(hp * HP, hp * HP + HP)
            sh4 = [P, HP, 9, S5H]
            tmp = [s_tt[:, n, :].rearrange("p (a b c) -> p a b c", a=HP, b=9) for n in range(4)]
            ins4 = [(s_C[r][:, q, :].unsqueeze(2).to_broadcast(sh4)) for r in range(2)]
            lam4 = [(L[r][:, q, :].unsqueeze(3).to_broadcast(sh4)) for r in range(2)]
            d(TT(tmp[0], ins4[0], lam4[0], MUL))
            d(TT(tmp[1], ins4[1], lam4[1], MUL))
            d(TT(tmp[2], ins4[0], lam4[1], MUL))
            one(TT(tmp[3], ins4[1], lam4[0], MUL))
            d(TT(s_G[0][:, q], tmp[0], tmp[1], SUB))
            one(STT(s_G[1][:, q].rearrange("p a b c -> p (a b c)"), s_tt[:, 2, :], -1.0, s_tt[:, 3, :], MUL, SUB))
        v.memset(junk[:], 0.0).then_inc(s("G_ready"), 1)

        dve.wait_ge(s("u_out"), 16 * S5T)
        v.memset(s_Toep[:], 0.0).then_inc(s("Toep_zero"), 1)
        u_r, u_i = cosv, sn
        for sq in range(3):
            cmul([u_r[:], u_i[:]], u_r[:], u_i[:], u_r[:], u_i[:], [e_x[:], e_n[:], e_r[:], e_q[:]])
            one(TT(e_e[:], e_e[:], e_e[:], MUL))
        d(v.tensor_copy(s_E[0][:, :, 0], u_r[:]))
        one(v.tensor_copy(s_E[1][:, :, 0], u_i[:]))
        st = [s_t[:, 512 * q:512 * q + 512] for q in range(4)]
        for e in range(7):
            n = 1 << e
            step = min(n, 16)
            for c0 in range(0, n, step):
                tmp = [s_t[:, 256 * m:256 * m + PAIRS * step].rearrange("p (a b) -> p a b", b=step) for m in range(4)]
                cmul([s_E[r][:, :, n + c0:n + c0 + step] for r in range(2)],
                     s_E[0][:, :, c0:c0 + step], s_E[1][:, :, c0:c0 + step],
                     wide(s_E[0][:, :, n - 1:n], step), wide(s_E[1][:, :, n - 1:n], step), tmp)
        dve.wait_ge(s("V_copied"), 4)
        for sign in (-1, 1):
            if sign == 1:
                for r in range(2):
                    for pr in range(PAIRS):
                        d(v.tensor_tensor_scan(s_V[r][:, pr, :], e_e[:, pr:pr + 1].to_broadcast([P, NC8]), s_V[r][:, pr, :],
                                               0.0, MUL, ADD))
                w()
            for q4 in range(4):
                q = slice(4 * q4, 4 * q4 + 4)
                tmp = [t[:, 0:512].rearrange("p (a b) -> p a b", b=NC8) for t in st]
                Er, Ei, Vr, Vi = s_E[0][:, q], s_E[1][:, q], s_V[0][:, q], s_V[1][:, q]
                d(TT(tmp[0], Er, Vr, MUL))
                d(TT(tmp[1], Ei, Vi, MUL))
                d(TT(tmp[2], Er, Vi, MUL))
                one(TT(tmp[3], Ei, Vr, MUL))
                if sign == -1:
                    d(TT(Vr, tmp[0], tmp[1], ADD))
                    one(TT(Vi, tmp[2], tmp[3], SUB))
                else:
                    d(TT(Vr, tmp[0], tmp[1], SUB))
                    one(TT(Vi, tmp[2], tmp[3], ADD))
        v.memset(junk[:], 0.0).then_inc(s("X_ready"), 1)
        dve.wait_ge(s("uP_in"), 16)
        tiles.n += S5T + KD

        def lo_gelu(t):
            dve.wait_ge(s("gelu_hi"), t + 1)
            TT(o_lo[:, t, :], s_Yp[:, t, :], o_hi[:, t, :].bitcast(F32), SUB).then_inc(s("gelu_split"), 1)
        for t in range(S5T):
            dve.wait_ge(s(f"Yp_in{t // 2}"), 16)
            STT(s_Yp[:, t, :], s_uP2[:, t, :], cols[:, V_S5D + t:V_S5D + t + 1], s_Yp[:, t, :], MUL, ADD).then_inc(s("yd_ready"), 1)
            if t:
                lo_gelu(t - 1)
        lo_gelu(S5T - 1)
        for t in range(S5T):
            n = tiles.next()
            freed(n)
            TT(s_Yp[:, t, :], s_Yp[:, t, :], s_sig[:], MUL).then_inc(s("glu_out"), 1)
            if t == 1:
                ada_mult(4)
        for t in range(S5T):
            dve.wait_ge(s("s5_hi"), t + 1)
            vw = lambda x: x.rearrange("p (c j) -> p j c", j=LC)
            TT(vw(o_lo[:, t, :]), s_Yp[:, t, :].rearrange("p (j c) -> p j c", j=LC), vw(o_hi[:, t, :].bitcast(F32)),
               SUB).then_inc(s("s5_split"), 1)

        def merged_lo(k):
            dve.wait_ge(s("merged_hi"), k + 1)
            TT(h_lo[:, k, :], M[:, k, :], h_hi[:, k, :].bitcast(F32), SUB).then_inc(s("merged_split"), 1)

        def merge(base):
            for q in range(2):
                freed(tiles.n - 2 + q)
            for j in range(KD):
                n = tiles.next()
                full(n)
                TT(M[:, j, :], acc[n % 2][:], M[:, j, :], MUL).then_inc(acc_free[n % 2], 1)
                freed(n)
                if j % 2 == 0:
                    dve.wait_ge(s(f"M_in{j // 2}"), 16 * (base // KD + 1))
                TT(M[:, j, :], M[:, j, :], m_prev[:, j, :], ADD).then_inc(s("merged_add"), 1)
                if base and j:
                    merged_lo(j - 1)
            if base:
                merged_lo(KD - 1)

        for q in range(2):
            freed(tiles.n - 2 + q)
        for j in range(KD):
            n = tiles.next()
            full(n)
            TT(M[:, j, :], acc[n % 2][:], M[:, j, :], MUL).then_inc(acc_free[n % 2], 1)
            if j < KD - 1:
                ada_mult(5 + j)
        dve.wait_ge(s("ada_used"), 12)
        one(TT(mod[:, 16:48], pX[:, 16:48], cols[:, V_ADAB + 16:V_ADAB + 48], ADD))
        STT(scale2[:], mod[:, M_SC2:M_SC2 + 8], 1.0, cols[:, V_N2:V_N2 + 8], ADD, MUL).then_inc(s("mod_ready"), 1)

        tiles.n += 2
        with dve.Fori(0, GLA_PAIRS) as i:
            tiles.loop(i, 10)
            chain.loop(i, 17)
            v.tensor_copy(gkw_cur[:], gkw[:, bass.ds(i * P, P)]).then_inc(s("gkw_ready"), 1)
            dve.wait_ge(s("z_full"), i + 1)
            TS(g_kinv[:], pX[:], cols[:, bass.ds(V_GKB + i, 1)], None, ADD).then_inc(s("g_z"), 1)
            dve.wait_ge(s("g_ln"), i + 1)
            one(STT(g_kinv[:], g_kinv[:], 0.0, g_eb[:], ALU.min, SUB))
            for n in range(NCH):
                t0 = n * GLA_CHUNK
                ins = v.tensor_tensor_scan(g_S[:, t0:t0 + GLA_CHUNK], ones[:, 0:GLA_CHUNK], g_kinv[:, t0:t0 + GLA_CHUNK],
                                           0.0, MUL, ADD)
            ins.then_inc(s("g_S_ready"), 1)
            dve.wait_ge(s("g_S_ready"), i + 1)
            Sv = v3(g_S, NCH)
            TT(v3(g_kl, NCH), Sv[:, :, GLA_CHUNK - 1:GLA_CHUNK].to_broadcast([P, NCH, GLA_CHUNK]), Sv, SUB
               ).then_inc(s("g_kx_ready"), 1)
            n = tiles.next()
            full(n)
            dve.wait_ge(s("g_klx"), i + 1)
            TT(g_kl[:], acc[n % 2][:], g_kl[:], MUL).then_inc(s("kl_ready"), 1)
            TT(g_kinv[:], acc[n % 2][:], g_kinv[:], MUL).then_inc(acc_free[n % 2], 1)
            n = tiles.next()
            full(n)
            STT(g_qd[:], acc[n % 2][:], GLA_DK ** -0.5, g_eb[:], MUL, MUL).then_inc(acc_free[n % 2], 1)
            tiles.n += 8
            one(v.memset(g_S0[:, 0, :], 0.0))
            for n in range(NCH - 1):
                if n % 8 == 0:
                    dve.wait_ge(s("ds_full"), i * 2 + (n // 8 + 1))
                ins = STT(g_S0[:, n + 1, :], g_S0[:, n, :], g_eb[:, 64 * n + 63:64 * n + 64],
                          [pX, pY][n // 8][:, ds_col(n):ds_col(n) + P], MUL, ADD)
                if n < NCH - 2:
                    one(ins)
            ins.then_inc(s("S0_ready"), 1)
            one(v.memset(g_attn[:], 0.0))
            for hd in range(2):
                dve.wait_ge(s("attn_full"), i * 2 + (hd + 1))
                settle(dve)
                v.copy_predicated(g_attn[:], gla_mask[:].unsqueeze(1).to_broadcast([P, 8, P]), v3(pX, 8)
                                  ).then_inc(s("attn_ready"), 1)
                no = i * 2 + (hd + 1)
                dve.wait_ge(s("g_rstd_ready"), no)
                STT(g_sq[:], pY[:], cols[:, V_GLAG:V_GLAG + 1], g_rstd[:], MUL, MUL).then_inc(s("g_o_read"), 1)
                dve.wait_ge(s("g_o_read"), no)
                TT(g_sq[:], g_sq[:], g_sil[:], MUL).then_inc(s("g_y_ready"), 1)
                dve.wait_ge(s("g_hi"), no)
                slot = bass.ds(i * 2 + hd, 1)
                TT(o_lo[:, slot, :].rearrange("p a b -> p (a b)"), g_sq[:],
                   o_hi[:, slot, :].rearrange("p a b -> p (a b)").bitcast(F32), SUB).then_inc(s("gla_split"), 1)
        tiles.end(GLA_PAIRS)
        chain.end(GLA_PAIRS)
        merge(0)

        dve.wait_ge(s("R_in"), 16)
        with dve.Fori(0, DH // 2) as i:
            tiles.loop(i, 42)
            chain.loop(i, 62)
            for hh in range(2):
                one(TS(d_R[:], d_R[:], 0.25, None, MUL))
                for qk in range(2):
                    no = i * 4 + (2 * hh + qk + 1)
                    n = tiles.next()
                    dve.wait_ge(s("d_ss_full"), no)
                    TS(d_tmp[:, 1, :], pX[:], 1.0 / DD, EPS, MUL, ADD).then_inc(s("d_var"), 1)
                    dve.wait_ge(s("d_rstd_ready"), no)
                    full(n)
                    qk_out = [d_q, d_k][qk]
                    STT(qk_out[:], acc[n % 2][:], [qg[:], cols[:, V_KG:V_KG + 1]][qk], d_rs[:], MUL, MUL
                        ).then_inc(acc_free[n % 2], 1)
                    one(TT(d_tmp[:, 1, :], d_tmp[:, 1, :], d_rs[:], MUL))
                    one(TT(d_tmp[:, 1, :], d_tmp[:, 1, :], d_rs[:], MUL))
                    one(TS(d_tmp[:, 1, :], d_tmp[:, 1, :], -0.5, 1.5, MUL, ADD))
                    freed(n)
                    TT(qk_out[:], qk_out[:], d_tmp[:, 1, :], MUL).then_inc(s("d_qk_ready"), 1)
                    dve.wait_ge(s("d_qk_ready"), no)
                tiles.n += 1

                n8, n2 = i * 16 + 8 * hh, i * 4 + 2 * hh

                for q in range(STEPS):
                    grp = (q - 6) // 4
                    if q < NQB:
                        kw = (q + 1) * QB
                        if q >= 2:
                            dve.wait_ge(s("d_w_ready"), n8 + (q - 1))
                        for j in range(2):
                            n = tiles.next()
                            full(n)
                            settle(dve)
                            v.tensor_tensor_reduce(out=d_s[:, q % 2, j, 0:kw], in0=acc[n % 2][:, 0:kw],
                                                   in1=d_R[:, T - kw:T], scale=1.0, scalar=-3e38, op0=ADD, op1=ALU.max,
                                                   accum_out=mx[:, q % 2, j:j + 1]).then_inc(acc_free[n % 2], 1)
                        freed(n)
                        TS(nmx[:, q % 2, :], mx[:, q % 2, :], -1.0, None, MUL).then_inc(s("d_mx_ready"), 1)
                    if 1 <= q < NQB + 1:
                        b = q - 1
                        kw = (b + 1) * QB
                        dve.wait_ge(s("d_p_ready"), n8 + (b + 1))
                        if b >= 2:
                            dve.wait_ge(s("d_wT_full"), n8 + (b - 1))
                        one(v.reciprocal(rinv[:, b % 2, :], rsum[:, b % 2, :]))
                        one(TT(rinv[:, b % 2, 1:2], rinv[:, b % 2, 1:2], neg_lam[:], MUL))
                        one(TS(d_s[:, b % 2, 1, 0:kw], d_s[:, b % 2, 1, 0:kw], rinv[:, b % 2, 1:2], None, MUL))
                        STT(d_w[:, b % 2, 0:kw], d_s[:, b % 2, 0, 0:kw], rinv[:, b % 2, 0:1], d_s[:, b % 2, 1, 0:kw],
                            MUL, ADD).then_inc(s("d_w_ready"), 1)
                    if q in (7, 11):
                        dve.wait_ge(s("d_orstd"), n2 + (grp + 1))
                        STT(o_sq[:], pY[:, grp * HALF:(grp + 1) * HALF], subg[:], o_sq[:], MUL, MUL).then_inc(s("d_o_read"), 1)
                    if q in (8, 12):
                        dve.wait_ge(s("d_hi"), n2 + (grp + 1))
                        pos = (slice(None), bass.ds(i * 2 + hh, 1), slice(grp * HALF, (grp + 1) * HALF))
                        TT(o_lo[pos].rearrange("p a b -> p (a b)"), o_sq[:],
                           o_hi[pos].rearrange("p a b -> p (a b)").bitcast(F32), SUB).then_inc(s("diff_split"), 1)
                    if q in GATE_AT:
                        tiles.n += 1
        tiles.end(DH // 2)
        chain.end(DH // 2)
        merge(KD)

        dve.wait_ge(s("xT_in"), 16)

        def add_squares(k):
            dve.wait_ge(s("sq2_ready"), k + 1)
            if k >= 2:
                dve.wait_ge(s("sq_added"), k - 1)
            TT(sq_sum[:], n_tmp[:, 0, :] if k == 1 else sq_sum[:], n_tmp[:, k % 2, :], ADD).then_inc(s("sq_added"), 1)

        for k in range(KD):
            n = tiles.next()
            full(n)
            STT(M[:, k, :], acc[n % 2][:], mod[:, M_GT1 + k:M_GT1 + k + 1], M[:, k, :], MUL, ADD).then_inc(acc_free[n % 2], 1)
            if k >= 2:
                add_squares(k - 1)
        add_squares(KD - 1)
        dve.wait_ge(s("nrm_rstd"), 2)
        norm_rest(2, M)

        def down(m0, count):
            for m in range(m0, m0 + count):
                n = tiles.next()
                full(n)
                STT(M[:, m, :], acc[n % 2][:], mod[:, M_GT2 + m:M_GT2 + m + 1], M[:, m, :], MUL, ADD).then_inc(acc_free[n % 2], 1)

        def up(g, par, start):
            for c in range(2):
                for ag in range(2):
                    n = tiles.next()
                    if ag == 0 and not start:
                        down(4 * c, 1)
                    dve.wait_ge(s("f_lin"), g * 4 + (2 * c + ag + 1))
                    buf = [f_a, f_g][ag][:, c, :]
                    ch = V_CONV + 22 * ag + g * 2 + c
                    d(STT(buf[:, 1:T], f_raw[:, ag, 0:T - 1], cols[:, bass.ds(ch + NT_FF, 1)], buf[:, 1:T], MUL, ADD))
                    if ag == 0 and not start:
                        down(4 * c + 1, 1)
                    w()
                    STT(buf[:, 2:T], f_raw[:, ag, 0:T - 2], cols[:, bass.ds(ch, 1)], buf[:, 2:T], MUL, ADD
                        ).then_inc(s("f_conv"), 1)
                    if ag == 0 and not start:
                        down(4 * c + 2, 2)
                dve.wait_ge(s("f_conv"), g * 4 + (2 * c + 2))
                dve.wait_ge(s("f_silu"), g * 2 + (c + 1))
                TT(f_a[:, c, :], f_a[:, c, :], f_g[:, c, :], MUL).then_inc(s("f_prod"), 1)
                dve.wait_ge(s("f_hi"), g * 2 + (c + 1))
                TT(o_lo[:, 2 * par + c, :], f_a[:, c, :], o_hi[:, 2 * par + c, :].bitcast(F32), SUB).then_inc(s("act_split"), 1)

        up(0, 0, True)
        with dve.Fori(0, (FG - 1) // 2) as i:
            tiles.loop(i, 24)
            chain.loop(i, 8)
            for q in range(2):
                up(i * 2 + (q + 1), (q + 1) % 2, False)
        tiles.end((FG - 1) // 2)
        chain.end((FG - 1) // 2)
        down(0, KD)

    ctx.close()


_INS = ["x", "c", "ada_w", "ada_b", "norm1_g", "w_in", "gla_gk_w", "gla_gk_b", "gla_norm_g", "s5_lambda_re",
        "s5_lambda_im", "s5_b_re", "s5_b_im", "s5_c_re", "s5_c_im", "s5_d", "s5_log_dt", "s5_glu_w", "s5_glu_b",
        "diff_q_norm_g", "diff_k_norm_g", "diff_lambda_q1", "diff_lambda_k1", "diff_lambda_q2", "diff_lambda_k2",
        "diff_subln_g", "w_branch_gla", "w_branch_s5", "w_branch_diff", "w_out", "norm2_g", "ffn_w_up",
        "ffn_conv_w", "ffn_conv_b", "ffn_w_down"]


def kernel(**inputs):
    import numpy as np
    import concourse.bacc as bacc
    from concourse.bass_utils import run_bass_kernel_spmd

    nc = bacc.Bacc("TRN2", target_bir_lowering=False, num_devices=1)
    arrays, aps = {}, {}
    for name in _INS:
        arr = np.ascontiguousarray(inputs[name])
        arrays[f"in_{name}"] = arr
        aps[name] = nc.dram_tensor(f"in_{name}", arr.shape, mybir.dt.from_np(arr.dtype), kind="ExternalInput").ap()
    aps["out"] = nc.dram_tensor("out_0", (1, T, D), F32, kind="ExternalOutput").ap()
    build(nc, aps)
    r = run_bass_kernel_spmd(nc, [arrays], core_ids=[0])
    return r.results[0]["out_0"]
```
